# Optimizing a Trainium2 kernel written in Bass

```python
import math
import jax, jax.numpy as jnp
from jax import lax
import numpy as np

D_MODEL = 1024
BATCH = 1
SEQ = 1024
DEPTH = 1

MEM_LEN = 256
EPS = 1e-6
D_MIX = D_MODEL
D_CONV = D_MIX // 2
CONV_HEADS = 8
CONV_WIDTH = 31
D_SSM = D_MIX - D_CONV
SSM_GROUP = 16
N_SSM_GROUPS = D_SSM // SSM_GROUP
SSM_STATE = 64
N_XHEADS = 4
XHEAD_DIM = D_MODEL // N_XHEADS
N_EXPERT_GROUPS = 4
EXPERTS_PER_GROUP = 8
N_EXPERTS = N_EXPERT_GROUPS * EXPERTS_PER_GROUP
TOP_K = 2
D_EXPERT = D_MODEL // 2
MOE_BLOCK = 128

kernel_name = "hymba_conformer_s5_hmoe_block"

def rms_norm(x, w):
    x32 = x.astype(jnp.float32)
    y = x32 * lax.rsqrt(jnp.mean(x32 * x32, axis=-1, keepdims=True) + EPS)
    return (y * w.astype(jnp.float32)).astype(x.dtype)

def conformer_conv(a, g, conv_w, conv_b, ln_w, ln_b):
    v = a * jax.nn.sigmoid(g)
    c = v.shape[-1]
    v = lax.conv_general_dilated(
        v, conv_w[:, None, :].astype(v.dtype), window_strides=(1,),
        padding=[(CONV_WIDTH - 1, 0)], dimension_numbers=('NWC', 'WIO', 'NWC'),
        feature_group_count=c) + conv_b.astype(v.dtype)
    v32 = v.astype(jnp.float32)
    mu = jnp.mean(v32, axis=-1, keepdims=True)
    var = jnp.mean(jnp.square(v32 - mu), axis=-1, keepdims=True)
    v32 = (v32 - mu) * lax.rsqrt(var + EPS) * ln_w.astype(jnp.float32) + ln_b.astype(jnp.float32)
    return jax.nn.silu(v32).astype(a.dtype)

def _diag_combine(e1, e2):
    a1, b1 = e1
    a2, b2 = e2
    return a1 * a2, a2 * b1 + b2

def s5_mixer(u, A_re, A_im, log_dt, B_re, B_im, C_re, C_im, D, glu_w):
    bsz, s, _ = u.shape
    u32 = u.astype(jnp.float32).reshape(bsz, s, N_SSM_GROUPS, SSM_GROUP)
    lam = lax.complex(A_re.astype(jnp.float32), A_im.astype(jnp.float32))
    dt = jnp.exp(log_dt.astype(jnp.float32))[:, None]
    a_bar = jnp.exp(lam * dt)
    b = lax.complex(B_re.astype(jnp.float32), B_im.astype(jnp.float32))
    b_bar = ((a_bar - 1.0) / lam)[..., None] * b
    bu = jnp.einsum('bsgc,gpc->bsgp', u32.astype(jnp.complex64), b_bar)
    a_seq = jnp.broadcast_to(a_bar, bu.shape)
    _, states = lax.associative_scan(_diag_combine, (a_seq, bu), axis=1)
    c = lax.complex(C_re.astype(jnp.float32), C_im.astype(jnp.float32))
    y = jnp.einsum('bsgp,gcp->bsgc', states, c).real + D.astype(jnp.float32) * u32
    y = jax.nn.gelu(y)
    ab = jnp.einsum('bsgc,gce->bsge', y, glu_w.astype(jnp.float32))
    out = ab[..., :SSM_GROUP] * jax.nn.sigmoid(ab[..., SSM_GROUP:])
    return out.reshape(bsz, s, D_SSM).astype(u.dtype)

def memory_cross_attention(h, m, wq, wk, wv, wo):
    bsz, s, _ = h.shape
    mlen = m.shape[1]
    q = (h @ wq).reshape(bsz, s, N_XHEADS, XHEAD_DIM).astype(jnp.float32)
    k = (m @ wk).reshape(bsz, mlen, N_XHEADS, XHEAD_DIM).astype(jnp.float32)
    v = (m @ wv).reshape(bsz, mlen, N_XHEADS, XHEAD_DIM).astype(jnp.float32)
    scores = jnp.einsum('bshd,bmhd->bhsm', q, k) * (XHEAD_DIM ** -0.5)
    p = jax.nn.softmax(scores, axis=-1)
    o = jnp.einsum('bhsm,bmhd->bshd', p, v).reshape(bsz, s, D_MODEL).astype(h.dtype)
    return o @ wo

def hierarchical_moe(h, wg, bg, we, be, w1, w3, w2):
    bsz, s, d = h.shape
    t = bsz * s
    xt = h.reshape(t, d)
    x32 = xt.astype(jnp.float32)
    g_probs = jax.nn.softmax(x32 @ wg.astype(jnp.float32) + bg.astype(jnp.float32), axis=-1)
    g_w, g_idx = lax.top_k(g_probs, 1)
    e_logits = (x32 @ we.astype(jnp.float32)).reshape(t, N_EXPERT_GROUPS, EXPERTS_PER_GROUP)
    e_logits = e_logits + be.astype(jnp.float32)
    e_logits = e_logits[jnp.arange(t), g_idx[:, 0]]
    top_l, top_i = lax.top_k(e_logits, TOP_K)
    gates = g_w * jax.nn.softmax(top_l, axis=-1)
    expert = g_idx * EPG_CONST() + top_i

    n_assign = t * TOP_K
    e_flat = expert.reshape(n_assign).astype(jnp.int32)
    gate_flat = gates.reshape(n_assign)
    tok_flat = jnp.arange(n_assign, dtype=jnp.int32) // TOP_K
    order = jnp.argsort(e_flat)
    e_sorted = e_flat[order]
    counts = jnp.bincount(e_flat, length=N_EXPERTS).astype(jnp.int32)
    padded = (counts + MOE_BLOCK - 1) // MOE_BLOCK * MOE_BLOCK
    start = jnp.cumsum(counts) - counts
    pstart = jnp.cumsum(padded) - padded
    rank = jnp.arange(n_assign, dtype=jnp.int32) - start[e_sorted]
    slot = pstart[e_sorted] + rank
    n_blocks = -(-n_assign // MOE_BLOCK) + N_EXPERTS
    cap = n_blocks * MOE_BLOCK
    slot_tok = jnp.full((cap,), t, jnp.int32).at[slot].set(tok_flat[order])
    slot_gate = jnp.zeros((cap,), jnp.float32).at[slot].set(gate_flat[order])
    block_start = jnp.arange(n_blocks, dtype=jnp.int32) * MOE_BLOCK
    pend = pstart + padded
    block_expert = jnp.minimum(
        jnp.sum((block_start[:, None] >= pend[None, :]).astype(jnp.int32), axis=1), N_EXPERTS - 1)

    x_pad = jnp.concatenate([xt, jnp.zeros((1, d), xt.dtype)], axis=0)
    xb = x_pad[slot_tok].reshape(n_blocks, MOE_BLOCK, d)

    def expert_block(args):
        xblk, e = args
        hid = jax.nn.silu(xblk @ w1[e]) * (xblk @ w3[e])
        return hid @ w2[e]

    yb = lax.map(expert_block, (xb, block_expert))
    y = yb.reshape(cap, d) * slot_gate[:, None].astype(yb.dtype)
    out = jnp.zeros((t + 1, d), y.dtype).at[slot_tok].add(y)[:t]
    return out.reshape(bsz, s, d).astype(h.dtype)

def EPG_CONST():
    return EXPERTS_PER_GROUP

def setup_inputs(seed: int = 0) -> dict:
    key = jax.random.key(seed)
    ks = jax.random.split(key, 40)
    L, D = DEPTH, D_MODEL
    G, P, c = N_SSM_GROUPS, SSM_STATE, SSM_GROUP
    f32 = jnp.float32

    def nrm(k, shape, scale):
        return jax.random.normal(k, shape, f32) * scale

    def gain(k, shape):
        return 1.0 + 0.05 * jax.random.normal(k, shape, f32)

    n_idx = jnp.arange(P, dtype=f32)
    return {
        "x": nrm(ks[0], (BATCH, SEQ, D), 1.0),
        "mem": nrm(ks[1], (BATCH, MEM_LEN, D), 1.0),
        "norm_mix_w": gain(ks[2], (L, D)),
        "w_in": nrm(ks[3], (L, D, 2 * D_CONV + D_SSM), D ** -0.5),
        "conv_w": nrm(ks[4], (L, CONV_WIDTH, D_CONV), CONV_WIDTH ** -0.5),
        "conv_b": nrm(ks[5], (L, D_CONV), 0.02),
        "conv_ln_w": gain(ks[6], (L, D_CONV)),
        "conv_ln_b": nrm(ks[7], (L, D_CONV), 0.02),
        "ssm_A_re": -0.5 + 0.01 * jax.random.normal(ks[8], (L, G, P), f32),
        "ssm_A_im": math.pi * n_idx + 0.01 * jax.random.normal(ks[9], (L, G, P), f32),
        "ssm_log_dt": jax.random.uniform(ks[10], (L, G), f32, math.log(1e-3), math.log(1e-1)),
        "ssm_B_re": nrm(ks[11], (L, G, P, c), (2 * c) ** -0.5),
        "ssm_B_im": nrm(ks[12], (L, G, P, c), (2 * c) ** -0.5),
        "ssm_C_re": nrm(ks[13], (L, G, c, P), (2 * P) ** -0.5),
        "ssm_C_im": nrm(ks[14], (L, G, c, P), (2 * P) ** -0.5),
        "ssm_D": 1.0 + 0.1 * jax.random.normal(ks[15], (L, G, c), f32),
        "ssm_glu_w": nrm(ks[16], (L, G, c, 2 * c), c ** -0.5),
        "w_out": nrm(ks[17], (L, D_MIX, D), D_MIX ** -0.5),
        "norm_x_w": gain(ks[18], (L, D)),
        "norm_mem_w": gain(ks[19], (L, D)),
        "xq_w": nrm(ks[20], (L, D, D), D ** -0.5),
        "xk_w": nrm(ks[21], (L, D, D), D ** -0.5),
        "xv_w": nrm(ks[22], (L, D, D), D ** -0.5),
        "xo_w": nrm(ks[23], (L, D, D), D ** -0.5),
        "norm_ffn_w": gain(ks[24], (L, D)),
        "router_group_w": nrm(ks[25], (L, D, N_EXPERT_GROUPS), D ** -0.5),
        "router_group_b": nrm(ks[26], (L, N_EXPERT_GROUPS), 0.01),
        "router_expert_w": nrm(ks[27], (L, D, N_EXPERTS), D ** -0.5),
        "router_expert_b": nrm(ks[28], (L, N_EXPERT_GROUPS, EXPERTS_PER_GROUP), 0.01),
        "moe_w1": nrm(ks[29], (L, N_EXPERTS, D, D_EXPERT), D ** -0.5),
        "moe_w3": nrm(ks[30], (L, N_EXPERTS, D, D_EXPERT), D ** -0.5),
        "moe_w2": nrm(ks[31], (L, N_EXPERTS, D_EXPERT, D), D_EXPERT ** -0.5),
        "final_norm_w": gain(ks[32], (D,)),
    }

def reference(x, mem, norm_mix_w, w_in, conv_w, conv_b, conv_ln_w, conv_ln_b,
              ssm_A_re, ssm_A_im, ssm_log_dt, ssm_B_re, ssm_B_im, ssm_C_re, ssm_C_im,
              ssm_D, ssm_glu_w, w_out, norm_x_w, norm_mem_w, xq_w, xk_w, xv_w, xo_w,
              norm_ffn_w, router_group_w, router_group_b, router_expert_w, router_expert_b,
              moe_w1, moe_w3, moe_w2, final_norm_w):
    h = x
    for l in range(DEPTH):
        hn = rms_norm(h, norm_mix_w[l])
        proj = hn @ w_in[l]
        conv_a = proj[..., :D_CONV]
        conv_g = proj[..., D_CONV:2 * D_CONV]
        ssm_u = proj[..., 2 * D_CONV:]
        y_conv = conformer_conv(conv_a, conv_g, conv_w[l], conv_b[l], conv_ln_w[l], conv_ln_b[l])
        y_ssm = s5_mixer(ssm_u, ssm_A_re[l], ssm_A_im[l], ssm_log_dt[l], ssm_B_re[l], ssm_B_im[l],
                         ssm_C_re[l], ssm_C_im[l], ssm_D[l], ssm_glu_w[l])
        h = h + jnp.concatenate([y_conv, y_ssm], axis=-1) @ w_out[l]
        h = h + memory_cross_attention(rms_norm(h, norm_x_w[l]), rms_norm(mem, norm_mem_w[l]),
                                       xq_w[l], xk_w[l], xv_w[l], xo_w[l])
        h = h + hierarchical_moe(rms_norm(h, norm_ffn_w[l]), router_group_w[l], router_group_b[l],
                                 router_expert_w[l], router_expert_b[l],
                                 moe_w1[l], moe_w3[l], moe_w2[l])
    return rms_norm(h, final_norm_w)


_drawn_inputs = setup_inputs


def setup_inputs(seed=0):
    import zlib

    import numpy as np

    out = dict(_drawn_inputs(seed))
    spreads = {}
    factors = {'ssm_A_re': 200.0,
     'norm_x_w': 3.237,
     'router_group_b': 12.055,
     'router_expert_b': 9.17,
     'ssm_A_im': 28.744,
     'ssm_log_dt': 25.748,
     'ssm_B_re': 34.336,
     'ssm_B_im': 38.648,
     'ssm_C_re': 37.496,
     'ssm_C_im': 34.288}
    for name, (base, spread) in spreads.items():
        noise = np.random.default_rng([zlib.crc32(name.encode()), seed]).standard_normal(out[name].shape)
        drawn = base * np.exp(spread * noise) if base else spread * noise
        out[name] = __import__('jax').numpy.asarray(drawn.astype(out[name].dtype))
    for name, factor in factors.items():
        out[name] = (out[name] * factor).astype(out[name].dtype)
    return out
```

```python
from contextlib import ExitStack

import numpy as np

import concourse.bass as bass
from concourse import mybir

F32 = mybir.dt.float32
I32 = mybir.dt.int32
ALU = mybir.AluOpType
ACT = mybir.ActivationFunctionType
AX = mybir.AxisListType

P = 128
KB = 1024
BANK = 512
NO_ROW = 1 << 20
ROUND = 12582912.0
LOG2E = 1.4426950408889634
LN2_HI, LN2_LO = 0.693359375, -2.12194440e-4
TWO_PI = 6.283185307179586
TWO_PI_A = 6.28125
TWO_PI_B = round((TWO_PI - TWO_PI_A) * 2.0**21) / 2.0**21
TWO_PI_C = TWO_PI - TWO_PI_A - TWO_PI_B
PI_LOW = 3.1415925


def hymba_layer(nc, x, mem, norm_mix_w, w_in, conv_w, conv_b, conv_ln_w, conv_ln_b,
                A_re, A_im, log_dt, B_re, B_im, C_re, C_im, ssm_D, glu_w, w_out,
                norm_x_w, norm_mem_w, xq_w, xk_w, xv_w, xo_w, norm_ffn_w,
                router_group_w, router_group_b, router_expert_w, router_expert_b,
                moe_w1, moe_w3, moe_w2, final_norm_w, out, upto=99):
    _, S, D = x.shape
    M = mem.shape[1]
    TAPS, DC = conv_w.shape[1:]
    G, NS, CH = B_re.shape[1:]
    NG = router_group_w.shape[2]
    NE = router_expert_w.shape[2]
    EPG = NE // NG
    F = moe_w1.shape[3]
    EPS = 1e-6
    NT = S // P
    KD = D // P
    KC = DC // P
    KF = F // P
    MT = M // P
    NH = 4
    HD = D // NH
    HK = HD // P
    T = 8
    NC = S // T
    Q4 = KC
    GQ = P // CH
    PQ = GQ // 2
    NP = G // 2
    NR = NG + NE
    MAXOV = 2 * S // P
    NB = NE + MAXOV
    assert CH * T == P and 2 * NS == P and NC == P and S == 2 * BANK and D == 2 * BANK

    u_bounce = nc.dram_tensor("u_bounce", (Q4, GQ, CH, T, NC), F32, kind="Internal").ap()
    y_bounce = nc.dram_tensor("y_bounce", (Q4, GQ, CH, T, NC), F32, kind="Internal").ap()
    xn_rows = nc.dram_tensor("xn_rows", (S, D), F32, kind="Internal").ap()
    y_rows = nc.dram_tensor("y_rows", (2 * S, D), F32, kind="Internal").ap()

    base = (nc.sbuf_base + 63) // 64 * 64

    def sb(name, kb, shape, dt=F32):
        return nc.alloc_sbuf_tensor_at(name, shape, dt, offset=base + int(kb * KB))

    slab = [sb(f"slab{i}", 16 * i, [P, KD, BANK]) for i in range(3)]
    h = sb("h", 48, [P, NT, D])
    uc = [sb(f"uc{i}", 48 + 4 * i, [P, GQ, NC]) for i in range(2)]
    rotated = sb("rotated", 56, [P, 2, PQ, NC])
    scanned = sb("scanned", 60, [P, 2, PQ, NC])
    rot_tmp = sb("rot_tmp", 64, [P, 2, PQ, NC])
    y_chunks = sb("y_chunks", 68, [P, GQ, NC])
    y_feat = sb("y_feat", 72, [P, T, NC])
    shifts = sb("shifts", 76, [P, T, P])
    mem_rows = sb("mem_rows", 68, [P, MT, D])
    xT = sb("xT", 80, [P, KD, S])
    kT = sb("kT", 80, [P, KD, M])
    vm = sb("vm", 88, [P, MT, D])
    memT = sb("memT", 104, [P, KD, M])
    yT = sb("yT", 96, [P, KD, S])
    conv_acc = yT[:, KC:KD, :]
    qT = sb("qT", 96, [P, KD, S])
    c_raw = sb("c_raw", 112, [CH, 2, G * NS])
    PAD = TAPS - 1
    conv_in = sb("conv_in", 128, [P, KC, S + PAD])
    squares = sb("squares", 128, [P, 2, KC, BANK])
    u_perm = sb("u_perm", 144.5, [P, Q4, T, NC])
    b_raw = sb("b_raw", 144.5, [P, 2, NP, CH])
    rows_raw = sb("rows_raw", 146.5, [P, P])
    taps_raw = sb("taps_raw", 147, [P, P])
    a_raw = sb("a_raw", 147.5, [NP, 3, P])
    dt_raw = sb("dt_raw", 149, [NP, 2])
    xs0 = [sb(f"xs0_{i}", 150 + 4 * i, [P, D]) for i in range(2)]
    hT = sb("hT", 128, [P, KD, S])
    oT = sb("oT", 128, [P, KD, S])
    lift = [sb("lift0", 160.5, [P, 2, PQ, P]), sb("lift1", 32, [P, 2, PQ, P])]
    toep = [sb("toep0", 164.5, [P, GQ, P]), sb("toep1", 36, [P, GQ, P])]
    readout = [sb("readout0", 168.5, [P, 2, PQ, P]), sb("readout1", 40, [P, 2, PQ, P])]
    phase = [sb("phase0", 172.5, [P, 2, PQ, NC]), sb("phase1", 44, [P, 2, PQ, NC])]
    bpow = sb("bpow", 176.5, [P, 2, PQ, P])
    kern = sb("kern", 180.5, [P, GQ, CH])
    glu_sig = sb("glu_sig", 181, [P, BANK])
    conv_a = sb("conv_a", 183, [P, BANK])
    conv_sg = sb("conv_sg", 185, [P, BANK])
    states = sb("states", 187, [P, 2, PQ, NC + 1])
    pool_tmp = sb("pool_tmp", 191.25, [P, 4, PQ * CH * 4])
    ln_tmp = sb("ln_tmp", 183, [P, BANK])
    at = [195.25]

    def small(name, shape, dt=F32):
        n = int(np.prod(shape[1:])) * 4
        t = sb(name, at[0], shape, dt)
        at[0] += (n + 31) // 32 * 32 / KB
        assert base + at[0] * KB <= nc.sbuf_usable_end, (name, at[0])
        return t

    ident = small("ident", [P, P])
    means = small("means", [P, P])
    par = small("par", [P, 5 * KD + 4 * KC])
    taps = small("taps", [P, TAPS * KC])
    ct = small("ct", [P, 2, NP, CH])
    bbar = small("bbar", [P, 2, NP, CH])
    pw = small("pw", [P, 2, 3, NP])
    ph = small("ph", [P, 2, 7, NP])
    rho = small("rho", [P, NP])
    t16 = small("t16", [P, 12, NP])
    stat = small("stat", [P, 3, NT])
    stat_m = small("stat_m", [P, 3, MT])
    pool_mark = small("pool_mark", [P, 1])
    xs = [sb(f"xs{i}", 160.5 + 4 * i, [P, D]) for i in range(2)]
    probs = [sb(f"probs{i}", 168.5 + 4 * i, [P, NH, M]) for i in range(2)]
    pT = [sb(f"pT{i}", 176.5 + 4 * i, [P, NH * MT, P]) for i in range(2)]
    fT = [sb(f"fT{i}", 184.5 + 4 * i, [P, KD, P]) for i in range(2)]
    glu_lhs = sb("glu_lhs", 203.25, [P, Q4, 2, P])
    assert base + 207.25 * KB <= nc.sbuf_usable_end and at[0] <= 203.25, at[0]

    junk_x = sb("junk_x", 128, [P, D])
    junk_m = sb("junk_m", 56, [P, D])
    junk = sb("junk", 192.75, [P, D], mybir.dt.bfloat16)
    ln_var = sb("ln_var", 183, [P, 2, BANK])
    negmax = sb("negmax", 194.75, [P, 2, NH])
    expsum = sb("expsum", 194.8125, [P, 2, NH])
    logits = sb("logits", 203.25, [P, NT, NR])
    router_w = sb("router_w", 204.5, [P, KD, NR])
    router_b = sb("router_b", 205.75, [P, NR])
    at[0] = 160.5

    def late(name, shape, dt=F32):
        n = int(np.prod(shape[1:])) * 4
        t = sb(name, at[0], shape, dt)
        at[0] += (n + 31) // 32 * 32 / KB
        assert at[0] <= 195.25, name
        return t

    upper = late("upper", [P, P])
    ones = late("ones", [P, P])
    iota_n = late("iota_n", [P, P])
    assign_no = late("assign_no", [P, 2, NT])
    limits = late("limits", [P, 7])
    lg = late("lg", [P, NT, NR])
    col = late("col", [P, 12, NT])
    gsel = late("gsel", [P, 2, NT, NG])
    em = late("em", [P, NT, NE])
    etmp = late("etmp", [P, NT, NE])
    pick = late("pick", [P, 2, NT, NE])
    both = late("both", [P, NT, NE])
    offs = late("offs", [P, NT + 1, NE])
    rank = late("rank", [P, NT, NE])
    over = late("over", [P, NE, 7])
    ev = late("ev", [P, 5, NE])
    gates = late("gates", [P, NT, 2])
    posi = late("posi", [P, 2, 2, NT], I32)
    posf = late("posf", [P, 2, 2, NT])
    row_of = sb("row_of", 128, [P, 2 * NT, P])
    block_of = sb("block_of", 136, [P, 2 * NT, NB])
    slotv = late("slotv", [P, 2, NB])
    rows_of_block = late("rows_of_block", [P, 2, NB], I32)
    ovcmp = late("ovcmp", [P, MAXOV, NE])
    ovf = late("ovf", [P, MAXOV + 1])
    meta = late("meta", [P, MAXOV + 1], I32)
    gidx = [late(f"gidx{i}", [P, 1], I32) for i in range(2)]
    sidx = [late(f"sidx{i}", [P, 1], I32) for i in range(2)]
    fin_w = sb("fin_w", 203.25, [P, D])
    wb = [slab, [sb(f"slab_b{i}", 80 + 16 * i, [P, KD, BANK]) for i in range(3)]]
    xg = [sb(f"xg{i}", 128 + 4 * i, [P, D]) for i in range(2)]
    xgT = [sb(f"xgT{i}", 136 + 4 * i, [P, KD, P]) for i in range(2)]
    gate_act = [sb(f"gate_act{i}", 144 + 2 * i, [P, F]) for i in range(2)]
    hid = [sb(f"hid{i}", 148 + 2 * i, [P, F]) for i in range(2)]
    hidT = [sb(f"hidT{i}", 152 + 2 * i, [P, KF, P]) for i in range(2)]
    yb = [sb("yb0", 156, [P, D]), sb("yb1", 197, [P, D])]
    NY = 4
    ytile = [sb(f"ytile{i}", 80 + 8 * i, [P, 2, D]) for i in range(NY)]
    otile = [sb(f"otile{i}", 112 + 4 * i, [P, D]) for i in range(2)]
    junk_f = sb("junk_f", 120, [P, D])

    bank = [nc.alloc_psum_tensor(f"bank{i}", [P, BANK], F32) for i in range(8)]

    def sem(name):
        return nc.alloc_semaphore(name)

    bank_full = [sem(f"bank_full{i}") for i in range(8)]
    bank_free = [sem(f"bank_free{i}") for i in range(8)]
    bank_uses = [0] * 8
    use_of = {}

    consts_ready = sem("consts_ready")
    pool_step = sem("pool_step")
    dve_step = sem("dve_step")
    act_step = sem("act_step")
    params_in = sem("params_in")
    craw_in = sem("craw_in")
    par_in = sem("par_in")
    braw_in = sem("braw_in")
    glu_in = sem("glu_in")
    x_in = [sem(f"x_in{t}") for t in range(NT)]
    mem_in = sem("mem_in")
    slab_in = [sem(f"slab_in{i}") for i in range(3)]
    setup_ready = sem("setup_ready")
    trig_in = sem("trig_in")
    trig_out = sem("trig_out")
    conv_a_ready = sem("conv_a_ready")
    conv_sg_ready = sem("conv_sg_ready")
    v_ready = sem("v_ready")
    conv_done = sem("conv_done")
    u_ready = sem("u_ready")
    ub_out = sem("ub_out")
    uc_in = [sem("uc_in0"), sem("uc_in1")]
    memT_ready = sem("memT_ready")
    bpow_ready = sem("bpow_ready")
    readout_ready = sem("readout_ready")
    phase_ready = sem("phase_ready")
    lift_ready = sem("lift_ready")
    kern_ready = sem("kern_ready")
    toep_ready = sem("toep_ready")
    shifts_ready = sem("shifts_ready")
    states_ready = sem("states_ready")
    ychunk_ready = sem("ychunk_ready")
    yb_out = sem("yb_out")
    yf_in = sem("yf_in")
    dterm_done = sem("dterm_done")
    gelu_done = sem("gelu_done")
    glu_sig_ready = sem("glu_sig_ready")
    yssm_ready = sem("yssm_ready")
    kv_ready = sem("kv_ready")
    centered = sem("centered")
    squared = sem("squared")
    ln_v = sem("ln_v")
    ln_root = sem("ln_root")
    ln_scaled = sem("ln_scaled")
    yconv_ready = sem("yconv_ready")
    h1_ready = sem("h1_ready")
    q_ready = sem("q_ready")
    negmax_ready = sem("negmax_ready")
    exp_done = sem("exp_done")
    probs_ready = sem("probs_ready")
    pT_ready = sem("pT_ready")
    oT_ready = sem("oT_ready")
    h2_ready = sem("h2_ready")
    router_in = sem("router_in")
    xn_out = [sem("xn_out0"), sem("xn_out1")]
    logit_ready = sem("logit_ready")
    route_consts = sem("route_consts")
    gexp_in = sem("gexp_in")
    gexp_out = sem("gexp_out")
    pexp_in = sem("pexp_in")
    pexp_out = sem("pexp_out")
    both_ready = sem("both_ready")
    sel_ready = sem("sel_ready")
    sel_used = sem("sel_used")

    class Norm:

        def __init__(self, name):
            self.squares, self.var, self.root, self.rstd, self.scaled, self.stored = (
                sem(f"{name}_{x}") for x in ("squares", "var", "root", "rstd", "scaled", "stored"))

    nx, nm, n1, n2, nf = (Norm(n) for n in ("nx", "nm", "n1", "n2", "nf"))
    w_in_sem = [[sem(f"moe_w{w}_in{b}") for w in (1, 3, 2)] for b in range(2)]
    xg_in = [sem("xg_in0"), sem("xg_in1")]
    y_sent = [sem("y_sent0"), sem("y_sent1")]
    gidx_ready = sem("gidx_ready")
    sidx_ready = sem("sidx_ready")
    xg_turned = sem("xg_turned")
    xgT_ready = sem("xgT_ready")
    up1_done = sem("up1_done")
    up3_done = sem("up3_done")
    gate_ready = sem("gate_ready")
    hid_ready = sem("hid_ready")
    hid_turned = sem("hid_turned")
    hidT_ready = sem("hidT_ready")
    down_done = sem("down_done")
    yb_ready = sem("yb_ready")
    final_w_in = sem("final_w_in")
    over_done = sem("over_done")
    xg_clear = sem("xg_clear")
    rows_moved = sem("rows_moved")
    y_in = [sem(f"y_in{i}") for i in range(NY)]
    comb = sem("comb")
    out_ready = sem("out_ready")
    out_stored = [sem("out_stored0"), sem("out_stored1")]

    def full(eng, key):
        b, n = use_of[key]
        eng.wait_ge(bank_full[b], n)
        return bank[b]

    def wait_for(eng, s, n):
        if not (isinstance(n, int) and n == 0):
            eng.wait_ge(s, n)

    def linker(eng, step):
        count = [0]

        def link(ins):
            count[0] += 1
            ins.then_inc(step, 1)
            eng.wait_ge(step, count[0])
        return link

    def col_major(w, c0, n):
        return w[:, c0:c0 + n].rearrange("(c p) n -> p c n", p=P)

    slabs = [(w_in[0], 0, 0, None), (w_in[0], BANK, 1, None), (w_in[0], 2 * BANK, 2, None),
             (xk_w[0], 0, 0, ("g", KC - 1, 1)), (xk_w[0], BANK, 1, ("g", KC - 1, 1)),
             (xv_w[0], 0, 0, ("k", 3)), (xv_w[0], BANK, 1, ("k", 7)),
             (w_out[0], 0, 0, ("v", 0, 1)), (w_out[0], BANK, 1, ("v", 1, 1)),
             (xq_w[0], 0, 2, ("y", Q4 - 1, 1)), (xq_w[0], BANK, 0, ("h1", NT - 1, 1)),
             (xo_w[0], 0, 1, ("h1", NT - 1, 1)), (xo_w[0], BANK, 2, ("q", 3, 1))]

    def slab_loaded(eng, n):
        place = slabs[n][2]
        eng.wait_ge(slab_in[place], 16 * sum(w[2] == place for w in slabs[:n + 1]))

    NQ = Q4
    PAIRS = range(PQ)

    with nc.Block() as block:

        @block.tensor
        def _(pe):
            def take(*banks):
                for b in banks:
                    if bank_uses[b]:
                        pe.wait_ge(bank_free[b], bank_uses[b])

            def give(b, ins, key):
                bank_uses[b] += 1
                use_of[key] = (b, bank_uses[b])
                ins.then_inc(bank_full[b], 1)

            def turn(out, src, n=P):
                return nc.tensor.transpose(out, src, ident[0:n, 0:n])

            pe.wait_ge(consts_ready, 1)
            pe.wait_ge(params_in, 16 * 12)
            give(0, turn(bank[0][:, 0:48], rows_raw[0:48, :], 48), "par")
            give(1, turn(bank[1][:, 0:TAPS * KC], taps_raw[0:TAPS * KC, :], TAPS * KC), "taps")
            def turn_rows(norm, src, t, banks, key):
                pe.wait_ge(norm.scaled, t + 1)
                take(*banks)
                for c in range(KD):
                    last = turn(bank[banks[c // 4]][:, (c % 4) * P:(c % 4 + 1) * P], src[:, c * P:(c + 1) * P])
                    if c == 3:
                        give(banks[0], last, (key, t, 0))
                bank_uses[banks[1]] += 1
                use_of[(key, t, 1)] = (banks[1], bank_uses[banks[1]])
                last.then_inc(bank_full[banks[1]], 1)

            for t in range(NT):
                turn_rows(nx, xs0[t % 2], t, (4, 5) if t % 2 else (6, 7), "x")

            pe.wait_ge(consts_ready, 3)
            for i in range(3):
                last = turn(bank[2][:, i * NP:(i + 1) * NP], a_raw[:, i, :], NP)
            give(2, last, "a_raw")
            pe.wait_ge(craw_in, 32)
            for ri in range(2):
                for p in range(NP):
                    o = (ri * NP + p) * CH
                    last = turn(bank[3][:, o:o + CH], c_raw[:, ri, p * P:(p + 1) * P], CH)
            give(3, last, "c_raw")

            pe.wait_ge(nx.stored, NT)
            for n in range(2):
                slab_loaded(pe, n)
            for i in range(KC):
                for half in range(2):
                    for w, b in ((0, half), (1, 2 + half)):
                        take(b)
                        for k in range(KD):
                            last = nc.tensor.matmul(bank[b][:], slab[w][:, k, i * P:(i + 1) * P],
                                                    xT[:, k, half * BANK:(half + 1) * BANK],
                                                    start=(k == 0), stop=(k == KD - 1))
                        give(b, last, ("ag"[w], i, half))
            slab_loaded(pe, 2)
            for i in range(KC):
                for half in range(2):
                    b = 4 + half
                    take(b)
                    for k in range(KD):
                        last = nc.tensor.matmul(bank[b][:], slab[2][:, k, i * P:(i + 1) * P],
                                                xT[:, k, half * BANK:(half + 1) * BANK],
                                                start=(k == 0), stop=(k == KD - 1))
                    give(b, last, ("u", i, half))
            for t in range(MT):
                turn_rows(nm, mem_rows[:, t, :], t, (6, 7), "m")

            def setup(q):
                pe.wait_ge(bpow_ready, q + 1)
                for ri in range(2):
                    take(ri)
                    for p in PAIRS:
                        last = turn(bank[ri][:, p * P:(p + 1) * P], bpow[:, ri, p, :])
                    give(ri, last, ("lift", q, ri))
                for g2 in range(2):
                    take(g2)
                    rows = slice(g2 * NS, (g2 + 1) * NS)
                    for p in PAIRS:
                        for ri in range(2):
                            last = nc.tensor.matmul(bank[g2][:, p * CH:(p + 1) * CH], bpow[rows, ri, p, :],
                                                    ct[rows, ri, q * PQ + p, :], start=(ri == 0), stop=(ri == 1))
                    give(g2, last, ("kern", q, g2))
                pe.wait_ge(kern_ready, 2 * q + 2)
                if q == 0:
                    pe.wait_ge(shifts_ready, 1)
                for jh in range(2):
                    take(jh)
                    for j in range(4):
                        last = nc.tensor.matmul(bank[jh][:, j * P:(j + 1) * P], shifts[:, 7 - 4 * jh - j, :],
                                                kern[:].rearrange("p g o -> p (g o)"), start=True, stop=True)
                    give(jh, last, ("toep", q, jh))

            def chunk_inputs(q):
                pe.wait_ge(uc_in[q % 2], 16 * (q // 2 + 1))
                pe.wait_ge(lift_ready, 2 * q + 2)
                for ri in range(2):
                    take(6 + ri)
                    for p in PAIRS:
                        for g2 in range(2):
                            last = nc.tensor.matmul(
                                bank[6 + ri][g2 * NS:(g2 + 1) * NS, p * NC:(p + 1) * NC],
                                lift[q % 2][:, ri, p, g2 * NS:(g2 + 1) * NS], uc[q % 2][:, 2 * p + g2, :],
                                start=True, stop=True)
                    give(6 + ri, last, ("S", q, ri))

            def chunk_outputs(q):
                pe.wait_ge(toep_ready, 2 * q + 2)
                pe.wait_ge(readout_ready, q + 1)
                pe.wait_ge(states_ready, q + 1)
                take(4, 5)
                for p in PAIRS:
                    for g2 in range(2):
                        nc.tensor.matmul(bank[4 + g2][:, p * NC:(p + 1) * NC], toep[q % 2][:, 2 * p + g2, :],
                                         uc[q % 2][:, 2 * p + g2, :], start=True, stop=False)
                    for ri in range(2):
                        for g2 in range(2):
                            rows = slice(g2 * NS, (g2 + 1) * NS)
                            last = nc.tensor.matmul(bank[4 + g2][:, p * NC:(p + 1) * NC],
                                                    readout[q % 2][rows, ri, p, :], states[rows, ri, p, 0:NC],
                                                    start=False, stop=(ri == 1))
                            if p == PQ - 1 and ri == 1 and g2 == 0:
                                give(4, last, ("y", q, 0))
                give(5, last, ("y", q, 1))

            def kv_piece(n):
                slab_loaded(pe, 3 + n)
                w = slab[slabs[3 + n][2]]
                if n == 0:
                    pe.wait_ge(memT_ready, MT * KD)
                if n < 2:
                    for m in range(4):
                        take(m)
                        for k in range(KD):
                            last = nc.tensor.matmul(bank[m][:, 0:M], w[:, k, m * P:(m + 1) * P], memT[:, k, :],
                                                    start=(k == 0), stop=(k == KD - 1))
                        give(m, last, ("k", 4 * n + m))
                else:
                    for mt in range(MT):
                        take(mt)
                        for k in range(KD):
                            last = nc.tensor.matmul(bank[mt][:], memT[:, k, mt * P:(mt + 1) * P], w[:, k, :],
                                                    start=(k == 0), stop=(k == KD - 1))
                        give(mt, last, ("v", n - 2, mt))

            def glu(q):
                pe.wait_ge(gelu_done, q + 1)
                if q == 0:
                    pe.wait_ge(glu_in, 16 * 2 * GQ)
                for jh in range(2):
                    for e in range(2):
                        take(2 + e)
                        last = nc.tensor.matmul(bank[2 + e][:], glu_lhs[:, q, e, :],
                                                y_feat[:, 4 * jh:4 * jh + 4, :].rearrange("p j c -> p (j c)"),
                                                start=True, stop=True)
                        give(2 + e, last, ("glu", q, jh, e))

            def channel_means(src, ready, key):
                for half in range(2):
                    pe.wait_ge(ready, half + 1 if ready is not conv_done else KC)
                    take(2 + half)
                    for k in range(KC):
                        last = nc.tensor.matmul(bank[2 + half][:], means[:], src(k, half),
                                                start=(k == 0), stop=(k == KC - 1))
                    give(2 + half, last, (key, half))

            setup(0)
            for q in range(NQ):
                chunk_inputs(q)
                kv_piece(q)
                if q > 0:
                    glu(q - 1)
                chunk_outputs(q)
                if q + 1 < NQ:
                    setup(q + 1)
                if q == 0:
                    channel_means(lambda k, half: conv_acc[:, k, half * BANK:(half + 1) * BANK], conv_done, "mean")
                if q == 1:
                    channel_means(lambda k, half: squares[:, half, k, :], squared, "lnvar")
            glu(NQ - 1)

            pe.wait_ge(yssm_ready, 2 * NQ)
            pe.wait_ge(yconv_ready, KC)
            slab_loaded(pe, 7)
            slab_loaded(pe, 8)
            for t in range(NT):
                for half in range(2):
                    b = 2 * (t % 2) + half
                    take(b)
                    for k in range(KD):
                        last = nc.tensor.matmul(bank[b][:], yT[:, (k + KC) % KD, t * P:(t + 1) * P],
                                                slab[half][:, k, :], start=(k == 0), stop=(k == KD - 1))
                    give(b, last, ("h1", t, half))
                if t > 0:
                    turn_rows(n1, xs[(t - 1) % 2], t - 1, (4, 5), "h1T")
            turn_rows(n1, xs[(NT - 1) % 2], NT - 1, (4, 5), "h1T")

            pe.wait_ge(n1.stored, NT)
            for m in range(KD):
                slab_loaded(pe, 9 + m // 4)
                w = slab[slabs[9 + m // 4][2]]
                for half in range(2):
                    b = 2 * (m % 2) + half
                    take(b)
                    for k in range(KD):
                        last = nc.tensor.matmul(bank[b][:], w[:, k, (m % 4) * P:(m % 4 + 1) * P],
                                                hT[:, k, half * BANK:(half + 1) * BANK],
                                                start=(k == 0), stop=(k == KD - 1))
                    give(b, last, ("q", m, half))

            pe.wait_ge(kv_ready, 12)
            pe.wait_ge(q_ready, 2 * KD)
            for s in range(NT + 4):
                if s < NT:
                    for b in range(2):
                        take(b)
                        for hd in (2 * b, 2 * b + 1):
                            for k in range(HK):
                                last = nc.tensor.matmul(bank[b][:, (hd % 2) * M:(hd % 2 + 1) * M],
                                                        qT[:, HK * hd + k, s * P:(s + 1) * P], kT[:, HK * hd + k, :],
                                                        start=(k == 0), stop=(k == HK - 1))
                        give(b, last, ("s", s, b))
                t = s - 1
                if 0 <= t < NT:
                    pe.wait_ge(probs_ready, t + 1)
                    for b in range(2):
                        take(4 + b)
                        for i in range(4):
                            hd, mt = 2 * b + i // 2, i % 2
                            last = turn(bank[4 + b][:, i * P:(i + 1) * P], probs[t % 2][:, hd, mt * P:(mt + 1) * P])
                        give(4 + b, last, ("pT", t, b))
                t = s - 2
                if 0 <= t < NT:
                    pe.wait_ge(oT_ready, 2 * t + 2)
                    for half in range(2):
                        slab_loaded(pe, 11 + half)
                        take(2 + half)
                        for k in range(KD):
                            last = nc.tensor.matmul(bank[2 + half][:], oT[:, k, t * P:(t + 1) * P],
                                                    slab[slabs[11 + half][2]][:, k, :],
                                                    start=(k == 0), stop=(k == KD - 1))
                        give(2 + half, last, ("h2", t, half))
                t = s - 1
                if 0 <= t < NT:
                    pe.wait_ge(pT_ready, 2 * t + 2)
                    for b in range(2):
                        take(6 + b)
                        for m in range(4 * b, 4 * b + 4):
                            for mt in range(MT):
                                last = nc.tensor.matmul(bank[6 + b][:, (m % 4) * P:(m % 4 + 1) * P],
                                                        vm[:, mt, m * P:(m + 1) * P],
                                                        pT[t % 2][:, (m // HK) * MT + mt, :],
                                                        start=(mt == 0), stop=(mt == MT - 1))
                        give(6 + b, last, ("o", t, b))
                t = s - 3
                if 0 <= t < NT:
                    turn_rows(nf, xs[t % 2], t, (4, 5), "h2T")
                t = s - 4
                if 0 <= t < NT:
                    pe.wait_ge(nf.stored, t + 1)
                    pe.wait_ge(router_in, 16 * 3)
                    take(6)
                    for k in range(KD):
                        last = nc.tensor.matmul(bank[6][:, 0:NR], fT[t % 2][:, k, :], router_w[:, k, :],
                                                start=(k == 0), stop=(k == KD - 1))
                    give(6, last, ("router", t))

            pe.wait_ge(both_ready, 1)
            pe.wait_ge(route_consts, 5)
            take(0, 1)
            mask = both[:].rearrange("p t e -> p (t e)")
            give(0, nc.tensor.matmul(bank[0][:, 0:NT * NE], upper[:], mask, start=True, stop=True), "rank")
            give(1, nc.tensor.matmul(bank[1][:, 0:NT * NE], ones[:], mask, start=True, stop=True), "total")
            take(2)
            pe.wait_ge(sel_ready, 1)
            for i in range(2 * NT):
                last = nc.tensor.matmul(bank[2][:, 0:NB], row_of[:, i, :], block_of[:, i, :],
                                        start=(i == 0), stop=(i == 2 * NT - 1))
            last.then_inc(sel_used, 1)
            bank_uses[2] += 1
            take(*range(8))

            def turn_tokens(b, n):
                pe.wait_ge(xg_in[b], 16 * n)
                for c in range(KD):
                    last = turn(bank[c // 4][:, (c % 4) * P:(c % 4 + 1) * P], xg[b][:, c:D:KD])
                last.then_inc(xg_turned, 1)

            def expert_up(b, n, i):
                pe.wait_ge(xgT_ready, i + 1)
                for w, done in ((0, up1_done), (1, up3_done)):
                    pe.wait_ge(w_in_sem[b][w], 16 * n)
                    for c in range(KD):
                        last = nc.tensor.matmul(bank[2 + w][:], xgT[b][:, c, :], wb[b][w][:, c, :],
                                                start=(c == 0), stop=(c == KD - 1))
                    last.then_inc(done, 1)

            def expert_down(b, n, i):
                pe.wait_ge(hid_ready, i + 1)
                for f in range(KF):
                    last = turn(bank[4][:, f * P:(f + 1) * P], hid[b][:, f:F:KF])
                last.then_inc(hid_turned, 1)
                pe.wait_ge(w_in_sem[b][2], 16 * n)
                pe.wait_ge(hidT_ready, i + 1)
                wait_for(pe, yb_ready, i)
                w2 = wb[b][2][:].rearrange("p c n -> p (c n)").rearrange("p (f d) -> p f d", f=KF)
                for half in range(2):
                    for f in range(KF):
                        last = nc.tensor.matmul(bank[5 + half][:], hidT[b][:, f, :],
                                                w2[:, f, half * BANK:(half + 1) * BANK],
                                                start=(f == 0), stop=(f == KF - 1))
                last.then_inc(down_done, 1)

            def pair(j, final):
                for b in range(2):
                    expert_up(b, j + 1, 2 * j + b)
                    if not (final and b == 1):
                        turn_tokens(1 - b, j + 1 + b)
                    expert_down(b, j + 1, 2 * j + b)

            turn_tokens(0, 1)
            pair(0, False)
            with pe.Fori(1, NE // 2 - 1) as j:
                pair(j, False)
            pair(NE // 2 - 1, True)

            further = pe.value_load(meta[0:1, MAXOV:MAXOV + 1], min_val=0, max_val=MAXOV)
            with pe.Fori(0, MAXOV // 2) as o:
                with pe.If(2 * o < further):
                    turn_tokens(0, NE // 2 + o + 1)
                    pair(NE // 2 + o, True)

        @block.sync
        def _(sp):
            def load_slab(n):
                w, c0, place, after = slabs[n]
                if after:
                    full(sp, after)
                sp.dma_start(slab[place][:], col_major(w, c0, BANK)).then_inc(slab_in[place], 16)

            x_rows = x[0].rearrange("(t p) d -> t p d", p=P)
            for t in range(4):
                sp.dma_start(h[:, t, :], x_rows[t]).then_inc(x_in[t], 16)
            load_slab(0)
            for t in range(4, NT):
                sp.dma_start(h[:, t, :], x_rows[t]).then_inc(x_in[t], 16)
            load_slab(1)
            load_slab(2)
            sp.wait_ge(nx.scaled, 7)
            sp.dma_start(mem_rows[:], mem[0].rearrange("(t p) d -> p t d", p=P)).then_inc(mem_in, 16)
            load_slab(3)
            load_slab(4)
            for q in range(NQ):
                sp.wait_ge(u_ready, 2 * q + 2)
                sp.dma_start(u_bounce[q].rearrange("g h j c -> (g h) (j c)"),
                             u_perm[:, q].rearrange("p j c -> p (j c)")).then_inc(ub_out, 16)
                sp.wait_ge(ub_out, 16 * q + 16)
                if q < 2:
                    sp.dma_start(uc[q][:], u_bounce[q].rearrange("g h j c -> (h j) g c")).then_inc(uc_in[q], 16)
            load_slab(5)
            for q in range(NQ):
                sp.wait_ge(ychunk_ready, 2 * q + 2)
                sp.dma_start(y_bounce[q].rearrange("g h j c -> (h j) g c"), y_chunks[:]).then_inc(yb_out, 16)
                sp.wait_ge(yb_out, 16 * q + 16)
                if q > 0:
                    full(sp, ("glu", q - 1, 1, 1))
                if q == 0:
                    full(sp, ("m", 1, 1))
                sp.dma_start(y_feat[:].rearrange("p j c -> p (j c)"),
                             y_bounce[q].rearrange("g h j c -> (g h) (j c)")).then_inc(yf_in, 16)
                if q + 2 < NQ:
                    full(sp, ("y", q, 1))
                    sp.dma_start(uc[q % 2][:], u_bounce[q + 2].rearrange("g h j c -> (h j) g c"))\
                      .then_inc(uc_in[q % 2], 16)
                if q < 3:
                    load_slab(6 + q)
            load_slab(9)
            full(sp, ("glu", NQ - 1, 1, 1))
            for t in range(NT):
                sp.dma_start(h[:, t, :], x_rows[t]).then_inc(x_in[t], 16)
            for n in (10, 11, 12):
                load_slab(n)

            def load_expert(b, e, before):
                for w, weights in enumerate((moe_w1, moe_w3, moe_w2)):
                    before(w)
                    sp.dma_start(wb[b][w][:].rearrange("p c n -> p (c n)"),
                                 weights[0, bass.ds(e, 1)].rearrange("o (p c) f -> p (o c f)", p=P))\
                      .then_inc(w_in_sem[b][w], 16)

            used = (up1_done, up3_done, down_done)
            load_expert(0, 0, lambda w: full(sp, (("q", 7, 1), ("h2", NT - 1, 0), ("h2", NT - 1, 1))[w]))
            load_expert(1, 1, lambda w: full(sp, ("o", NT - 1, 1)))
            with sp.Fori(1, NE // 2) as j:
                for b in range(2):
                    load_expert(b, 2 * j + b, lambda w: sp.wait_ge(used[w], 2 * j + b - 1))
            full(sp, "total")
            sp.wait_ge(gidx_ready, 1)
            further = sp.value_load(meta[0:1, MAXOV:MAXOV + 1], min_val=0, max_val=MAXOV)
            with sp.Fori(0, MAXOV // 2) as o:
                with sp.If(2 * o < further):
                    for b in range(2):
                        e = sp.value_load(meta[0:1, bass.ds(2 * o + b, 1)], min_val=0, max_val=NE - 1)
                        load_expert(b, e, lambda w: sp.wait_ge(used[w], NE + 2 * o + b - 1))

            sp.dma_start(fin_w[:], final_norm_w.partition_broadcast(P)).then_inc(final_w_in, 16)
            sp.wait_ge(over_done, 1)
            pairs = y_rows.rearrange("(t p k) d -> t p k d", p=P, k=2)
            for t in range(NT):
                if t >= NY:
                    sp.wait_ge(comb, t - NY + 1)
                sp.dma_start(ytile[t % NY][:], pairs[t]).then_inc(y_in[t % NY], 16)

        @block.gpsimd
        def _(pool):
            link = linker(pool, pool_step)
            link(nc.gpsimd.memset(ident[:], 0.0))
            nc.gpsimd.affine_select(out=ident[:], in_=ident[:], compare_op=ALU.not_equal, fill=1.0, base=0,
                                    pattern=[[-1, P]], channel_multiplier=1).then_inc(consts_ready, 1)
            nc.gpsimd.memset(means[:], 1.0 / DC).then_inc(consts_ready, 1)
            for ri, b in enumerate((B_re, B_im)):
                pool.dma_start(b_raw[:, ri], b[0].rearrange("(n g) p h -> (g p) n h", g=2)).then_inc(braw_in, 16)
            pool.wait_ge(params_in, 16 * 12)
            nc.gpsimd.tensor_copy(a_raw[:, 2, :].rearrange("n (g p) -> n g p", g=2),
                                  dt_raw[:].unsqueeze(2).to_broadcast([NP, 2, NS])).then_inc(consts_ready, 1)
            link(nc.gpsimd.memset(glu_lhs[:], 0.0))
            for g in range(GQ):
                for e in range(2):
                    pool.dma_start(glu_lhs[g * CH:(g + 1) * CH, :, e, g * CH:(g + 1) * CH],
                                   glu_w[0].rearrange("(q g) h (e o) -> g e h q o", g=GQ, e=2)[g, e])\
                        .then_inc(glu_in, 16)
            pool.wait_ge(nx.squares, NT)
            nc.gpsimd.memset(conv_in[:, :, 0:PAD], 0.0).then_inc(v_ready, 1)
            pool.wait_ge(nx.scaled, NT)
            link(nc.gpsimd.memset(shifts[:], 0.0))
            for d in range(T):
                part = shifts[:, d, :].rearrange("p (h j) -> p h j", j=T)[:, :, 0:T - d]
                last = nc.gpsimd.affine_select(out=part, in_=part, compare_op=ALU.not_equal, fill=1.0, base=-d,
                                               pattern=[[-T, CH], [-1, T - d]], channel_multiplier=1)
            last.then_inc(shifts_ready, 1)

            def gated(i, half):
                n = 2 * i + half + 1
                pool.wait_ge(conv_a_ready, n)
                pool.wait_ge(conv_sg_ready, n)
                nc.gpsimd.tensor_tensor(conv_in[:, i, PAD + half * BANK:PAD + (half + 1) * BANK],
                                        conv_a[:], conv_sg[:], ALU.mult).then_inc(v_ready, 1)

            def power_up(dst, src, coef, conj, shape, ready=None, count=0):
                n = 1
                for x in shape:
                    n *= x

                def flat(i):
                    t = pool_tmp[:, i, 0:n]
                    return t.rearrange("p (a b c) -> p a b c", a=shape[0], b=shape[1]) if len(shape) == 3 \
                        else t.rearrange("p (a b) -> p a b", a=shape[0])
                re, im = coef
                nc.gpsimd.tensor_tensor(flat(0), src[0], re, ALU.mult)
                nc.gpsimd.tensor_tensor(flat(1), src[1], im, ALU.mult)
                nc.gpsimd.tensor_tensor(flat(2), src[1], re, ALU.mult)
                link(nc.gpsimd.tensor_tensor(flat(3), src[0], im, ALU.mult))
                nc.gpsimd.tensor_tensor(dst[0], flat(0), flat(1), ALU.add if conj else ALU.subtract)
                last = nc.gpsimd.tensor_tensor(dst[1], flat(2), flat(3), ALU.subtract if conj else ALU.add)
                if ready is None:
                    link(last)
                else:
                    last.then_inc(ready, 1)
                    pool.wait_ge(ready, count)

            def tables(q):
                if q == 0:
                    pool.wait_ge(setup_ready, 1)
                ps = slice(q * PQ, (q + 1) * PQ)
                vin = bpow[:].rearrange("p r n (h s) -> p r n h s", s=T)
                vout = readout[q % 2][:].rearrange("p r n (h s) -> p r n h s", s=T)

                def coef(k, w):
                    return [pw[:, ri, k, ps].unsqueeze(2).unsqueeze(3).to_broadcast([P, PQ, CH, w])
                            for ri in range(2)]
                if q > 0:
                    full(pool, ("lift", q - 1, 1))
                    full(pool, ("kern", q - 1, 1))
                for ri in range(2):
                    last = nc.gpsimd.tensor_copy(vin[:, ri, :, :, T - 1], bbar[:, ri, ps, :])
                link(last)
                for k, w in enumerate((1, 2, 4)):
                    a, b = T - 2 * w, T - w
                    power_up([vin[:, ri, :, :, a:b] for ri in range(2)],
                             [vin[:, ri, :, :, b:b + w] for ri in range(2)], coef(k, w), False, (PQ, CH, w),
                             bpow_ready if k == 2 else None, q + 1)
                if q >= 2:
                    full(pool, ("y", q - 2, 1))
                if q == 1:
                    full(pool, ("u", KC - 1, 1))
                power_up([vout[:, ri, :, :, 0:1] for ri in range(2)],
                         [ct[:, ri, ps, :].unsqueeze(3) for ri in range(2)], coef(0, 1), True, (PQ, CH, 1))
                for k, w in enumerate((1, 2, 4)):
                    power_up([vout[:, ri, :, :, w:2 * w] for ri in range(2)],
                             [vout[:, ri, :, :, 0:w] for ri in range(2)], coef(k, w), True, (PQ, CH, w),
                             readout_ready if k == 2 else None, q + 1)
                if q >= 2:
                    pool.wait_ge(states_ready, q - 1)
                e = phase[q % 2]
                nc.gpsimd.memset(e[:, 0, :, 0:1], 1.0)
                link(nc.gpsimd.memset(e[:, 1, :, 0:1], 0.0))
                for k in range(7):
                    w = 1 << k
                    power_up([e[:, ri, :, w:2 * w] for ri in range(2)], [e[:, ri, :, 0:w] for ri in range(2)],
                             [ph[:, ri, k, ps].unsqueeze(2).to_broadcast([P, PQ, w]) for ri in range(2)],
                             False, (PQ, w), phase_ready if k == 6 else None, q + 1)

            for i in range(KC):
                gated(i, 0)
                gated(i, 1)
                if i == 1:
                    tables(0)
            for q in range(1, NQ):
                tables(q)

            full(pool, ("router", NT - 1))
            for b in range(2):
                pool.wait_ge(xn_out[b], 16 * NT // 2)
            link(nc.gpsimd.memset(upper[:], 1.0))
            nc.gpsimd.affine_select(out=upper[:], in_=upper[:], compare_op=ALU.is_gt, fill=0.0, base=0,
                                    pattern=[[1, P]], channel_multiplier=-1).then_inc(route_consts, 1)
            nc.gpsimd.memset(ones[:], 1.0).then_inc(route_consts, 1)
            iota = dict(allow_small_or_imprecise_dtypes=True)
            nc.gpsimd.iota(iota_n[:], pattern=[[1, P]], base=0, channel_multiplier=0, **iota).then_inc(route_consts, 1)
            nc.gpsimd.iota(assign_no[:], pattern=[[1, 2], [2 * P, NT]], base=1, channel_multiplier=2, **iota)\
                .then_inc(route_consts, 1)
            nc.gpsimd.iota(limits[:], pattern=[[P, 7]], base=P, channel_multiplier=0, **iota).then_inc(route_consts, 1)

            last_token = pool.to_reg(S - 1)
            last_row = pool.to_reg(2 * S - 1)

            def fetch(b):
                pool.sem_inc(rows_moved, 1)
                nc.gpsimd.indirect_dma_start(
                    out=xg[b][:], out_offset=None, in_=xn_rows,
                    in_offset=bass.IndirectOffsetOnAxis(ap=gidx[b][:, 0:1], axis=0),
                    bounds_check=last_token, oob_is_err=False).then_inc(xg_in[b], 16)

            def send(b, i):
                pool.wait_ge(sidx_ready, i + 1)
                pool.wait_ge(yb_ready, i + 1)
                pool.sem_inc(rows_moved, 1)
                nc.gpsimd.indirect_dma_start(
                    out=y_rows, out_offset=bass.IndirectOffsetOnAxis(ap=sidx[b][:, 0:1], axis=0),
                    in_=yb[b][:], in_offset=None,
                    bounds_check=last_row, oob_is_err=False).then_inc(y_sent[b], 16)

            pool.wait_ge(sel_used, 1)
            for b in range(2):
                nc.gpsimd.memset(xg[b][:], 0.0).then_inc(xg_clear, 1)
            pool.wait_ge(xg_clear, 2)
            for b in range(2):
                pool.wait_ge(gidx_ready, b + 1)
                fetch(b)
            with pool.Fori(0, NE // 2 - 1) as j:
                for b in range(2):
                    send(b, 2 * j + b)
                    pool.wait_ge(gidx_ready, 2 * j + b + 3)
                    pool.wait_ge(xg_turned, 2 * j + b + 1)
                    fetch(b)
            for b in range(2):
                send(b, NE - 2 + b)
            further = pool.value_load(meta[0:1, MAXOV:MAXOV + 1], min_val=0, max_val=MAXOV)
            with pool.Fori(0, MAXOV // 2) as o:
                with pool.If(2 * o < further):
                    for b in range(2):
                        pool.wait_ge(gidx_ready, NE + 2 * o + b + 1)
                        fetch(b)
                    for b in range(2):
                        send(b, NE + 2 * o + b)
                    for b in range(2):
                        pool.wait_ge(y_sent[b], 16 * (NE // 2 + 1) + 16 * o)
            for b in range(2):
                pool.wait_ge(y_sent[b], 16 * (NE // 2))
            nc.gpsimd.memset(pool_mark[:], 0.0).then_inc(over_done, 1)

            out_rows = out[0].rearrange("(t p) d -> t p d", p=P)
            for t in range(NT):
                pool.wait_ge(out_ready, t + 1)
                pool.dma_start(out_rows[t], otile[t % 2][:]).then_inc(out_stored[t % 2], 16)
            for b in range(2):
                pool.wait_ge(out_stored[b], 16 * NT // 2)

        @block.scalar
        def _(act):
            link = linker(act, act_step)
            rows = ((norm_mix_w, 0), (norm_x_w, 8), (norm_mem_w, 16), (norm_ffn_w, 24))
            for w, r in rows:
                act.dma_start(rows_raw[r:r + KD, :], w[0].rearrange("(c p) -> c p", p=P)).then_inc(params_in, 16)
            for i, w in enumerate((conv_b, conv_ln_w, conv_ln_b, ssm_D.rearrange("a g c -> a (g c)"))):
                act.dma_start(rows_raw[32 + 4 * i:36 + 4 * i, :],
                               w[0].rearrange("(c p) -> c p", p=P)).then_inc(params_in, 16)
            act.dma_start(taps_raw[0:TAPS * KC, :], conv_w[0].rearrange("k (c p) -> (k c) p", p=P))\
                .then_inc(params_in, 16)
            act.dma_start(a_raw[:, 0, :], A_re[0].rearrange("(n g) p -> n (g p)", g=2)).then_inc(params_in, 16)
            act.dma_start(a_raw[:, 1, :], A_im[0].rearrange("(n g) p -> n (g p)", g=2)).then_inc(params_in, 16)
            act.dma_start(dt_raw[:], log_dt[0].rearrange("(n g) -> n g", g=2)).then_inc(params_in, 16)
            act.dma_start(c_raw[:, 0, :].rearrange("h (g p) -> h g p", p=NS),
                           C_re[0].rearrange("g h p -> h g p")).then_inc(craw_in, 16)
            act.dma_start(c_raw[:, 1, :].rearrange("h (g p) -> h g p", p=NS),
                           C_im[0].rearrange("g h p -> h g p")).then_inc(craw_in, 16)
            act.dma_start(par[:, 48:56], norm_ffn_w[0].rearrange("(p c) -> p c", p=P)).then_inc(par_in, 16)

            def act_squares(norm, src, t, scratch, st):
                if t > 0:
                    act.wait_ge(norm.squares, t)
                nc.scalar.activation(scratch, src, ACT.Square, accum_out=st[:, 0, t:t + 1])\
                    .then_inc(norm.squares, 1)

            def act_root(norm, t, st):
                act.wait_ge(norm.var, t + 1)
                nc.scalar.activation(st[:, 1, t:t + 1], st[:, 1, t:t + 1], ACT.Sqrt).then_inc(norm.root, 1)

            def act_scale(norm, dst, src, t, st):
                act.wait_ge(norm.rstd, t + 1)
                nc.scalar.activation(dst, src, ACT.Copy, scale=st[:, 2, t:t + 1]).then_inc(norm.scaled, 1)

            act.wait_ge(x_in[0], 16)
            act_squares(nx, h[:, 0, :], 0, junk_x[:], stat)
            for t in range(NT):
                if t + 1 < NT:
                    act.wait_ge(x_in[t + 1], 16)
                    act_squares(nx, h[:, t + 1, :], t + 1, junk_x[:], stat)
                act_root(nx, t, stat)
            act.wait_ge(trig_in, 1)
            nc.scalar.activation(t16[:, 9], t16[:, 4], ACT.Sin).then_inc(trig_out, 1)
            nc.scalar.activation(t16[:, 10], t16[:, 4], ACT.Sin, scale=0.5).then_inc(trig_out, 1)
            act.wait_ge(mem_in, 16)
            act.wait_ge(nx.scaled, NT)
            for t in range(MT):
                act_squares(nm, mem_rows[:, t, :], t, junk_m[:], stat_m)
                act_root(nm, t, stat_m)
                act_scale(nm, mem_rows[:, t, :], mem_rows[:, t, :], t, stat_m)

            for i in range(KC):
                for half in range(2):
                    n = 2 * i + half
                    if n > 0:
                        act.wait_ge(v_ready, n + 1)
                    src = full(act, ("a", i, half))
                    nc.scalar.activation(conv_a[:], src[:], ACT.Copy).then_inc(conv_a_ready, 1)
                    act.wait_ge(conv_a_ready, n + 1)
                    nc.scalar.sem_inc(bank_free[half], 1)
                    src = full(act, ("g", i, half))
                    nc.scalar.activation(conv_sg[:], src[:], ACT.Sigmoid).then_inc(conv_sg_ready, 1)
                    act.wait_ge(conv_sg_ready, n + 1)
                    nc.scalar.sem_inc(bank_free[2 + half], 1)
            for q in range(NQ):
                for half in range(2):
                    src = full(act, ("u", q, half))
                    nc.scalar.activation(u_perm[:, q, :, half * NC // 2:(half + 1) * NC // 2],
                                         src[:].rearrange("p (c j) -> p j c", j=T), ACT.Copy).then_inc(u_ready, 1)
                    act.wait_ge(u_ready, 2 * q + half + 1)
                    nc.scalar.sem_inc(bank_free[4 + half], 1)
            for t in range(MT):
                for c in range(KD):
                    src = full(act, ("m", t, c // 4))
                    nc.scalar.activation(memT[:, c, t * P:(t + 1) * P], src[:, (c % 4) * P:(c % 4 + 1) * P], ACT.Copy,
                                         scale=par[:, 16 + c:17 + c]).then_inc(memT_ready, 1)
                    if c % 4 == 3:
                        act.wait_ge(memT_ready, t * KD + c + 1)
                        nc.scalar.sem_inc(bank_free[6 + c // 4], 1)

            def read_out(key, dst, src, ready, count, **how):
                b, _ = use_of[key]
                full(act, key)
                nc.scalar.activation(dst, src(bank[b]), how.pop("func", ACT.Copy), **how).then_inc(ready, 1)
                act.wait_ge(ready, count)
                nc.scalar.sem_inc(bank_free[b], 1)

            def setup_out(q):
                for ri in range(2):
                    if ri == 0 and q >= 2:
                        full(act, ("S", q - 2, 1))
                    read_out(("lift", q, ri), lift[q % 2][:, ri].rearrange("p n m -> p (n m)"), lambda b: b[:],
                             lift_ready, 2 * q + ri + 1)
                for g2 in range(2):
                    if q > 0 and g2 == 0:
                        full(act, ("toep", q - 1, 1))
                    read_out(("kern", q, g2), kern[:].rearrange("p (n g) o -> p g n o", g=2)[:, g2],
                             lambda b: b[:, 0:PQ * CH].rearrange("p (n o) -> p n o", o=CH), kern_ready, 2 * q + g2 + 1)
                for jh in range(2):
                    if q >= 2 and jh == 0:
                        full(act, ("y", q - 2, 1))
                    read_out(("toep", q, jh),
                             toep[q % 2][:].rearrange("p g (o j) -> p j g o", j=T)[:, 4 * jh:4 * jh + 4],
                             lambda b: b[:].rearrange("p (j g o) -> p j g o", j=4, g=GQ), toep_ready, 2 * q + jh + 1)

            kv = [0]

            def kv_out(n):
                if n < 2:
                    for m in range(4):
                        kv[0] += 1
                        read_out(("k", 4 * n + m), kT[:, 4 * n + m, :], lambda b: b[:, 0:M], kv_ready, kv[0])
                else:
                    for mt in range(MT):
                        kv[0] += 1
                        read_out(("v", n - 2, mt), vm[:, mt, (n - 2) * BANK:(n - 1) * BANK], lambda b: b[:],
                                 kv_ready, kv[0])

            def glu_gates(q):
                act.wait_ge(dterm_done, q + 1)
                nc.scalar.activation(y_feat[:], y_feat[:], ACT.Gelu_apprx_tanh).then_inc(gelu_done, 1)
                for jh in range(2):
                    n = 2 * q + jh
                    if n > 0:
                        act.wait_ge(yssm_ready, n)
                    read_out(("glu", q, jh, 1), glu_sig[:], lambda b: b[:], glu_sig_ready, n + 1, func=ACT.Sigmoid)

            setup_out(0)
            for q in range(NQ):
                kv_out(q)
                if q > 0:
                    glu_gates(q - 1)
                for g2 in range(2):
                    if g2 == 0 and q > 0:
                        act.wait_ge(yb_out, 16 * q)
                    read_out(("y", q, g2), y_chunks[:].rearrange("p (n g) c -> p g n c", g=2)[:, g2],
                             lambda b: b[:].rearrange("p (n c) -> p n c", c=NC), ychunk_ready, 2 * q + g2 + 1)
                if q + 1 < NQ:
                    setup_out(q + 1)
                if q == 0:
                    for half in range(2):
                        act.wait_ge(centered, half + 1)
                        nc.scalar.activation(squares[:, half], conv_acc[:, :, half * BANK:(half + 1) * BANK],
                                             ACT.Square).then_inc(squared, 1)
                if q == 1:
                    act.wait_ge(ln_v, 2)
                    nc.scalar.activation(ln_var[:], ln_var[:], ACT.Sqrt).then_inc(ln_root, 1)
                    act.wait_ge(ln_scaled, 2)
                    for k in range(KC):
                        nc.scalar.activation(conv_acc[:, k, :], conv_acc[:, k, :], ACT.Silu,
                                             bias=par[:, 40 + k:41 + k], scale=par[:, 36 + k:37 + k])\
                            .then_inc(yconv_ready, 1)
            glu_gates(NQ - 1)

            full(act, ("glu", NQ - 1, 1, 1))
            act.dma_start(router_w[:, :, 0:NG], router_group_w[0].rearrange("(c p) n -> p c n", p=P))\
               .then_inc(router_in, 16)
            act.dma_start(router_w[:, :, NG:NR], router_expert_w[0].rearrange("(c p) n -> p c n", p=P))\
               .then_inc(router_in, 16)
            act.dma_start(router_b[:, 0:NG], router_group_b[0].partition_broadcast(P)).then_inc(router_in, 16)
            act.dma_start(router_b[:, NG:NR], router_expert_b[0].rearrange("g e -> (g e)").partition_broadcast(P))\
               .then_inc(router_in, 16)

            for t in range(NT):
                act.wait_ge(h1_ready, 2 * t + 2)
                act_squares(n1, h[:, t, :], t, junk[:], stat)
                act_root(n1, t, stat)
                if t >= 2:
                    full(act, ("h1T", t - 2, 1))
                act_scale(n1, xs[t % 2][:], h[:, t, :], t, stat)
            for m in range(KD):
                for half in range(2):
                    read_out(("q", m, half), qT[:, m, half * BANK:(half + 1) * BANK], lambda b: b[:],
                             q_ready, 2 * m + half + 1, scale=float(HD) ** -0.5)

            for s in range(NT + 4):
                t = s
                if t < NT:
                    act.wait_ge(negmax_ready, 2 * t + 2)
                    if t >= 2:
                        full(act, ("pT", t - 2, 1))
                    for hd in range(NH):
                        nc.scalar.activation(probs[t % 2][:, hd, :], bank[hd // 2][:, (hd % 2) * M:(hd % 2 + 1) * M],
                                             ACT.Exp, bias=negmax[:, t % 2, hd:hd + 1],
                                             accum_out=expsum[:, t % 2, hd:hd + 1]).then_inc(exp_done, 1)
                        if hd % 2:
                            act.wait_ge(exp_done, NH * t + hd + 1)
                            nc.scalar.sem_inc(bank_free[hd // 2], 1)
                t = s - 2
                if 0 <= t < NT:
                    act.wait_ge(h2_ready, 2 * t + 2)
                    if t == 0:
                        act.wait_ge(n1.squares, NT)
                    act_squares(nf, h[:, t, :], t, junk[:], stat)
                    act_root(nf, t, stat)
                    if t >= 2:
                        full(act, ("h2T", t - 2, 1))
                        act.wait_ge(xn_out[t % 2], 16 * (t // 2))
                    act_scale(nf, xs[t % 2][:], h[:, t, :], t, stat)
                    act.wait_ge(nf.scaled, t + 1)
                    act.dma_start(xn_rows[t * P:(t + 1) * P, :], xs[t % 2][:]).then_inc(xn_out[t % 2], 16)
                t = s - 1
                if 0 <= t < NT:
                    for b in range(2):
                        read_out(("o", t, b), oT[:, 4 * b:4 * b + 4, t * P:(t + 1) * P],
                                 lambda x: x[:].rearrange("p (m n) -> p m n", n=P), oT_ready, 2 * t + b + 1)
                t = s - 4
                if 0 <= t < NT:
                    read_out(("router", t), logits[:, t, :], lambda b: b[:, 0:NR], logit_ready, t + 1)

            act.wait_ge(gexp_in, 1)
            nc.scalar.activation(gsel[:, 0], gsel[:, 0], ACT.Exp).then_inc(gexp_out, 1)
            act.wait_ge(pexp_in, 1)
            nc.scalar.activation(col[:, 6], col[:, 6], ACT.Exp).then_inc(pexp_out, 1)

            def expert_act(b, n, i):
                act.wait_ge(up1_done, i + 1)
                nc.scalar.activation(gate_act[b][:], bank[2][:], ACT.Silu).then_inc(gate_ready, 1)
                act.wait_ge(hid_turned, i + 1)
                nc.scalar.activation(hidT[b][:].rearrange("p f n -> p (f n)"), bank[4][:], ACT.Copy)\
                    .then_inc(hidT_ready, 1)
                act.wait_ge(down_done, i + 1)
                wait_for(act, y_sent[b], 16 * n - 16)
                nc.scalar.activation(yb[b][:, 0:BANK], bank[5][:], ACT.Copy)
                nc.scalar.activation(yb[b][:, BANK:D], bank[6][:], ACT.Copy).then_inc(yb_ready, 1)

            for b in range(2):
                expert_act(b, 1, b)
            with act.Fori(1, NE // 2) as j:
                for b in range(2):
                    expert_act(b, j + 1, 2 * j + b)
            further = act.value_load(meta[0:1, MAXOV:MAXOV + 1], min_val=0, max_val=MAXOV)
            with act.Fori(0, MAXOV // 2) as o:
                with act.If(2 * o < further):
                    for b in range(2):
                        expert_act(b, NE // 2 + o + 1, NE + 2 * o + b)

            act.wait_ge(comb, 1)
            act_squares(n2, h[:, 0, :], 0, junk_f[:], stat)
            for t in range(NT):
                if t + 1 < NT:
                    act.wait_ge(comb, t + 2)
                    act_squares(n2, h[:, t + 1, :], t + 1, junk_f[:], stat)
                act_root(n2, t, stat)

        @block.vector
        def _(dve):
            link = linker(dve, dve_step)
            V = nc.vector

            def ts(out, a, s1, s2, op0, op1=ALU.bypass):
                return V.tensor_scalar(out, a, s1, s2, op0, op1)

            def stt(out, a, s, b, op0, op1):
                return V.scalar_tensor_tensor(out=out, in0=a, scalar=s, in1=b, op0=op0, op1=op1)

            def tt(out, a, b, op):
                return V.tensor_tensor(out, a, b, op)

            def frees(key, ins):
                ins.then_inc(bank_free[use_of[key][0]], 1)

            def dve_var(norm, t, st):
                dve.wait_ge(norm.squares, t + 1)
                ts(st[:, 1, t:t + 1], st[:, 0, t:t + 1], 1.0 / D, EPS, ALU.mult, ALU.add).then_inc(norm.var, 1)

            def dve_rstd(norm, t, st):
                dve.wait_ge(norm.root, t + 1)
                V.reciprocal(st[:, 2, t:t + 1], st[:, 1, t:t + 1]).then_inc(norm.rstd, 1)

            def dve_store(norm, key, dst, t, c0):
                for b in range(2):
                    src = full(dve, (key, t, b))
                    w = par[:, c0 + 4 * b:c0 + 4 * b + 4].unsqueeze(2).to_broadcast([P, 4, P])
                    link(tt(dst[:, 4 * b:4 * b + 4], src[:].rearrange("p (c n) -> p c n", n=P), w, ALU.mult))
                    V.sem_inc(bank_free[use_of[(key, t, b)][0]], 1)
                V.sem_inc(norm.stored, 1)

            full(dve, "par")
            link(V.tensor_copy(par[:, 0:48], bank[0][:, 0:48]))
            V.sem_inc(bank_free[0], 1)
            dve_var(nx, 0, stat)
            for t in range(NT + 1):
                if t < NT:
                    if t + 1 < NT:
                        dve_var(nx, t + 1, stat)
                    dve_rstd(nx, t, stat)
                    dve.wait_ge(nx.rstd, t + 1)
                    if t >= 2:
                        full(dve, ("x", t - 2, 1))
                    ts(xs0[t % 2][:], h[:, t, :], stat[:, 2, t:t + 1], None, ALU.mult).then_inc(nx.scaled, 1)
                if t > 0:
                    dve_store(nx, "x", xT[:, :, (t - 1) * P:t * P], t - 1, 0)
            full(dve, "taps")
            link(V.tensor_copy(taps[:], bank[1][:, 0:TAPS * KC]))
            V.sem_inc(bank_free[1], 1)
            full(dve, "a_raw")
            link(V.tensor_copy(t16[:, 0:3], bank[2][:, 0:3 * NP].rearrange("p (i n) -> p i n", n=NP)))
            V.sem_inc(bank_free[2], 1)
            full(dve, "c_raw")
            raw = bank[3][:].rearrange("p (r n h) -> p r n h", r=2, n=NP)
            link(V.tensor_copy(ct[:, 0], raw[:, 0]))
            link(ts(ct[:, 1], raw[:, 1], -1.0, None, ALU.mult))
            V.sem_inc(bank_free[3], 1)


            def z(i):
                return t16[:, i]
            are, aim, ldt = z(0), z(1), z(2)

            def expm1_poly(out, f):
                link(ts(out, f, 1.0 / 5040, None, ALU.mult))
                for c in (1.0 / 720, 1.0 / 120, 1.0 / 24, 1.0 / 6, 0.5, 1.0):
                    link(stt(out, out, c, f, ALU.add, ALU.mult))

            link(ts(z(3), ldt, LOG2E, ROUND, ALU.mult, ALU.add))
            link(ts(z(3), z(3), ROUND, None, ALU.subtract))
            link(stt(z(4), z(3), -LN2_HI, ldt, ALU.mult, ALU.add))
            link(stt(z(4), z(3), -LN2_LO, z(4), ALU.mult, ALU.add))
            expm1_poly(z(5), z(4))
            link(ts(z(3), z(3), -127.0, 128.0, ALU.max, ALU.min))
            link(ts(z(6).bitcast(I32), z(3), 127.0, float(1 << 23), ALU.add, ALU.mult))
            link(stt(z(2), z(5), 1.0, z(6), ALU.add, ALU.mult))
            link(tt(z(7), are, z(2), ALU.mult))
            link(tt(z(8), aim, z(2), ALU.mult))
            link(ts(z(7), z(7), -87.0, 1.0 / 256, ALU.max, ALU.mult))
            expm1_poly(z(5), z(7))
            for _ in range(8):
                link(stt(z(5), z(5), 2.0, z(5), ALU.add, ALU.mult))
            link(ts(z(3), z(8), 1.0 / TWO_PI, ROUND, ALU.mult, ALU.add))
            link(ts(z(3), z(3), ROUND, None, ALU.subtract))
            link(stt(z(4), z(3), -TWO_PI_A, z(8), ALU.mult, ALU.add))
            link(stt(z(4), z(3), -TWO_PI_B, z(4), ALU.mult, ALU.add))
            link(stt(z(4), z(3), -TWO_PI_C, z(4), ALU.mult, ALU.add))
            ts(z(4), z(4), -PI_LOW, PI_LOW, ALU.max, ALU.min).then_inc(trig_in, 1)
            dve.wait_ge(trig_out, 2)
            link(stt(z(6), z(10), -2.0, z(10), ALU.mult, ALU.mult))
            link(ts(z(11), z(6), 1.0, None, ALU.add))
            link(ts(z(8), z(5), 1.0, None, ALU.add))
            link(tt(pw[:, 0, 0], z(8), z(11), ALU.mult))
            link(tt(pw[:, 1, 0], z(8), z(9), ALU.mult))
            link(tt(z(3), z(5), z(11), ALU.mult))
            link(tt(z(3), z(3), z(6), ALU.add))
            link(tt(z(4), are, are, ALU.mult))
            link(tt(z(7), aim, aim, ALU.mult))
            link(tt(z(4), z(4), z(7), ALU.add))
            link(V.reciprocal(z(4), z(4)))
            link(tt(z(5), z(3), are, ALU.mult))
            link(tt(z(6), pw[:, 1, 0], aim, ALU.mult))
            link(tt(z(5), z(5), z(6), ALU.add))
            link(tt(z(5), z(5), z(4), ALU.mult))
            link(tt(z(6), pw[:, 1, 0], are, ALU.mult))
            link(tt(z(7), z(3), aim, ALU.mult))
            link(tt(z(6), z(6), z(7), ALU.subtract))
            link(tt(z(6), z(6), z(4), ALU.mult))
            dve.wait_ge(braw_in, 32)
            wre = z(5).unsqueeze(2).to_broadcast([P, NP, CH])
            wim = z(6).unsqueeze(2).to_broadcast([P, NP, CH])
            link(tt(bbar[:, 0], b_raw[:, 0], wre, ALU.mult))
            link(tt(bbar[:, 1], b_raw[:, 1], wim, ALU.mult))
            link(tt(bbar[:, 0], bbar[:, 0], bbar[:, 1], ALU.subtract))
            link(tt(bbar[:, 1], b_raw[:, 1], wre, ALU.mult))
            link(tt(b_raw[:, 0], b_raw[:, 0], wim, ALU.mult))
            link(tt(bbar[:, 1], bbar[:, 1], b_raw[:, 0], ALU.add))

            def square(dre, dim, re, im):
                link(tt(z(3), im, im, ALU.mult))
                link(tt(z(4), re, re, ALU.mult))
                link(stt(dim, re, 2.0, im, ALU.mult, ALU.mult))
                link(tt(dre, z(4), z(3), ALU.subtract))
            square(pw[:, 0, 1], pw[:, 1, 1], pw[:, 0, 0], pw[:, 1, 0])
            square(pw[:, 0, 2], pw[:, 1, 2], pw[:, 0, 1], pw[:, 1, 1])
            link(tt(rho[:], z(8), z(8), ALU.mult))
            link(tt(rho[:], rho[:], rho[:], ALU.mult))
            link(tt(rho[:], rho[:], rho[:], ALU.mult))
            square(z(5), z(6), z(11), z(9))
            square(z(7), z(8), z(5), z(6))
            square(ph[:, 0, 0], ph[:, 1, 0], z(7), z(8))
            for k in range(6):
                square(ph[:, 0, k + 1], ph[:, 1, k + 1], ph[:, 0, k], ph[:, 1, k])
            V.sem_inc(setup_ready, 1)

            for t in range(MT):
                dve_var(nm, t, stat_m)
                dve_rstd(nm, t, stat_m)
            for i in range(KC):
                dve.wait_ge(v_ready, 2 * i + 3)
                link(ts(conv_acc[:, i, :], conv_in[:, i, 0:S], taps[:, i:i + 1], par[:, 32 + i:33 + i],
                        ALU.mult, ALU.add))
                for k in range(1, TAPS):
                    ins = stt(conv_acc[:, i, :], conv_in[:, i, k:k + S], taps[:, k * KC + i:k * KC + i + 1],
                              conv_acc[:, i, :], ALU.mult, ALU.add)
                    if k < TAPS - 1:
                        link(ins)
                ins.then_inc(conv_done, 1)

            def rotate(q):
                cos, sin = phase[q % 2][:, 0], phase[q % 2][:, 1]
                re, im = (bank[6 + ri][:].rearrange("p (n c) -> p n c", c=NC) for ri in range(2))
                dve.wait_ge(phase_ready, q + 1)
                full(dve, ("S", q, 0))
                full(dve, ("S", q, 1))
                tt(rotated[:, 0], re, cos, ALU.mult)
                tt(rot_tmp[:, 0], im, sin, ALU.mult)
                tt(rotated[:, 1], im, cos, ALU.mult)
                link(tt(rot_tmp[:, 1], re, sin, ALU.mult))
                V.sem_inc(bank_free[6], 1)
                V.sem_inc(bank_free[7], 1)
                tt(rotated[:, 0], rotated[:, 0], rot_tmp[:, 0], ALU.add)
                link(tt(rotated[:, 1], rotated[:, 1], rot_tmp[:, 1], ALU.subtract))
                for ri in range(2):
                    for p in PAIRS:
                        n = q * PQ + p
                        last = V.tensor_tensor_scan(scanned[:, ri, p, :], rho[:, n:n + 1].to_broadcast([P, NC]),
                                                    rotated[:, ri, p, :], 0.0, ALU.mult, ALU.add)
                link(last)
                tt(rotated[:, 0], scanned[:, 0], cos, ALU.mult)
                tt(rot_tmp[:, 0], scanned[:, 1], sin, ALU.mult)
                tt(rotated[:, 1], scanned[:, 0], sin, ALU.mult)
                link(tt(rot_tmp[:, 1], scanned[:, 1], cos, ALU.mult))
                if q == 0:
                    link(V.memset(states[:, :, :, 0:1], 0.0))
                else:
                    full(dve, ("y", q - 1, 1))
                tt(states[:, 0, :, 1:NC + 1], rotated[:, 0], rot_tmp[:, 0], ALU.subtract)
                link(tt(states[:, 1, :, 1:NC + 1], rotated[:, 1], rot_tmp[:, 1], ALU.add))
                V.sem_inc(states_ready, 1)

            def direct(q):
                dve.wait_ge(yf_in, 16 * q + 16)
                stt(y_feat[:], u_perm[:, q], par[:, 44 + q:45 + q], y_feat[:], ALU.mult, ALU.add)\
                    .then_inc(dterm_done, 1)

            def gated(q):
                for jh in range(2):
                    n = 2 * q + jh + 1
                    dve.wait_ge(glu_sig_ready, n)
                    src = full(dve, ("glu", q, jh, 0))
                    tt(yT[:, q, :].rearrange("p (c j) -> p j c", j=T)[:, 4 * jh:4 * jh + 4],
                       src[:].rearrange("p (j c) -> p j c", j=4),
                       glu_sig[:].rearrange("p (j c) -> p j c", j=4), ALU.mult).then_inc(yssm_ready, 1)
                    dve.wait_ge(yssm_ready, n)
                    V.sem_inc(bank_free[use_of[("glu", q, jh, 0)][0]], 1)

            def half_of_conv(half):
                return conv_acc[:, :, half * BANK:(half + 1) * BANK]

            rotate(0)
            for half in range(2):
                src = full(dve, ("mean", half))
                tt(half_of_conv(half), half_of_conv(half), src[:].unsqueeze(1).to_broadcast([P, KC, BANK]),
                   ALU.subtract).then_inc(centered, 1)
                dve.wait_ge(centered, half + 1)
                V.sem_inc(bank_free[use_of[("mean", half)][0]], 1)
            direct(0)
            rotate(1)
            gated(0)
            for half in range(2):
                src = full(dve, ("lnvar", half))
                ts(ln_var[:, half], src[:], EPS, None, ALU.add).then_inc(ln_v, 1)
                dve.wait_ge(ln_v, half + 1)
                V.sem_inc(bank_free[use_of[("lnvar", half)][0]], 1)
            dve.wait_ge(ln_root, 1)
            link(V.reciprocal(ln_var[:], ln_var[:]))
            for half in range(2):
                tt(half_of_conv(half), half_of_conv(half), ln_var[:, half].unsqueeze(1).to_broadcast([P, KC, BANK]),
                   ALU.mult).then_inc(ln_scaled, 1)
            direct(1)
            rotate(2)
            gated(1)
            direct(2)
            rotate(3)
            gated(2)
            direct(3)
            gated(3)

            for t in range(NT):
                dve.wait_ge(x_in[t], 32)
                for half in range(2):
                    src = full(dve, ("h1", t, half))
                    part = h[:, t, half * BANK:(half + 1) * BANK]
                    tt(part, part, src[:], ALU.add).then_inc(h1_ready, 1)
                    dve.wait_ge(h1_ready, 2 * t + half + 1)
                    V.sem_inc(bank_free[use_of[("h1", t, half)][0]], 1)
                if t > 0:
                    dve_store(n1, "h1T", hT[:, :, (t - 1) * P:t * P], t - 1, 8)
                dve_var(n1, t, stat)
                dve_rstd(n1, t, stat)
            dve_store(n1, "h1T", hT[:, :, (NT - 1) * P:NT * P], NT - 1, 8)

            for s in range(NT + 4):
                t = s
                if t < NT:
                    for b in range(2):
                        src = full(dve, ("s", t, b))
                        V.tensor_reduce(out=negmax[:, t % 2, 2 * b:2 * b + 2],
                                        in_=src[:].rearrange("p (h m) -> p h m", m=M), axis=AX.X, op=ALU.max,
                                        negate=True).then_inc(negmax_ready, 1)
                t = s - 1
                if 0 <= t < NT:
                    for b in range(2):
                        src = full(dve, ("pT", t, b))
                        if t >= 2 and b == 0:
                            full(dve, ("o", t - 2, 1))
                        V.tensor_copy(pT[t % 2][:, 4 * b:4 * b + 4, :], src[:].rearrange("p (i n) -> p i n", n=P))\
                            .then_inc(pT_ready, 1)
                        dve.wait_ge(pT_ready, 2 * t + b + 1)
                        V.sem_inc(bank_free[use_of[("pT", t, b)][0]], 1)
                t = s
                if t < NT:
                    dve.wait_ge(exp_done, NH * (t + 1))
                    link(V.reciprocal(expsum[:, t % 2], expsum[:, t % 2]))
                    tt(probs[t % 2][:], probs[t % 2][:], expsum[:, t % 2].unsqueeze(2).to_broadcast([P, NH, M]),
                       ALU.mult).then_inc(probs_ready, 1)
                t = s - 2
                if 0 <= t < NT:
                    for half in range(2):
                        src = full(dve, ("h2", t, half))
                        part = h[:, t, half * BANK:(half + 1) * BANK]
                        tt(part, part, src[:], ALU.add).then_inc(h2_ready, 1)
                        dve.wait_ge(h2_ready, 2 * t + half + 1)
                        V.sem_inc(bank_free[use_of[("h2", t, half)][0]], 1)
                    dve_var(nf, t, stat)
                    dve_rstd(nf, t, stat)
                t = s - 3
                if 0 <= t < NT:
                    if t >= 2:
                        full(dve, ("router", t - 2))
                    dve_store(nf, "h2T", fT[t % 2], t, 24)

            dve.wait_ge(logit_ready, NT)
            dve.wait_ge(route_consts, 5)
            dve.wait_ge(router_in, 64)

            def wide(a, n):
                return a.unsqueeze(2).to_broadcast([P, NT, n])

            def numbers(n):
                return iota_n[:, 0:n].unsqueeze(1).to_broadcast([P, NT, n])

            link(tt(lg[:], logits[:], router_b[:].unsqueeze(1).to_broadcast([P, NT, NR]), ALU.add))

            def first_of_max(src, n, top, which, onehot, tmp):
                link(V.tensor_reduce(out=top, in_=src, axis=AX.X, op=ALU.max))
                link(tt(tmp, src, wide(top, n), ALU.is_ge))
                link(ts(tmp, tmp, -128.0, 128.0, ALU.mult, ALU.add))
                link(tt(tmp, tmp, numbers(n), ALU.add))
                link(V.tensor_reduce(out=which, in_=tmp, axis=AX.X, op=ALU.min))
                link(tt(onehot, numbers(n), wide(which, n), ALU.is_equal))

            first_of_max(lg[:, :, 0:NG], NG, col[:, 0], col[:, 1], gsel[:, 1], gsel[:, 0])
            tt(gsel[:, 0], lg[:, :, 0:NG], wide(col[:, 0], NG), ALU.subtract).then_inc(gexp_in, 1)
            link(ts(etmp[:, :, 0:NG], gsel[:, 1], -1.0, 1e30, ALU.add, ALU.mult))
            link(tt(em[:].rearrange("p t (g e) -> p t g e", e=EPG),
                    lg[:, :, NG:NR].rearrange("p t (g e) -> p t g e", e=EPG),
                    etmp[:, :, 0:NG].unsqueeze(3).to_broadcast([P, NT, NG, EPG]), ALU.add))
            first_of_max(em[:], NE, col[:, 2], col[:, 3], pick[:, 0], etmp[:])
            link(stt(em[:], pick[:, 0], -3e30, em[:], ALU.mult, ALU.add))
            first_of_max(em[:], NE, col[:, 4], col[:, 5], pick[:, 1], etmp[:])
            tt(col[:, 6], col[:, 4], col[:, 2], ALU.subtract).then_inc(pexp_in, 1)
            tt(both[:], pick[:, 0], pick[:, 1], ALU.add).then_inc(both_ready, 1)
            dve.wait_ge(gexp_out, 1)
            link(V.tensor_reduce(out=col[:, 7], in_=gsel[:, 0], axis=AX.X, op=ALU.add))
            link(V.reciprocal(col[:, 7], col[:, 7]))
            dve.wait_ge(pexp_out, 1)
            link(ts(col[:, 8], col[:, 6], 1.0, None, ALU.add))
            link(V.reciprocal(col[:, 8], col[:, 8]))
            link(tt(gates[:, :, 0], col[:, 7], col[:, 8], ALU.mult))
            link(tt(gates[:, :, 1], gates[:, :, 0], col[:, 6], ALU.mult))
            full(dve, "total")
            total = bank[1][:, 0:NT * NE].rearrange("p (t e) -> p t e", e=NE)
            link(V.memset(offs[:, 0, :], 0.0))
            for t in range(NT):
                link(tt(offs[:, t + 1], offs[:, t], total[:, t], ALU.add))
            V.sem_inc(bank_free[1], 1)
            full(dve, "rank")
            link(tt(rank[:], bank[0][:, 0:NT * NE].rearrange("p (t e) -> p t e", e=NE), offs[:, 0:NT], ALU.add))
            V.sem_inc(bank_free[0], 1)
            further, upto_e, shift_e, first_e = ev[:, 0], ev[:, 1], ev[:, 2], ev[:, 3]
            link(tt(over[:], offs[:, NT].unsqueeze(2).to_broadcast([P, NE, 7]),
                    limits[:].unsqueeze(1).to_broadcast([P, NE, 7]), ALU.is_gt))
            link(V.tensor_reduce(out=further, in_=over[:], axis=AX.X, op=ALU.add))
            link(V.tensor_tensor_scan(upto_e, ones[:, 0:NE], further, 0.0, ALU.mult, ALU.add))
            link(tt(shift_e, upto_e, further, ALU.subtract))
            link(tt(shift_e, shift_e, iota_n[:, 0:NE], ALU.subtract))
            link(ts(shift_e, shift_e, float(NE - 1), float(P), ALU.add, ALU.mult))
            link(ts(first_e, iota_n[:, 0:NE], float(P), None, ALU.mult))
            link(ts(etmp[:], rank[:], float(P), None, ALU.is_ge))
            link(tt(etmp[:], etmp[:], shift_e.unsqueeze(1).to_broadcast([P, NT, NE]), ALU.mult))
            link(tt(rank[:], rank[:], etmp[:], ALU.add))
            link(tt(rank[:], rank[:], first_e.unsqueeze(1).to_broadcast([P, NT, NE]), ALU.add))
            for k in range(2):
                link(tt(etmp[:], rank[:], pick[:, k], ALU.mult))
                link(V.tensor_reduce(out=posf[:, 0, k], in_=etmp[:], axis=AX.X, op=ALU.add))
            link(V.tensor_copy(posi[:, 0], posf[:, 0]))
            link(ts(posi[:, 1], posi[:, 0], 7, None, ALU.logical_shift_right))
            link(ts(posi[:, 0], posi[:, 0], P - 1, None, ALU.bitwise_and))
            link(V.tensor_copy(posf[:], posi[:]))
            def spread(a, n):
                return a.rearrange("p k t -> p (k t)").unsqueeze(2).to_broadcast([P, 2 * NT, n])

            def count(n):
                return iota_n[:, 0:n].unsqueeze(1).to_broadcast([P, 2 * NT, n])
            tt(row_of[:], count(P), spread(posf[:, 0], P), ALU.is_equal)
            link(tt(block_of[:], count(NB), spread(posf[:, 1], NB), ALU.is_equal))
            tt(block_of[:], block_of[:], spread(assign_no[:], NB), ALU.mult).then_inc(sel_ready, 1)
            dve.wait_ge(sel_used, 1)
            slots = bank[2][:, 0:NB]
            link(ts(slotv[:, 0], slots, 0.0, float(NO_ROW), ALU.is_equal, ALU.mult))
            link(stt(slotv[:, 1], slots, -1.0, slotv[:, 0], ALU.add, ALU.add))
            V.sem_inc(bank_free[2], 1)
            link(V.tensor_copy(rows_of_block[:, 1], slotv[:, 1]))
            link(ts(rows_of_block[:, 0], rows_of_block[:, 1], 1, None, ALU.logical_shift_right))
            link(tt(ovcmp[:], iota_n[:, 0:MAXOV].unsqueeze(2).to_broadcast([P, MAXOV, NE]),
                    upto_e.unsqueeze(1).to_broadcast([P, MAXOV, NE]), ALU.is_ge))
            link(V.tensor_reduce(out=ovf[:, 0:MAXOV], in_=ovcmp[:], axis=AX.X, op=ALU.add))
            link(ts(ovf[:, 0:MAXOV], ovf[:, 0:MAXOV], float(NE - 1), None, ALU.min))
            link(V.tensor_copy(ovf[:, MAXOV:MAXOV + 1], ev[:, 1, NE - 1:NE]))
            link(V.tensor_copy(meta[:], ovf[:]))

            def copy_rows(which, dst, block, ready):
                V.tensor_copy(dst[:], rows_of_block[:, which, bass.ds(block, 1)]).then_inc(ready, 1)

            def store_turned(b):
                for half in range(2):
                    w = par[:, 48 + 4 * half:52 + 4 * half].unsqueeze(2).to_broadcast([P, 4, P])
                    last = tt(xgT[b][:, 4 * half:4 * half + 4], bank[half][:].rearrange("p (c n) -> p c n", n=P), w,
                              ALU.mult)
                last.then_inc(xgT_ready, 1)

            def gate_up(b, i):
                dve.wait_ge(gate_ready, i + 1)
                dve.wait_ge(up3_done, i + 1)
                tt(hid[b][:], gate_act[b][:], bank[3][:], ALU.mult).then_inc(hid_ready, 1)

            def pair(j, final):
                for b in range(2):
                    i = 2 * j + b
                    gate_up(b, i)
                    if not (final and b == 1):
                        dve.wait_ge(xg_turned, i + 2)
                        store_turned(1 - b)
                    wait_for(dve, y_sent[b], 16 * j)
                    copy_rows(1, sidx[b], i, sidx_ready)
                    if not final:
                        dve.wait_ge(xg_in[b], 16 * j + 16)
                        copy_rows(0, gidx[b], i + 2, gidx_ready)

            copy_rows(0, gidx[0], 0, gidx_ready)
            copy_rows(0, gidx[1], 1, gidx_ready)
            dve.wait_ge(xg_turned, 1)
            store_turned(0)
            pair(0, False)
            with dve.Fori(1, NE // 2 - 1) as j:
                pair(j, False)
            pair(NE // 2 - 1, True)
            count = dve.value_load(meta[0:1, MAXOV:MAXOV + 1], min_val=0, max_val=MAXOV)
            with dve.Fori(0, MAXOV // 2) as o:
                with dve.If(2 * o < count):
                    for b in range(2):
                        dve.wait_ge(xg_in[b], 16 * (NE // 2) + 16 * o)
                        copy_rows(0, gidx[b], 2 * o + (NE + b), gidx_ready)
                    dve.wait_ge(xg_turned, NE + 1 + 2 * o)
                    store_turned(0)
                    pair(NE // 2 + o, True)

            dve.wait_ge(final_w_in, 16)

            def combine(t):
                dve.wait_ge(y_in[t % NY], 16 * (t // NY + 1))
                link(stt(h[:, t, :], ytile[t % NY][:, 0], gates[:, t, 0:1], h[:, t, :], ALU.mult, ALU.add))
                stt(h[:, t, :], ytile[t % NY][:, 1], gates[:, t, 1:2], h[:, t, :], ALU.mult, ALU.add).then_inc(comb, 1)
            combine(0)
            for t in range(NT):
                if t + 1 < NT:
                    combine(t + 1)
                dve_var(n2, t, stat)
                dve_rstd(n2, t, stat)
                dve.wait_ge(n2.rstd, t + 1)
                dve.wait_ge(comb, t + 1)
                if t >= 2:
                    dve.wait_ge(out_stored[t % 2], 16 * (t // 2))
                stt(otile[t % 2][:], h[:, t, :], stat[:, 2, t:t + 1], fin_w[:], ALU.mult, ALU.mult)\
                    .then_inc(out_ready, 1)


NAMES = ["x", "mem", "norm_mix_w", "w_in", "conv_w", "conv_b", "conv_ln_w", "conv_ln_b",
         "ssm_A_re", "ssm_A_im", "ssm_log_dt", "ssm_B_re", "ssm_B_im", "ssm_C_re", "ssm_C_im",
         "ssm_D", "ssm_glu_w", "w_out", "norm_x_w", "norm_mem_w", "xq_w", "xk_w", "xv_w", "xo_w",
         "norm_ffn_w", "router_group_w", "router_group_b", "router_expert_w", "router_expert_b",
         "moe_w1", "moe_w3", "moe_w2", "final_norm_w"]


def build(nc, shapes):
    args = [nc.dram_tensor(n, shapes[n], F32, kind="ExternalInput").ap() for n in NAMES]
    out = nc.dram_tensor("out", shapes["x"], F32, kind="ExternalOutput").ap()
    hymba_layer(nc, *args, out)


def kernel(**inputs):
    import concourse.bacc as bacc
    from concourse.bass_utils import run_bass_kernel_spmd

    arrays = {n: np.ascontiguousarray(inputs[n]) for n in NAMES}
    nc = bacc.Bacc("TRN2", target_bir_lowering=False, num_devices=1)
    build(nc, {n: a.shape for n, a in arrays.items()})
    result = run_bass_kernel_spmd(nc, [arrays], core_ids=[0])
    return result.results[0]["out"]
```

```python
from contextlib import ExitStack

import numpy as np

import concourse.bass as bass
from concourse import mybir

F32 = mybir.dt.float32
F32R = mybir.dt.float32r
I32 = mybir.dt.int32
ALU = mybir.AluOpType
ACT = mybir.ActivationFunctionType
AX = mybir.AxisListType

P = 128
KB = 1024
BANK = 512
NO_ROW = 1 << 20
ROUND = 12582912.0
LOG2E = 1.4426950408889634
LN2_HI, LN2_LO = 0.693359375, -2.12194440e-4
TWO_PI = 6.283185307179586
TWO_PI_A = 6.28125
TWO_PI_B = round((TWO_PI - TWO_PI_A) * 2.0**21) / 2.0**21
TWO_PI_C = TWO_PI - TWO_PI_A - TWO_PI_B
PI_LOW = 3.1415925


def hymba_layer(nc, x, mem, norm_mix_w, w_in, conv_w, conv_b, conv_ln_w, conv_ln_b,
                A_re, A_im, log_dt, B_re, B_im, C_re, C_im, ssm_D, glu_w, w_out,
                norm_x_w, norm_mem_w, xq_w, xk_w, xv_w, xo_w, norm_ffn_w,
                router_group_w, router_group_b, router_expert_w, router_expert_b,
                moe_w1, moe_w3, moe_w2, final_norm_w, out, upto=99):
    _, S, D = x.shape
    M = mem.shape[1]
    TAPS, DC = conv_w.shape[1:]
    G, NS, CH = B_re.shape[1:]
    NG = router_group_w.shape[2]
    NE = router_expert_w.shape[2]
    EPG = NE // NG
    F = moe_w1.shape[3]
    EPS = 1e-6
    NT = S // P
    KD = D // P
    KC = DC // P
    KF = F // P
    MT = M // P
    NH = 4
    HD = D // NH
    HK = HD // P
    T = 8
    NC = S // T
    Q4 = KC
    GQ = P // CH
    PQ = GQ // 2
    NP = G // 2
    NR = NG + NE
    MAXOV = 2 * S // P
    NB = NE + MAXOV
    assert CH * T == P and 2 * NS == P and NC == P and S == 2 * BANK and D == 2 * BANK

    u_bounce = nc.dram_tensor("u_bounce", (Q4, GQ, CH, T, NC), F32, kind="Internal").ap()
    y_bounce = nc.dram_tensor("y_bounce", (Q4, GQ, CH, T, NC), F32, kind="Internal").ap()
    xn_rows = nc.dram_tensor("xn_rows", (S, D), F32, kind="Internal").ap()
    y_rows = nc.dram_tensor("y_rows", (2 * S, D), F32, kind="Internal").ap()

    base = (nc.sbuf_base + 63) // 64 * 64

    def sb(name, kb, shape, dt=F32):
        return nc.alloc_sbuf_tensor_at(name, shape, dt, offset=base + int(kb * KB))

    slab = [sb(f"slab{i}", 16 * i, [P, KD, BANK]) for i in range(3)]
    h = sb("h", 48, [P, NT, D])
    uc = [sb(f"uc{i}", 48 + 4 * i, [P, GQ, NC]) for i in range(2)]
    rotated = sb("rotated", 56, [P, 2, PQ, NC])
    scanned = sb("scanned", 60, [P, 2, PQ, NC])
    rot_tmp = sb("rot_tmp", 64, [P, 2, PQ, NC])
    y_chunks = sb("y_chunks", 68, [P, GQ, NC])
    y_feat = sb("y_feat", 72, [P, T, NC])
    shifts = sb("shifts", 76, [P, T, P])
    mem_rows = sb("mem_rows", 68, [P, MT, D])
    xT = sb("xT", 80, [P, KD, S])
    kT = sb("kT", 80, [P, KD, M])
    vm = sb("vm", 88, [P, MT, D])
    memT = sb("memT", 104, [P, KD, M])
    yT = sb("yT", 96, [P, KD, S])
    conv_acc = yT[:, KC:KD, :]
    qT = sb("qT", 96, [P, KD, S])
    c_raw = sb("c_raw", 112, [CH, 2, G * NS])
    PAD = TAPS - 1
    conv_in = sb("conv_in", 128, [P, KC, S + PAD])
    squares = sb("squares", 128, [P, 2, KC, BANK])
    u_perm = sb("u_perm", 144.5, [P, Q4, T, NC])
    b_raw = sb("b_raw", 144.5, [P, 2, NP, CH])
    rows_raw = sb("rows_raw", 146.5, [P, P])
    taps_raw = sb("taps_raw", 147, [P, P])
    a_raw = sb("a_raw", 147.5, [NP, 3, P])
    dt_raw = sb("dt_raw", 149, [NP, 2])
    xs0 = [sb(f"xs0_{i}", 150 + 4 * i, [P, D]) for i in range(2)]
    hT = sb("hT", 128, [P, KD, S])
    oT = sb("oT", 128, [P, KD, S])
    lift = [sb("lift0", 160.5, [P, 2, PQ, P]), sb("lift1", 32, [P, 2, PQ, P])]
    toep = [sb("toep0", 164.5, [P, GQ, P]), sb("toep1", 36, [P, GQ, P])]
    readout = [sb("readout0", 168.5, [P, 2, PQ, P]), sb("readout1", 40, [P, 2, PQ, P])]
    phase = [sb("phase0", 172.5, [P, 2, PQ, NC]), sb("phase1", 44, [P, 2, PQ, NC])]
    bpow = sb("bpow", 176.5, [P, 2, PQ, P])
    kern = sb("kern", 180.5, [P, GQ, CH])
    glu_sig = sb("glu_sig", 181, [P, BANK])
    conv_a = sb("conv_a", 183, [P, BANK])
    conv_sg = sb("conv_sg", 185, [P, BANK])
    states = sb("states", 187, [P, 2, PQ, NC + 1])
    pool_tmp = sb("pool_tmp", 191.25, [P, 4, PQ * CH * 4])
    ln_tmp = sb("ln_tmp", 183, [P, BANK])
    at = [195.25]

    def small(name, shape, dt=F32):
        n = int(np.prod(shape[1:])) * 4
        t = sb(name, at[0], shape, dt)
        at[0] += (n + 31) // 32 * 32 / KB
        assert base + at[0] * KB <= nc.sbuf_usable_end, (name, at[0])
        return t

    ident = small("ident", [P, P])
    means = small("means", [P, P])
    par = small("par", [P, 5 * KD + 4 * KC])
    taps = small("taps", [P, TAPS * KC])
    ct = small("ct", [P, 2, NP, CH])
    bbar = small("bbar", [P, 2, NP, CH])
    pw = small("pw", [P, 2, 3, NP])
    ph = small("ph", [P, 2, 7, NP])
    rho = small("rho", [P, NP])
    t16 = small("t16", [P, 12, NP])
    stat = small("stat", [P, 3, NT])
    stat_m = small("stat_m", [P, 3, MT])
    pool_mark = small("pool_mark", [P, 1])
    xs = [sb(f"xs{i}", 160.5 + 4 * i, [P, D]) for i in range(2)]
    probs = [sb(f"probs{i}", 168.5 + 4 * i, [P, NH, M]) for i in range(2)]
    pT = [sb(f"pT{i}", 176.5 + 4 * i, [P, NH * MT, P]) for i in range(2)]
    fT = [sb(f"fT{i}", 184.5 + 4 * i, [P, KD, P]) for i in range(2)]
    glu_lhs = sb("glu_lhs", 203.25, [P, Q4, 2, P])
    assert base + 207.25 * KB <= nc.sbuf_usable_end and at[0] <= 203.25, at[0]

    junk_x = sb("junk_x", 128, [P, D])
    junk_m = sb("junk_m", 56, [P, D])
    junk = sb("junk", 192.75, [P, D], mybir.dt.bfloat16)
    ln_var = sb("ln_var", 183, [P, 2, BANK])
    negmax = sb("negmax", 194.75, [P, 2, NH])
    expsum = sb("expsum", 194.8125, [P, 2, NH])
    logits = sb("logits", 203.25, [P, NT, NR])
    router_w = sb("router_w", 204.5, [P, KD, NR])
    router_b = sb("router_b", 205.75, [P, NR])
    at[0] = 160.5

    def late(name, shape, dt=F32):
        n = int(np.prod(shape[1:])) * 4
        t = sb(name, at[0], shape, dt)
        at[0] += (n + 31) // 32 * 32 / KB
        assert at[0] <= 195.25, name
        return t

    upper = late("upper", [P, P])
    ones = late("ones", [P, P])
    iota_n = late("iota_n", [P, P])
    assign_no = late("assign_no", [P, 2, NT])
    limits = late("limits", [P, 7])
    lg = late("lg", [P, NT, NR])
    col = late("col", [P, 12, NT])
    gsel = late("gsel", [P, 2, NT, NG])
    em = late("em", [P, NT, NE])
    etmp = late("etmp", [P, NT, NE])
    pick = late("pick", [P, 2, NT, NE])
    both = late("both", [P, NT, NE])
    offs = late("offs", [P, NT + 1, NE])
    rank = late("rank", [P, NT, NE])
    over = late("over", [P, NE, 7])
    ev = late("ev", [P, 5, NE])
    posi = late("posi", [P, 2, 2, NT], I32)
    posf = late("posf", [P, 2, 2, NT])
    row_of = sb("row_of", 144, [P, 2 * NT, P])
    block_of = sb("block_of", 152, [P, 2 * NT, NB])
    slotv = late("slotv", [P, 2, NB])
    ovcmp = late("ovcmp", [P, MAXOV, NE])
    ovf = late("ovf", [P, MAXOV + 1])
    assert at[0] <= 192
    at[0] = 192
    gates = late("gates", [P, NT, 2])
    rows_of_block = late("rows_of_block", [P, 2, NB], I32)
    meta = late("meta", [P, MAXOV + 1], I32)
    gidx = [late(f"gidx{i}", [P, 1], I32) for i in range(2)]
    sidx = [late(f"sidx{i}", [P, 1], I32) for i in range(2)]
    fin_w = sb("fin_w", 203.25, [P, D])
    NRAW, NSPLIT = 6, 4
    HALF = KD // 2
    raw = [sb(f"raw{i}", 8 * i, [P, HALF, F]) for i in range(NRAW)]
    w_hi = [sb(f"w_hi{i}", 80 + 16 * i, [P, HALF, F], F32R) for i in range(NSPLIT)]
    w_lo = [sb(f"w_lo{i}", 88 + 16 * i, [P, HALF, F], F32R) for i in range(NSPLIT)]
    xg = [sb(f"xg{i}", 144 + 4 * i, [P, D]) for i in range(2)]
    xw = sb("xw", 152, [P, KD, P])
    x_hi = [sb(f"x_hi{i}", 156 + 8 * i, [P, KD, P], F32R) for i in range(2)]
    x_lo = [sb(f"x_lo{i}", 160 + 8 * i, [P, KD, P], F32R) for i in range(2)]
    gate_act = sb("gate_act", 172, [P, F])
    hid = sb("hid", 174, [P, F])
    hid_hi = sb("hid_hi", 176, [P, KF, P], F32R)
    hid_lo = sb("hid_lo", 178, [P, KF, P], F32R)
    yb = [sb(f"yb{i}", 180 + 4 * i, [P, D]) for i in range(2)]
    NY = 4
    ytile = [sb(f"ytile{i}", 80 + 8 * i, [P, 2, D]) for i in range(NY)]
    otile = [sb(f"otile{i}", 112 + 4 * i, [P, D]) for i in range(2)]
    junk_f = sb("junk_f", 120, [P, D])

    bank = [nc.alloc_psum_tensor(f"bank{i}", [P, BANK], F32) for i in range(8)]

    def sem(name):
        return nc.alloc_semaphore(name)

    bank_full = [sem(f"bank_full{i}") for i in range(8)]
    bank_free = [sem(f"bank_free{i}") for i in range(8)]
    bank_uses = [0] * 8
    use_of = {}

    consts_ready = sem("consts_ready")
    pool_step = sem("pool_step")
    dve_step = sem("dve_step")
    act_step = sem("act_step")
    params_in = sem("params_in")
    craw_in = sem("craw_in")
    par_in = sem("par_in")
    braw_in = sem("braw_in")
    glu_in = sem("glu_in")
    x_in = [sem(f"x_in{t}") for t in range(NT)]
    mem_in = sem("mem_in")
    slab_in = [sem(f"slab_in{i}") for i in range(3)]
    setup_ready = sem("setup_ready")
    trig_in = sem("trig_in")
    trig_out = sem("trig_out")
    conv_a_ready = sem("conv_a_ready")
    conv_sg_ready = sem("conv_sg_ready")
    v_ready = sem("v_ready")
    conv_done = sem("conv_done")
    u_ready = sem("u_ready")
    ub_out = sem("ub_out")
    uc_in = [sem("uc_in0"), sem("uc_in1")]
    memT_ready = sem("memT_ready")
    bpow_ready = sem("bpow_ready")
    readout_ready = sem("readout_ready")
    phase_ready = sem("phase_ready")
    lift_ready = sem("lift_ready")
    kern_ready = sem("kern_ready")
    toep_ready = sem("toep_ready")
    shifts_ready = sem("shifts_ready")
    states_ready = sem("states_ready")
    ychunk_ready = sem("ychunk_ready")
    yb_out = sem("yb_out")
    yf_in = sem("yf_in")
    dterm_done = sem("dterm_done")
    gelu_done = sem("gelu_done")
    glu_sig_ready = sem("glu_sig_ready")
    yssm_ready = sem("yssm_ready")
    kv_ready = sem("kv_ready")
    centered = sem("centered")
    squared = sem("squared")
    ln_v = sem("ln_v")
    ln_root = sem("ln_root")
    ln_scaled = sem("ln_scaled")
    yconv_ready = sem("yconv_ready")
    h1_ready = sem("h1_ready")
    q_ready = sem("q_ready")
    negmax_ready = sem("negmax_ready")
    exp_done = sem("exp_done")
    probs_ready = sem("probs_ready")
    pT_ready = sem("pT_ready")
    oT_ready = sem("oT_ready")
    h2_ready = sem("h2_ready")
    router_in = sem("router_in")
    xn_out = [sem("xn_out0"), sem("xn_out1")]
    logit_ready = sem("logit_ready")
    route_consts = sem("route_consts")
    gexp_in = sem("gexp_in")
    gexp_out = sem("gexp_out")
    pexp_in = sem("pexp_in")
    pexp_out = sem("pexp_out")
    both_ready = sem("both_ready")
    sel_ready = sem("sel_ready")
    sel_used = sem("sel_used")

    class Norm:

        def __init__(self, name, turned=True):
            self.squares, self.var, self.root, self.rstd = (
                sem(f"{name}_{x}") for x in ("squares", "var", "root", "rstd"))
            if turned:
                self.scaled, self.stored = sem(f"{name}_scaled"), sem(f"{name}_stored")

    nx, nm, n1, nf = (Norm(n) for n in ("nx", "nm", "n1", "nf"))
    n2 = Norm("n2", turned=False)
    raw_in = [sem(f"raw_in{i}") for i in range(6)]
    hi_ready = sem("hi_ready")
    lo_ready = sem("lo_ready")
    piece_used = sem("piece_used")
    xg_in = [sem("xg_in0"), sem("xg_in1")]
    y_sent = [sem("y_sent0"), sem("y_sent1")]
    gidx_ready = sem("gidx_ready")
    sidx_ready = sem("sidx_ready")
    xg_turned = sem("xg_turned")
    xw_ready = sem("xw_ready")
    x_hi_ready = sem("x_hi_ready")
    x_lo_ready = sem("x_lo_ready")
    gate_ready = sem("gate_ready")
    hid_ready = sem("hid_ready")
    hid_turned = sem("hid_turned")
    hid_hi_ready = sem("hid_hi_ready")
    hid_lo_ready = sem("hid_lo_ready")
    yb_ready = sem("yb_ready")
    final_w_in = sem("final_w_in")
    over_done = sem("over_done")
    xg_clear = sem("xg_clear")
    rows_moved = sem("rows_moved")
    y_in = [sem(f"y_in{i}") for i in range(NY)]
    comb = sem("comb")
    out_ready = sem("out_ready")
    out_stored = [sem("out_stored0"), sem("out_stored1")]

    def full(eng, key):
        b, n = use_of[key]
        eng.wait_ge(bank_full[b], n)
        return bank[b]

    def wait_for(eng, s, n):
        if not (isinstance(n, int) and n <= 0):
            eng.wait_ge(s, n)

    def linker(eng, step):
        count = [0]

        def link(ins):
            count[0] += 1
            ins.then_inc(step, 1)
            eng.wait_ge(step, count[0])
        return link

    def col_major(w, c0, n):
        return w[:, c0:c0 + n].rearrange("(c p) n -> p c n", p=P)

    slabs = [(w_in[0], 0, 0, None), (w_in[0], BANK, 1, None), (w_in[0], 2 * BANK, 2, None),
             (xk_w[0], 0, 0, ("g", KC - 1, 1)), (xk_w[0], BANK, 1, ("g", KC - 1, 1)),
             (xv_w[0], 0, 0, ("k", 3)), (xv_w[0], BANK, 1, ("k", 7)),
             (w_out[0], 0, 0, ("v", 0, 1)), (w_out[0], BANK, 1, ("v", 1, 1)),
             (xq_w[0], 0, 2, ("y", Q4 - 1, 1)), (xq_w[0], BANK, 0, ("h1", NT - 1, 1)),
             (xo_w[0], 0, 1, ("h1", NT - 1, 1)), (xo_w[0], BANK, 2, ("q", 3, 1))]

    def slab_loaded(eng, n):
        place = slabs[n][2]
        eng.wait_ge(slab_in[place], 16 * sum(w[2] == place for w in slabs[:n + 1]))

    NQ = Q4
    PAIRS = range(PQ)

    with nc.Block() as block:

        @block.tensor
        def _(pe):
            def take(*banks):
                for b in banks:
                    if bank_uses[b]:
                        pe.wait_ge(bank_free[b], bank_uses[b])

            def give(b, ins, key):
                bank_uses[b] += 1
                use_of[key] = (b, bank_uses[b])
                ins.then_inc(bank_full[b], 1)

            def turn(out, src, n=P):
                return nc.tensor.transpose(out, src, ident[0:n, 0:n])

            pe.wait_ge(consts_ready, 1)
            pe.wait_ge(params_in, 16 * 12)
            give(0, turn(bank[0][:, 0:48], rows_raw[0:48, :], 48), "par")
            give(1, turn(bank[1][:, 0:TAPS * KC], taps_raw[0:TAPS * KC, :], TAPS * KC), "taps")
            def turn_rows(norm, src, t, banks, key):
                pe.wait_ge(norm.scaled, t + 1)
                take(*banks)
                for c in range(KD):
                    last = turn(bank[banks[c // 4]][:, (c % 4) * P:(c % 4 + 1) * P], src[:, c * P:(c + 1) * P])
                    if c == 3:
                        give(banks[0], last, (key, t, 0))
                bank_uses[banks[1]] += 1
                use_of[(key, t, 1)] = (banks[1], bank_uses[banks[1]])
                last.then_inc(bank_full[banks[1]], 1)

            for t in range(NT):
                turn_rows(nx, xs0[t % 2], t, (4, 5) if t % 2 else (6, 7), "x")

            pe.wait_ge(consts_ready, 3)
            for i in range(3):
                last = turn(bank[2][:, i * NP:(i + 1) * NP], a_raw[:, i, :], NP)
            give(2, last, "a_raw")
            pe.wait_ge(craw_in, 32)
            for ri in range(2):
                for p in range(NP):
                    o = (ri * NP + p) * CH
                    last = turn(bank[3][:, o:o + CH], c_raw[:, ri, p * P:(p + 1) * P], CH)
            give(3, last, "c_raw")

            pe.wait_ge(nx.stored, NT)
            for n in range(2):
                slab_loaded(pe, n)
            for i in range(KC):
                for half in range(2):
                    for w, b in ((0, half), (1, 2 + half)):
                        take(b)
                        for k in range(KD):
                            last = nc.tensor.matmul(bank[b][:], slab[w][:, k, i * P:(i + 1) * P],
                                                    xT[:, k, half * BANK:(half + 1) * BANK],
                                                    start=(k == 0), stop=(k == KD - 1))
                        give(b, last, ("ag"[w], i, half))
            slab_loaded(pe, 2)
            for i in range(KC):
                for half in range(2):
                    b = 4 + half
                    take(b)
                    for k in range(KD):
                        last = nc.tensor.matmul(bank[b][:], slab[2][:, k, i * P:(i + 1) * P],
                                                xT[:, k, half * BANK:(half + 1) * BANK],
                                                start=(k == 0), stop=(k == KD - 1))
                    give(b, last, ("u", i, half))
            for t in range(MT):
                turn_rows(nm, mem_rows[:, t, :], t, (6, 7), "m")

            def setup(q):
                pe.wait_ge(bpow_ready, q + 1)
                for ri in range(2):
                    take(ri)
                    for p in PAIRS:
                        last = turn(bank[ri][:, p * P:(p + 1) * P], bpow[:, ri, p, :])
                    give(ri, last, ("lift", q, ri))
                for g2 in range(2):
                    take(g2)
                    rows = slice(g2 * NS, (g2 + 1) * NS)
                    for p in PAIRS:
                        for ri in range(2):
                            last = nc.tensor.matmul(bank[g2][:, p * CH:(p + 1) * CH], bpow[rows, ri, p, :],
                                                    ct[rows, ri, q * PQ + p, :], start=(ri == 0), stop=(ri == 1))
                    give(g2, last, ("kern", q, g2))
                pe.wait_ge(kern_ready, 2 * q + 2)
                if q == 0:
                    pe.wait_ge(shifts_ready, 1)
                for jh in range(2):
                    take(jh)
                    for j in range(4):
                        last = nc.tensor.matmul(bank[jh][:, j * P:(j + 1) * P], shifts[:, 7 - 4 * jh - j, :],
                                                kern[:].rearrange("p g o -> p (g o)"), start=True, stop=True)
                    give(jh, last, ("toep", q, jh))

            def chunk_inputs(q):
                pe.wait_ge(uc_in[q % 2], 16 * (q // 2 + 1))
                pe.wait_ge(lift_ready, 2 * q + 2)
                for ri in range(2):
                    take(6 + ri)
                    for p in PAIRS:
                        for g2 in range(2):
                            last = nc.tensor.matmul(
                                bank[6 + ri][g2 * NS:(g2 + 1) * NS, p * NC:(p + 1) * NC],
                                lift[q % 2][:, ri, p, g2 * NS:(g2 + 1) * NS], uc[q % 2][:, 2 * p + g2, :],
                                start=True, stop=True)
                    give(6 + ri, last, ("S", q, ri))

            def chunk_outputs(q):
                pe.wait_ge(toep_ready, 2 * q + 2)
                pe.wait_ge(readout_ready, q + 1)
                pe.wait_ge(states_ready, q + 1)
                take(4, 5)
                for p in PAIRS:
                    for g2 in range(2):
                        nc.tensor.matmul(bank[4 + g2][:, p * NC:(p + 1) * NC], toep[q % 2][:, 2 * p + g2, :],
                                         uc[q % 2][:, 2 * p + g2, :], start=True, stop=False)
                    for ri in range(2):
                        for g2 in range(2):
                            rows = slice(g2 * NS, (g2 + 1) * NS)
                            last = nc.tensor.matmul(bank[4 + g2][:, p * NC:(p + 1) * NC],
                                                    readout[q % 2][rows, ri, p, :], states[rows, ri, p, 0:NC],
                                                    start=False, stop=(ri == 1))
                            if p == PQ - 1 and ri == 1 and g2 == 0:
                                give(4, last, ("y", q, 0))
                give(5, last, ("y", q, 1))

            def kv_piece(n):
                slab_loaded(pe, 3 + n)
                w = slab[slabs[3 + n][2]]
                if n == 0:
                    pe.wait_ge(memT_ready, MT * KD)
                if n < 2:
                    for m in range(4):
                        take(m)
                        for k in range(KD):
                            last = nc.tensor.matmul(bank[m][:, 0:M], w[:, k, m * P:(m + 1) * P], memT[:, k, :],
                                                    start=(k == 0), stop=(k == KD - 1))
                        give(m, last, ("k", 4 * n + m))
                else:
                    for mt in range(MT):
                        take(mt)
                        for k in range(KD):
                            last = nc.tensor.matmul(bank[mt][:], memT[:, k, mt * P:(mt + 1) * P], w[:, k, :],
                                                    start=(k == 0), stop=(k == KD - 1))
                        give(mt, last, ("v", n - 2, mt))

            def glu(q):
                pe.wait_ge(gelu_done, q + 1)
                if q == 0:
                    pe.wait_ge(glu_in, 16 * 2 * GQ)
                for jh in range(2):
                    for e in range(2):
                        take(2 + e)
                        last = nc.tensor.matmul(bank[2 + e][:], glu_lhs[:, q, e, :],
                                                y_feat[:, 4 * jh:4 * jh + 4, :].rearrange("p j c -> p (j c)"),
                                                start=True, stop=True)
                        give(2 + e, last, ("glu", q, jh, e))

            def channel_means(src, ready, key):
                for half in range(2):
                    pe.wait_ge(ready, half + 1 if ready is not conv_done else KC)
                    take(2 + half)
                    for k in range(KC):
                        last = nc.tensor.matmul(bank[2 + half][:], means[:], src(k, half),
                                                start=(k == 0), stop=(k == KC - 1))
                    give(2 + half, last, (key, half))

            setup(0)
            for q in range(NQ):
                chunk_inputs(q)
                kv_piece(q)
                if q > 0:
                    glu(q - 1)
                chunk_outputs(q)
                if q + 1 < NQ:
                    setup(q + 1)
                if q == 0:
                    channel_means(lambda k, half: conv_acc[:, k, half * BANK:(half + 1) * BANK], conv_done, "mean")
                if q == 1:
                    channel_means(lambda k, half: squares[:, half, k, :], squared, "lnvar")
            glu(NQ - 1)

            pe.wait_ge(yssm_ready, 2 * NQ)
            pe.wait_ge(yconv_ready, KC)
            slab_loaded(pe, 7)
            slab_loaded(pe, 8)
            for t in range(NT):
                for half in range(2):
                    b = 2 * (t % 2) + half
                    take(b)
                    for k in range(KD):
                        last = nc.tensor.matmul(bank[b][:], yT[:, (k + KC) % KD, t * P:(t + 1) * P],
                                                slab[half][:, k, :], start=(k == 0), stop=(k == KD - 1))
                    give(b, last, ("h1", t, half))
                if t > 0:
                    turn_rows(n1, xs[(t - 1) % 2], t - 1, (4, 5), "h1T")
            turn_rows(n1, xs[(NT - 1) % 2], NT - 1, (4, 5), "h1T")

            pe.wait_ge(n1.stored, NT)
            for m in range(KD):
                slab_loaded(pe, 9 + m // 4)
                w = slab[slabs[9 + m // 4][2]]
                for half in range(2):
                    b = 2 * (m % 2) + half
                    take(b)
                    for k in range(KD):
                        last = nc.tensor.matmul(bank[b][:], w[:, k, (m % 4) * P:(m % 4 + 1) * P],
                                                hT[:, k, half * BANK:(half + 1) * BANK],
                                                start=(k == 0), stop=(k == KD - 1))
                    give(b, last, ("q", m, half))

            pe.wait_ge(kv_ready, 12)
            pe.wait_ge(q_ready, 2 * KD)
            for s in range(NT + 4):
                if s < NT:
                    for b in range(2):
                        take(b)
                        for hd in (2 * b, 2 * b + 1):
                            for k in range(HK):
                                last = nc.tensor.matmul(bank[b][:, (hd % 2) * M:(hd % 2 + 1) * M],
                                                        qT[:, HK * hd + k, s * P:(s + 1) * P], kT[:, HK * hd + k, :],
                                                        start=(k == 0), stop=(k == HK - 1))
                        give(b, last, ("s", s, b))
                t = s - 1
                if 0 <= t < NT:
                    pe.wait_ge(probs_ready, t + 1)
                    for b in range(2):
                        take(4 + b)
                        for i in range(4):
                            hd, mt = 2 * b + i // 2, i % 2
                            last = turn(bank[4 + b][:, i * P:(i + 1) * P], probs[t % 2][:, hd, mt * P:(mt + 1) * P])
                        give(4 + b, last, ("pT", t, b))
                t = s - 2
                if 0 <= t < NT:
                    pe.wait_ge(oT_ready, 2 * t + 2)
                    for half in range(2):
                        slab_loaded(pe, 11 + half)
                        take(2 + half)
                        for k in range(KD):
                            last = nc.tensor.matmul(bank[2 + half][:], oT[:, k, t * P:(t + 1) * P],
                                                    slab[slabs[11 + half][2]][:, k, :],
                                                    start=(k == 0), stop=(k == KD - 1))
                        give(2 + half, last, ("h2", t, half))
                t = s - 1
                if 0 <= t < NT:
                    pe.wait_ge(pT_ready, 2 * t + 2)
                    for b in range(2):
                        take(6 + b)
                        for m in range(4 * b, 4 * b + 4):
                            for mt in range(MT):
                                last = nc.tensor.matmul(bank[6 + b][:, (m % 4) * P:(m % 4 + 1) * P],
                                                        vm[:, mt, m * P:(m + 1) * P],
                                                        pT[t % 2][:, (m // HK) * MT + mt, :],
                                                        start=(mt == 0), stop=(mt == MT - 1))
                        give(6 + b, last, ("o", t, b))
                t = s - 3
                if 0 <= t < NT:
                    turn_rows(nf, xs[t % 2], t, (4, 5), "h2T")
                t = s - 4
                if 0 <= t < NT:
                    pe.wait_ge(nf.stored, t + 1)
                    pe.wait_ge(router_in, 16 * 3)
                    take(6)
                    for k in range(KD):
                        last = nc.tensor.matmul(bank[6][:, 0:NR], fT[t % 2][:, k, :], router_w[:, k, :],
                                                start=(k == 0), stop=(k == KD - 1))
                    give(6, last, ("router", t))

            pe.wait_ge(both_ready, 1)
            pe.wait_ge(route_consts, 5)
            take(0, 1)
            mask = both[:].rearrange("p t e -> p (t e)")
            give(0, nc.tensor.matmul(bank[0][:, 0:NT * NE], upper[:], mask, start=True, stop=True), "rank")
            give(1, nc.tensor.matmul(bank[1][:, 0:NT * NE], ones[:], mask, start=True, stop=True), "total")
            take(2)
            pe.wait_ge(sel_ready, 1)
            for i in range(2 * NT):
                last = nc.tensor.matmul(bank[2][:, 0:NB], row_of[:, i, :], block_of[:, i, :],
                                        start=(i == 0), stop=(i == 2 * NT - 1))
            last.then_inc(sel_used, 1)
            bank_uses[2] += 1
            take(*range(8))

            def turn_tokens(b, n, i):
                pe.wait_ge(xg_in[b], 16 * n)
                wait_for(pe, xw_ready, i)
                for c in range(KD):
                    last = turn(bank[c // 4][:, (c % 4) * P:(c % 4 + 1) * P], xg[b][:, c:D:KD])
                last.then_inc(xg_turned, 1)

            def split_product(out, a_hi, a_lo, b_hi, b_lo, first, final):
                nc.tensor.matmul(out, a_hi, b_hi, start=first, stop=False)
                nc.tensor.matmul(out, a_hi, b_lo, start=False, stop=False)
                return nc.tensor.matmul(out, a_lo, b_hi, start=False, stop=final)

            def piece_ready(j, k):
                pe.wait_ge(hi_ready, 12 * j + k + 1)
                pe.wait_ge(lo_ready, 12 * j + k + 1)
                return w_hi[k % NSPLIT], w_lo[k % NSPLIT]

            def up(j, k, b, out, half):
                hi, lo = piece_ready(j, k)
                for c in range(HALF):
                    d = half * HALF + c
                    last = split_product(out, x_hi[b][:, d, :], x_lo[b][:, d, :], hi[:, c, :], lo[:, c, :],
                                         d == 0, d == KD - 1)
                last.then_inc(piece_used, 1)

            def turn_hidden(i):
                pe.wait_ge(hid_ready, i + 1)
                for f in range(KF):
                    last = turn(bank[4][:, f * P:(f + 1) * P], hid[:, f:F:KF])
                last.then_inc(hid_turned, 1)

            def down(j, k, i):
                pe.wait_ge(hid_hi_ready, i + 1)
                pe.wait_ge(hid_lo_ready, i + 1)
                wait_for(pe, yb_ready, i)
                for part in range(2):
                    hi, lo = (w[:].rearrange("p c n -> p (c n)").rearrange("p (f d) -> p f d", d=D)
                              for w in piece_ready(j, k + part))
                    for f in range(KF // 2):
                        g = part * (KF // 2) + f
                        for half in range(2):
                            cols = slice(half * BANK, (half + 1) * BANK)
                            last = split_product(bank[5 + half][:], hid_hi[:, g, :], hid_lo[:, g, :],
                                                 hi[:, f, cols], lo[:, f, cols], g == 0, g == KF - 1)
                    last.then_inc(piece_used, 1)

            def tokens_ready(i):
                pe.wait_ge(x_hi_ready, i + 1)
                pe.wait_ge(x_lo_ready, i + 1)
                wait_for(pe, gate_ready, i)

            def first_block(j):
                tokens_ready(2 * j)
                up(j, 0, 0, bank[2][:], 0)
                up(j, 1, 0, bank[2][:], 1)
                turn_tokens(1, j + 1, 2 * j + 1)
                wait_for(pe, hid_ready, 2 * j)
                up(j, 2, 0, bank[3][:], 0)
                up(j, 3, 0, bank[3][:], 1)

            def next_block(j, s, final=False):
                i, b, k = 2 * j + 1 + s, 1 - s, 4 + 6 * s
                tokens_ready(i)
                up(j, k, b, bank[2][:], 0)
                turn_hidden(i - 1)
                up(j, k + 1, b, bank[2][:], 1)
                down(j, k + 2, i - 1)
                if not final:
                    turn_tokens(s, j + 2, i + 1)
                up(j, k + 4, b, bank[3][:], 0)
                up(j, k + 5, b, bank[3][:], 1)

            def last_down(j):
                turn_hidden(2 * j + 1)
                down(j, 10, 2 * j + 1)

            turn_tokens(0, 1, 0)
            first_block(0)
            for s in range(2):
                next_block(0, s)
            with pe.Fori(1, NE // 2 - 1) as j:
                for s in range(2):
                    next_block(j, s)
            next_block(NE // 2 - 1, 0, final=True)
            last_down(NE // 2 - 1)

            further = pe.value_load(meta[0:1, MAXOV:MAXOV + 1], min_val=0, max_val=MAXOV)
            with pe.Fori(0, MAXOV // 2) as o:
                with pe.If(2 * o < further):
                    turn_tokens(0, NE // 2 + o + 1, NE + 2 * o)
                    first_block(NE // 2 + o)
                    next_block(NE // 2 + o, 0, final=True)
                    last_down(NE // 2 + o)

        @block.sync
        def _(sp):
            def load_slab(n):
                w, c0, place, after = slabs[n]
                if after:
                    full(sp, after)
                sp.dma_start(slab[place][:], col_major(w, c0, BANK)).then_inc(slab_in[place], 16)

            x_rows = x[0].rearrange("(t p) d -> t p d", p=P)
            for t in range(4):
                sp.dma_start(h[:, t, :], x_rows[t]).then_inc(x_in[t], 16)
            load_slab(0)
            for t in range(4, NT):
                sp.dma_start(h[:, t, :], x_rows[t]).then_inc(x_in[t], 16)
            load_slab(1)
            load_slab(2)
            sp.wait_ge(nx.scaled, 7)
            sp.dma_start(mem_rows[:], mem[0].rearrange("(t p) d -> p t d", p=P)).then_inc(mem_in, 16)
            load_slab(3)
            load_slab(4)
            for q in range(NQ):
                sp.wait_ge(u_ready, 2 * q + 2)
                sp.dma_start(u_bounce[q].rearrange("g h j c -> (g h) (j c)"),
                             u_perm[:, q].rearrange("p j c -> p (j c)")).then_inc(ub_out, 16)
                sp.wait_ge(ub_out, 16 * q + 16)
                if q < 2:
                    sp.dma_start(uc[q][:], u_bounce[q].rearrange("g h j c -> (h j) g c")).then_inc(uc_in[q], 16)
            load_slab(5)
            for q in range(NQ):
                sp.wait_ge(ychunk_ready, 2 * q + 2)
                sp.dma_start(y_bounce[q].rearrange("g h j c -> (h j) g c"), y_chunks[:]).then_inc(yb_out, 16)
                sp.wait_ge(yb_out, 16 * q + 16)
                if q > 0:
                    full(sp, ("glu", q - 1, 1, 1))
                if q == 0:
                    full(sp, ("m", 1, 1))
                sp.dma_start(y_feat[:].rearrange("p j c -> p (j c)"),
                             y_bounce[q].rearrange("g h j c -> (g h) (j c)")).then_inc(yf_in, 16)
                if q + 2 < NQ:
                    full(sp, ("y", q, 1))
                    sp.dma_start(uc[q % 2][:], u_bounce[q + 2].rearrange("g h j c -> (h j) g c"))\
                      .then_inc(uc_in[q % 2], 16)
                if q < 3:
                    load_slab(6 + q)
            load_slab(9)
            full(sp, ("glu", NQ - 1, 1, 1))
            for t in range(NT):
                sp.dma_start(h[:, t, :], x_rows[t]).then_inc(x_in[t], 16)
            for n in (10, 11, 12):
                load_slab(n)

            w1, w3, w2 = moe_w1[0], moe_w3[0], moe_w2[0]

            def load_half(j, k, weights, e, half):
                for part in (hi_ready, lo_ready):
                    wait_for(sp, part, 12 * j + k - NRAW + 1)
                n = HALF * F
                sp.dma_start(raw[k % NRAW][:].rearrange("p c f -> p (c f)"),
                             weights[bass.ds(e, 1)].rearrange("o (p c) f -> p (o c f)", p=P)
                             [:, half * n:(half + 1) * n]).then_inc(raw_in[k % NRAW], 16)

            def load_first(j, e):
                for k, (w, half) in enumerate(((w1, 0), (w1, 1), (w3, 0), (w3, 1))):
                    load_half(j, k, w, e, half)

            def load_next(j, s, e, before):
                for k, (w, n, half) in enumerate(((w1, e, 0), (w1, e, 1), (w2, before, 0), (w2, before, 1),
                                                  (w3, e, 0), (w3, e, 1))):
                    load_half(j, 4 + 6 * s + k, w, n, half)

            def load_last(j, e):
                for half in range(2):
                    load_half(j, 10 + half, w2, e, half)

            full(sp, ("q", 7, 1))
            for key in (("h2", NT - 1, 0), ("h2", NT - 1, 1)):
                full(sp, key)
            load_first(0, 0)
            for s in range(2):
                load_next(0, s, 1 + s, s)
            with sp.Fori(1, NE // 2 - 1) as j:
                for s in range(2):
                    load_next(j, s, 2 * j + 1 + s, 2 * j + s)
            load_next(NE // 2 - 1, 0, NE - 1, NE - 2)
            load_last(NE // 2 - 1, NE - 1)
            full(sp, "total")
            sp.wait_ge(gidx_ready, 1)
            further = sp.value_load(meta[0:1, MAXOV:MAXOV + 1], min_val=0, max_val=MAXOV)
            with sp.Fori(0, MAXOV // 2) as o:
                with sp.If(2 * o < further):
                    e0, e1 = (sp.value_load(meta[0:1, bass.ds(2 * o + b, 1)], min_val=0, max_val=NE - 1)
                              for b in range(2))
                    load_first(NE // 2 + o, e0)
                    load_next(NE // 2 + o, 0, e1, e0)
                    load_last(NE // 2 + o, e1)

            sp.dma_start(fin_w[:], final_norm_w.partition_broadcast(P)).then_inc(final_w_in, 16)
            sp.wait_ge(over_done, 1)
            pairs = y_rows.rearrange("(t p k) d -> t p k d", p=P, k=2)
            for t in range(NT):
                if t >= NY:
                    sp.wait_ge(comb, t - NY + 1)
                sp.dma_start(ytile[t % NY][:], pairs[t]).then_inc(y_in[t % NY], 16)

        @block.gpsimd
        def _(pool):
            link = linker(pool, pool_step)
            link(nc.gpsimd.memset(ident[:], 0.0))
            nc.gpsimd.affine_select(out=ident[:], in_=ident[:], compare_op=ALU.not_equal, fill=1.0, base=0,
                                    pattern=[[-1, P]], channel_multiplier=1).then_inc(consts_ready, 1)
            nc.gpsimd.memset(means[:], 1.0 / DC).then_inc(consts_ready, 1)
            for ri, b in enumerate((B_re, B_im)):
                pool.dma_start(b_raw[:, ri], b[0].rearrange("(n g) p h -> (g p) n h", g=2)).then_inc(braw_in, 16)
            pool.wait_ge(params_in, 16 * 12)
            nc.gpsimd.tensor_copy(a_raw[:, 2, :].rearrange("n (g p) -> n g p", g=2),
                                  dt_raw[:].unsqueeze(2).to_broadcast([NP, 2, NS])).then_inc(consts_ready, 1)
            link(nc.gpsimd.memset(glu_lhs[:], 0.0))
            for g in range(GQ):
                for e in range(2):
                    pool.dma_start(glu_lhs[g * CH:(g + 1) * CH, :, e, g * CH:(g + 1) * CH],
                                   glu_w[0].rearrange("(q g) h (e o) -> g e h q o", g=GQ, e=2)[g, e])\
                        .then_inc(glu_in, 16)
            pool.wait_ge(nx.squares, NT)
            nc.gpsimd.memset(conv_in[:, :, 0:PAD], 0.0).then_inc(v_ready, 1)
            pool.wait_ge(nx.scaled, NT)
            link(nc.gpsimd.memset(shifts[:], 0.0))
            for d in range(T):
                part = shifts[:, d, :].rearrange("p (h j) -> p h j", j=T)[:, :, 0:T - d]
                last = nc.gpsimd.affine_select(out=part, in_=part, compare_op=ALU.not_equal, fill=1.0, base=-d,
                                               pattern=[[-T, CH], [-1, T - d]], channel_multiplier=1)
            last.then_inc(shifts_ready, 1)

            def gated(i, half):
                n = 2 * i + half + 1
                pool.wait_ge(conv_a_ready, n)
                pool.wait_ge(conv_sg_ready, n)
                nc.gpsimd.tensor_tensor(conv_in[:, i, PAD + half * BANK:PAD + (half + 1) * BANK],
                                        conv_a[:], conv_sg[:], ALU.mult).then_inc(v_ready, 1)

            def power_up(dst, src, coef, conj, shape, ready=None, count=0):
                n = 1
                for x in shape:
                    n *= x

                def flat(i):
                    t = pool_tmp[:, i, 0:n]
                    return t.rearrange("p (a b c) -> p a b c", a=shape[0], b=shape[1]) if len(shape) == 3 \
                        else t.rearrange("p (a b) -> p a b", a=shape[0])
                re, im = coef
                nc.gpsimd.tensor_tensor(flat(0), src[0], re, ALU.mult)
                nc.gpsimd.tensor_tensor(flat(1), src[1], im, ALU.mult)
                nc.gpsimd.tensor_tensor(flat(2), src[1], re, ALU.mult)
                link(nc.gpsimd.tensor_tensor(flat(3), src[0], im, ALU.mult))
                nc.gpsimd.tensor_tensor(dst[0], flat(0), flat(1), ALU.add if conj else ALU.subtract)
                last = nc.gpsimd.tensor_tensor(dst[1], flat(2), flat(3), ALU.subtract if conj else ALU.add)
                if ready is None:
                    link(last)
                else:
                    last.then_inc(ready, 1)
                    pool.wait_ge(ready, count)

            def tables(q):
                if q == 0:
                    pool.wait_ge(setup_ready, 1)
                ps = slice(q * PQ, (q + 1) * PQ)
                vin = bpow[:].rearrange("p r n (h s) -> p r n h s", s=T)
                vout = readout[q % 2][:].rearrange("p r n (h s) -> p r n h s", s=T)

                def coef(k, w):
                    return [pw[:, ri, k, ps].unsqueeze(2).unsqueeze(3).to_broadcast([P, PQ, CH, w])
                            for ri in range(2)]
                if q > 0:
                    full(pool, ("lift", q - 1, 1))
                    full(pool, ("kern", q - 1, 1))
                for ri in range(2):
                    last = nc.gpsimd.tensor_copy(vin[:, ri, :, :, T - 1], bbar[:, ri, ps, :])
                link(last)
                for k, w in enumerate((1, 2, 4)):
                    a, b = T - 2 * w, T - w
                    power_up([vin[:, ri, :, :, a:b] for ri in range(2)],
                             [vin[:, ri, :, :, b:b + w] for ri in range(2)], coef(k, w), False, (PQ, CH, w),
                             bpow_ready if k == 2 else None, q + 1)
                if q >= 2:
                    full(pool, ("y", q - 2, 1))
                if q == 1:
                    full(pool, ("u", KC - 1, 1))
                power_up([vout[:, ri, :, :, 0:1] for ri in range(2)],
                         [ct[:, ri, ps, :].unsqueeze(3) for ri in range(2)], coef(0, 1), True, (PQ, CH, 1))
                for k, w in enumerate((1, 2, 4)):
                    power_up([vout[:, ri, :, :, w:2 * w] for ri in range(2)],
                             [vout[:, ri, :, :, 0:w] for ri in range(2)], coef(k, w), True, (PQ, CH, w),
                             readout_ready if k == 2 else None, q + 1)
                if q >= 2:
                    pool.wait_ge(states_ready, q - 1)
                e = phase[q % 2]
                nc.gpsimd.memset(e[:, 0, :, 0:1], 1.0)
                link(nc.gpsimd.memset(e[:, 1, :, 0:1], 0.0))
                for k in range(7):
                    w = 1 << k
                    power_up([e[:, ri, :, w:2 * w] for ri in range(2)], [e[:, ri, :, 0:w] for ri in range(2)],
                             [ph[:, ri, k, ps].unsqueeze(2).to_broadcast([P, PQ, w]) for ri in range(2)],
                             False, (PQ, w), phase_ready if k == 6 else None, q + 1)

            for i in range(KC):
                gated(i, 0)
                gated(i, 1)
                if i == 1:
                    tables(0)
            for q in range(1, NQ):
                tables(q)

            full(pool, ("router", NT - 1))
            for b in range(2):
                pool.wait_ge(xn_out[b], 16 * NT // 2)
            link(nc.gpsimd.memset(upper[:], 1.0))
            nc.gpsimd.affine_select(out=upper[:], in_=upper[:], compare_op=ALU.is_gt, fill=0.0, base=0,
                                    pattern=[[1, P]], channel_multiplier=-1).then_inc(route_consts, 1)
            nc.gpsimd.memset(ones[:], 1.0).then_inc(route_consts, 1)
            iota = dict(allow_small_or_imprecise_dtypes=True)
            nc.gpsimd.iota(iota_n[:], pattern=[[1, P]], base=0, channel_multiplier=0, **iota).then_inc(route_consts, 1)
            nc.gpsimd.iota(assign_no[:], pattern=[[1, 2], [2 * P, NT]], base=1, channel_multiplier=2, **iota)\
                .then_inc(route_consts, 1)
            nc.gpsimd.iota(limits[:], pattern=[[P, 7]], base=P, channel_multiplier=0, **iota).then_inc(route_consts, 1)

            for k in range(NSPLIT):
                pool.wait_ge(hi_ready, k + 1)
                nc.gpsimd.tensor_tensor(out=w_lo[k][:], in0=raw[k][:], in1=w_hi[k][:].bitcast(F32), op=ALU.subtract)\
                    .then_inc(lo_ready, 1)

            last_token = pool.to_reg(S - 1)
            last_row = pool.to_reg(2 * S - 1)

            def fetch(b):
                pool.sem_inc(rows_moved, 1)
                nc.gpsimd.indirect_dma_start(
                    out=xg[b][:], out_offset=None, in_=xn_rows,
                    in_offset=bass.IndirectOffsetOnAxis(ap=gidx[b][:, 0:1], axis=0),
                    bounds_check=last_token, oob_is_err=False).then_inc(xg_in[b], 16)

            def send(b, i):
                pool.wait_ge(sidx_ready, i + 1)
                pool.wait_ge(yb_ready, i + 1)
                pool.sem_inc(rows_moved, 1)
                nc.gpsimd.indirect_dma_start(
                    out=y_rows, out_offset=bass.IndirectOffsetOnAxis(ap=sidx[b][:, 0:1], axis=0),
                    in_=yb[b][:], in_offset=None,
                    bounds_check=last_row, oob_is_err=False).then_inc(y_sent[b], 16)

            pool.wait_ge(sel_used, 1)
            for b in range(2):
                nc.gpsimd.memset(xg[b][:], 0.0).then_inc(xg_clear, 1)
            pool.wait_ge(xg_clear, 2)
            for b in range(2):
                pool.wait_ge(gidx_ready, b + 1)
                fetch(b)
            for i in (2, 3):
                pool.wait_ge(gidx_ready, i + 1)
                pool.wait_ge(xg_turned, i - 1)
                fetch(i % 2)
            with pool.Fori(0, NE // 2 - 2) as j:
                for b in range(2):
                    send(b, 2 * j + b)
                    pool.wait_ge(gidx_ready, 2 * j + b + 5)
                    pool.wait_ge(xg_turned, 2 * j + b + 3)
                    fetch(b)
            for i in range(NE - 4, NE):
                send(i % 2, i)
            further = pool.value_load(meta[0:1, MAXOV:MAXOV + 1], min_val=0, max_val=MAXOV)
            with pool.Fori(0, MAXOV // 2) as o:
                with pool.If(2 * o < further):
                    for b in range(2):
                        pool.wait_ge(gidx_ready, NE + 2 * o + b + 1)
                        fetch(b)
                    for b in range(2):
                        send(b, NE + 2 * o + b)
                    for b in range(2):
                        pool.wait_ge(y_sent[b], 16 * (NE // 2 + 1) + 16 * o)
            for b in range(2):
                pool.wait_ge(y_sent[b], 16 * (NE // 2))
            nc.gpsimd.memset(pool_mark[:], 0.0).then_inc(over_done, 1)

            out_rows = out[0].rearrange("(t p) d -> t p d", p=P)
            for t in range(NT):
                pool.wait_ge(out_ready, t + 1)
                pool.dma_start(out_rows[t], otile[t % 2][:]).then_inc(out_stored[t % 2], 16)
            for b in range(2):
                pool.wait_ge(out_stored[b], 16 * NT // 2)

        @block.scalar
        def _(act):
            link = linker(act, act_step)
            rows = ((norm_mix_w, 0), (norm_x_w, 8), (norm_mem_w, 16), (norm_ffn_w, 24))
            for w, r in rows:
                act.dma_start(rows_raw[r:r + KD, :], w[0].rearrange("(c p) -> c p", p=P)).then_inc(params_in, 16)
            for i, w in enumerate((conv_b, conv_ln_w, conv_ln_b, ssm_D.rearrange("a g c -> a (g c)"))):
                act.dma_start(rows_raw[32 + 4 * i:36 + 4 * i, :],
                               w[0].rearrange("(c p) -> c p", p=P)).then_inc(params_in, 16)
            act.dma_start(taps_raw[0:TAPS * KC, :], conv_w[0].rearrange("k (c p) -> (k c) p", p=P))\
                .then_inc(params_in, 16)
            act.dma_start(a_raw[:, 0, :], A_re[0].rearrange("(n g) p -> n (g p)", g=2)).then_inc(params_in, 16)
            act.dma_start(a_raw[:, 1, :], A_im[0].rearrange("(n g) p -> n (g p)", g=2)).then_inc(params_in, 16)
            act.dma_start(dt_raw[:], log_dt[0].rearrange("(n g) -> n g", g=2)).then_inc(params_in, 16)
            act.dma_start(c_raw[:, 0, :].rearrange("h (g p) -> h g p", p=NS),
                           C_re[0].rearrange("g h p -> h g p")).then_inc(craw_in, 16)
            act.dma_start(c_raw[:, 1, :].rearrange("h (g p) -> h g p", p=NS),
                           C_im[0].rearrange("g h p -> h g p")).then_inc(craw_in, 16)
            act.dma_start(par[:, 48:56], norm_ffn_w[0].rearrange("(p c) -> p c", p=P)).then_inc(par_in, 16)

            def act_squares(norm, src, t, scratch, st):
                if t > 0:
                    act.wait_ge(norm.squares, t)
                nc.scalar.activation(scratch, src, ACT.Square, accum_out=st[:, 0, t:t + 1])\
                    .then_inc(norm.squares, 1)

            def act_root(norm, t, st):
                act.wait_ge(norm.var, t + 1)
                nc.scalar.activation(st[:, 1, t:t + 1], st[:, 1, t:t + 1], ACT.Sqrt).then_inc(norm.root, 1)

            def act_scale(norm, dst, src, t, st):
                act.wait_ge(norm.rstd, t + 1)
                nc.scalar.activation(dst, src, ACT.Copy, scale=st[:, 2, t:t + 1]).then_inc(norm.scaled, 1)

            act.wait_ge(x_in[0], 16)
            act_squares(nx, h[:, 0, :], 0, junk_x[:], stat)
            for t in range(NT):
                if t + 1 < NT:
                    act.wait_ge(x_in[t + 1], 16)
                    act_squares(nx, h[:, t + 1, :], t + 1, junk_x[:], stat)
                act_root(nx, t, stat)
            act.wait_ge(trig_in, 1)
            nc.scalar.activation(t16[:, 9], t16[:, 4], ACT.Sin).then_inc(trig_out, 1)
            nc.scalar.activation(t16[:, 10], t16[:, 4], ACT.Sin, scale=0.5).then_inc(trig_out, 1)
            act.wait_ge(mem_in, 16)
            act.wait_ge(nx.scaled, NT)
            for t in range(MT):
                act_squares(nm, mem_rows[:, t, :], t, junk_m[:], stat_m)
                act_root(nm, t, stat_m)
                act_scale(nm, mem_rows[:, t, :], mem_rows[:, t, :], t, stat_m)

            for i in range(KC):
                for half in range(2):
                    n = 2 * i + half
                    if n > 0:
                        act.wait_ge(v_ready, n + 1)
                    src = full(act, ("a", i, half))
                    nc.scalar.activation(conv_a[:], src[:], ACT.Copy).then_inc(conv_a_ready, 1)
                    act.wait_ge(conv_a_ready, n + 1)
                    nc.scalar.sem_inc(bank_free[half], 1)
                    src = full(act, ("g", i, half))
                    nc.scalar.activation(conv_sg[:], src[:], ACT.Sigmoid).then_inc(conv_sg_ready, 1)
                    act.wait_ge(conv_sg_ready, n + 1)
                    nc.scalar.sem_inc(bank_free[2 + half], 1)
            for q in range(NQ):
                for half in range(2):
                    src = full(act, ("u", q, half))
                    nc.scalar.activation(u_perm[:, q, :, half * NC // 2:(half + 1) * NC // 2],
                                         src[:].rearrange("p (c j) -> p j c", j=T), ACT.Copy).then_inc(u_ready, 1)
                    act.wait_ge(u_ready, 2 * q + half + 1)
                    nc.scalar.sem_inc(bank_free[4 + half], 1)
            for t in range(MT):
                for c in range(KD):
                    src = full(act, ("m", t, c // 4))
                    nc.scalar.activation(memT[:, c, t * P:(t + 1) * P], src[:, (c % 4) * P:(c % 4 + 1) * P], ACT.Copy,
                                         scale=par[:, 16 + c:17 + c]).then_inc(memT_ready, 1)
                    if c % 4 == 3:
                        act.wait_ge(memT_ready, t * KD + c + 1)
                        nc.scalar.sem_inc(bank_free[6 + c // 4], 1)

            def read_out(key, dst, src, ready, count, **how):
                b, _ = use_of[key]
                full(act, key)
                nc.scalar.activation(dst, src(bank[b]), how.pop("func", ACT.Copy), **how).then_inc(ready, 1)
                act.wait_ge(ready, count)
                nc.scalar.sem_inc(bank_free[b], 1)

            def setup_out(q):
                for ri in range(2):
                    if ri == 0 and q >= 2:
                        full(act, ("S", q - 2, 1))
                    read_out(("lift", q, ri), lift[q % 2][:, ri].rearrange("p n m -> p (n m)"), lambda b: b[:],
                             lift_ready, 2 * q + ri + 1)
                for g2 in range(2):
                    if q > 0 and g2 == 0:
                        full(act, ("toep", q - 1, 1))
                    read_out(("kern", q, g2), kern[:].rearrange("p (n g) o -> p g n o", g=2)[:, g2],
                             lambda b: b[:, 0:PQ * CH].rearrange("p (n o) -> p n o", o=CH), kern_ready, 2 * q + g2 + 1)
                for jh in range(2):
                    if q >= 2 and jh == 0:
                        full(act, ("y", q - 2, 1))
                    read_out(("toep", q, jh),
                             toep[q % 2][:].rearrange("p g (o j) -> p j g o", j=T)[:, 4 * jh:4 * jh + 4],
                             lambda b: b[:].rearrange("p (j g o) -> p j g o", j=4, g=GQ), toep_ready, 2 * q + jh + 1)

            kv = [0]

            def kv_out(n):
                if n < 2:
                    for m in range(4):
                        kv[0] += 1
                        read_out(("k", 4 * n + m), kT[:, 4 * n + m, :], lambda b: b[:, 0:M], kv_ready, kv[0])
                else:
                    for mt in range(MT):
                        kv[0] += 1
                        read_out(("v", n - 2, mt), vm[:, mt, (n - 2) * BANK:(n - 1) * BANK], lambda b: b[:],
                                 kv_ready, kv[0])

            def glu_gates(q):
                act.wait_ge(dterm_done, q + 1)
                nc.scalar.activation(y_feat[:], y_feat[:], ACT.Gelu_apprx_tanh).then_inc(gelu_done, 1)
                for jh in range(2):
                    n = 2 * q + jh
                    if n > 0:
                        act.wait_ge(yssm_ready, n)
                    read_out(("glu", q, jh, 1), glu_sig[:], lambda b: b[:], glu_sig_ready, n + 1, func=ACT.Sigmoid)

            setup_out(0)
            for q in range(NQ):
                kv_out(q)
                if q > 0:
                    glu_gates(q - 1)
                for g2 in range(2):
                    if g2 == 0 and q > 0:
                        act.wait_ge(yb_out, 16 * q)
                    read_out(("y", q, g2), y_chunks[:].rearrange("p (n g) c -> p g n c", g=2)[:, g2],
                             lambda b: b[:].rearrange("p (n c) -> p n c", c=NC), ychunk_ready, 2 * q + g2 + 1)
                if q + 1 < NQ:
                    setup_out(q + 1)
                if q == 0:
                    for half in range(2):
                        act.wait_ge(centered, half + 1)
                        nc.scalar.activation(squares[:, half], conv_acc[:, :, half * BANK:(half + 1) * BANK],
                                             ACT.Square).then_inc(squared, 1)
                if q == 1:
                    act.wait_ge(ln_v, 2)
                    nc.scalar.activation(ln_var[:], ln_var[:], ACT.Sqrt).then_inc(ln_root, 1)
                    act.wait_ge(ln_scaled, 2)
                    for k in range(KC):
                        nc.scalar.activation(conv_acc[:, k, :], conv_acc[:, k, :], ACT.Silu,
                                             bias=par[:, 40 + k:41 + k], scale=par[:, 36 + k:37 + k])\
                            .then_inc(yconv_ready, 1)
            glu_gates(NQ - 1)

            full(act, ("glu", NQ - 1, 1, 1))
            act.dma_start(router_w[:, :, 0:NG], router_group_w[0].rearrange("(c p) n -> p c n", p=P))\
               .then_inc(router_in, 16)
            act.dma_start(router_w[:, :, NG:NR], router_expert_w[0].rearrange("(c p) n -> p c n", p=P))\
               .then_inc(router_in, 16)
            act.dma_start(router_b[:, 0:NG], router_group_b[0].partition_broadcast(P)).then_inc(router_in, 16)
            act.dma_start(router_b[:, NG:NR], router_expert_b[0].rearrange("g e -> (g e)").partition_broadcast(P))\
               .then_inc(router_in, 16)

            for t in range(NT):
                act.wait_ge(h1_ready, 2 * t + 2)
                act_squares(n1, h[:, t, :], t, junk[:], stat)
                act_root(n1, t, stat)
                if t >= 2:
                    full(act, ("h1T", t - 2, 1))
                act_scale(n1, xs[t % 2][:], h[:, t, :], t, stat)
            for m in range(KD):
                for half in range(2):
                    read_out(("q", m, half), qT[:, m, half * BANK:(half + 1) * BANK], lambda b: b[:],
                             q_ready, 2 * m + half + 1, scale=float(HD) ** -0.5)

            for s in range(NT + 4):
                t = s
                if t < NT:
                    act.wait_ge(negmax_ready, 2 * t + 2)
                    if t >= 2:
                        full(act, ("pT", t - 2, 1))
                    for hd in range(NH):
                        nc.scalar.activation(probs[t % 2][:, hd, :], bank[hd // 2][:, (hd % 2) * M:(hd % 2 + 1) * M],
                                             ACT.Exp, bias=negmax[:, t % 2, hd:hd + 1],
                                             accum_out=expsum[:, t % 2, hd:hd + 1]).then_inc(exp_done, 1)
                        if hd % 2:
                            act.wait_ge(exp_done, NH * t + hd + 1)
                            nc.scalar.sem_inc(bank_free[hd // 2], 1)
                t = s - 2
                if 0 <= t < NT:
                    act.wait_ge(h2_ready, 2 * t + 2)
                    if t == 0:
                        act.wait_ge(n1.squares, NT)
                    act_squares(nf, h[:, t, :], t, junk[:], stat)
                    act_root(nf, t, stat)
                    if t >= 2:
                        full(act, ("h2T", t - 2, 1))
                        act.wait_ge(xn_out[t % 2], 16 * (t // 2))
                    act_scale(nf, xs[t % 2][:], h[:, t, :], t, stat)
                    act.wait_ge(nf.scaled, t + 1)
                    act.dma_start(xn_rows[t * P:(t + 1) * P, :], xs[t % 2][:]).then_inc(xn_out[t % 2], 16)
                t = s - 1
                if 0 <= t < NT:
                    for b in range(2):
                        read_out(("o", t, b), oT[:, 4 * b:4 * b + 4, t * P:(t + 1) * P],
                                 lambda x: x[:].rearrange("p (m n) -> p m n", n=P), oT_ready, 2 * t + b + 1)
                t = s - 4
                if 0 <= t < NT:
                    read_out(("router", t), logits[:, t, :], lambda b: b[:, 0:NR], logit_ready, t + 1)

            act.wait_ge(gexp_in, 1)
            nc.scalar.activation(gsel[:, 0], gsel[:, 0], ACT.Exp).then_inc(gexp_out, 1)
            act.wait_ge(pexp_in, 1)
            nc.scalar.activation(col[:, 6], col[:, 6], ACT.Exp).then_inc(pexp_out, 1)

            def split_high(j, k):
                act.wait_ge(raw_in[k % NRAW], 16 * (2 * j + k // NRAW + 1))
                wait_for(act, piece_used, 12 * j + k - NSPLIT + 1)
                nc.scalar.activation(w_hi[k % NSPLIT][:], raw[k % NRAW][:], ACT.Copy).then_inc(hi_ready, 1)

            def tokens_high(b, i):
                act.wait_ge(xw_ready, i + 1)
                nc.scalar.activation(x_hi[b][:], xw[:], ACT.Copy).then_inc(x_hi_ready, 1)

            def gate_of(j, k):
                act.wait_ge(piece_used, 12 * j + k)
                nc.scalar.activation(gate_act[:], bank[2][:], ACT.Silu).then_inc(gate_ready, 1)

            def hidden_high(i):
                act.wait_ge(hid_turned, i + 1)
                nc.scalar.activation(hid_hi[:].rearrange("p f n -> p (f n)"), bank[4][:], ACT.Copy)\
                    .then_inc(hid_hi_ready, 1)

            def rows_out(j, k, b):
                act.wait_ge(piece_used, 12 * j + k)
                wait_for(act, y_sent[b], 16 * j)
                nc.scalar.activation(yb[b][:, 0:BANK], bank[5][:], ACT.Copy)
                nc.scalar.activation(yb[b][:, BANK:D], bank[6][:], ACT.Copy).then_inc(yb_ready, 1)

            def first_block(j):
                for k in range(NSPLIT):
                    split_high(j, k)
                tokens_high(0, 2 * j)
                split_high(j, 4)
                gate_of(j, 2)
                split_high(j, 5)
                tokens_high(1, 2 * j + 1)
                split_high(j, 6)
                split_high(j, 7)

            def next_block(j, s, final=False):
                i, k = 2 * j + 1 + s, 4 + 6 * s
                hidden_high(i - 1)
                split_high(j, k + 4)
                gate_of(j, k + 2)
                split_high(j, k + 5)
                split_high(j, k + 6)
                rows_out(j, k + 4, s)
                split_high(j, k + 7)
                if not final:
                    tokens_high(s, i + 1)
                    split_high(j, k + 8)
                    split_high(j, k + 9)

            def last_down(j):
                hidden_high(2 * j + 1)
                rows_out(j, 12, 1)

            for key in (("o", NT - 1, 1), ("h2", NT - 1, 1)):
                full(act, key)
            first_block(0)
            for s in range(2):
                next_block(0, s)
            with act.Fori(1, NE // 2 - 1) as j:
                for s in range(2):
                    next_block(j, s)
            next_block(NE // 2 - 1, 0, final=True)
            last_down(NE // 2 - 1)
            further = act.value_load(meta[0:1, MAXOV:MAXOV + 1], min_val=0, max_val=MAXOV)
            with act.Fori(0, MAXOV // 2) as o:
                with act.If(2 * o < further):
                    first_block(NE // 2 + o)
                    next_block(NE // 2 + o, 0, final=True)
                    last_down(NE // 2 + o)

            act.wait_ge(comb, 1)
            act_squares(n2, h[:, 0, :], 0, junk_f[:], stat)
            for t in range(NT):
                if t + 1 < NT:
                    act.wait_ge(comb, t + 2)
                    act_squares(n2, h[:, t + 1, :], t + 1, junk_f[:], stat)
                act_root(n2, t, stat)

        @block.vector
        def _(dve):
            link = linker(dve, dve_step)
            V = nc.vector

            def ts(out, a, s1, s2, op0, op1=ALU.bypass):
                return V.tensor_scalar(out, a, s1, s2, op0, op1)

            def stt(out, a, s, b, op0, op1):
                return V.scalar_tensor_tensor(out=out, in0=a, scalar=s, in1=b, op0=op0, op1=op1)

            def tt(out, a, b, op):
                return V.tensor_tensor(out, a, b, op)

            def frees(key, ins):
                ins.then_inc(bank_free[use_of[key][0]], 1)

            def dve_var(norm, t, st):
                dve.wait_ge(norm.squares, t + 1)
                ts(st[:, 1, t:t + 1], st[:, 0, t:t + 1], 1.0 / D, EPS, ALU.mult, ALU.add).then_inc(norm.var, 1)

            def dve_rstd(norm, t, st):
                dve.wait_ge(norm.root, t + 1)
                V.reciprocal(st[:, 2, t:t + 1], st[:, 1, t:t + 1]).then_inc(norm.rstd, 1)

            def dve_store(norm, key, dst, t, c0):
                for b in range(2):
                    src = full(dve, (key, t, b))
                    w = par[:, c0 + 4 * b:c0 + 4 * b + 4].unsqueeze(2).to_broadcast([P, 4, P])
                    link(tt(dst[:, 4 * b:4 * b + 4], src[:].rearrange("p (c n) -> p c n", n=P), w, ALU.mult))
                    V.sem_inc(bank_free[use_of[(key, t, b)][0]], 1)
                V.sem_inc(norm.stored, 1)

            full(dve, "par")
            link(V.tensor_copy(par[:, 0:48], bank[0][:, 0:48]))
            V.sem_inc(bank_free[0], 1)
            dve_var(nx, 0, stat)
            for t in range(NT + 1):
                if t < NT:
                    if t + 1 < NT:
                        dve_var(nx, t + 1, stat)
                    dve_rstd(nx, t, stat)
                    dve.wait_ge(nx.rstd, t + 1)
                    if t >= 2:
                        full(dve, ("x", t - 2, 1))
                    ts(xs0[t % 2][:], h[:, t, :], stat[:, 2, t:t + 1], None, ALU.mult).then_inc(nx.scaled, 1)
                if t > 0:
                    dve_store(nx, "x", xT[:, :, (t - 1) * P:t * P], t - 1, 0)
            full(dve, "taps")
            link(V.tensor_copy(taps[:], bank[1][:, 0:TAPS * KC]))
            V.sem_inc(bank_free[1], 1)
            full(dve, "a_raw")
            link(V.tensor_copy(t16[:, 0:3], bank[2][:, 0:3 * NP].rearrange("p (i n) -> p i n", n=NP)))
            V.sem_inc(bank_free[2], 1)
            full(dve, "c_raw")
            c_turned = bank[3][:].rearrange("p (r n h) -> p r n h", r=2, n=NP)
            link(V.tensor_copy(ct[:, 0], c_turned[:, 0]))
            link(ts(ct[:, 1], c_turned[:, 1], -1.0, None, ALU.mult))
            V.sem_inc(bank_free[3], 1)


            def z(i):
                return t16[:, i]
            are, aim, ldt = z(0), z(1), z(2)

            def expm1_poly(out, f):
                link(ts(out, f, 1.0 / 5040, None, ALU.mult))
                for c in (1.0 / 720, 1.0 / 120, 1.0 / 24, 1.0 / 6, 0.5, 1.0):
                    link(stt(out, out, c, f, ALU.add, ALU.mult))

            link(ts(z(3), ldt, LOG2E, ROUND, ALU.mult, ALU.add))
            link(ts(z(3), z(3), ROUND, None, ALU.subtract))
            link(stt(z(4), z(3), -LN2_HI, ldt, ALU.mult, ALU.add))
            link(stt(z(4), z(3), -LN2_LO, z(4), ALU.mult, ALU.add))
            expm1_poly(z(5), z(4))
            link(ts(z(3), z(3), -127.0, 128.0, ALU.max, ALU.min))
            link(ts(z(6).bitcast(I32), z(3), 127.0, float(1 << 23), ALU.add, ALU.mult))
            link(stt(z(2), z(5), 1.0, z(6), ALU.add, ALU.mult))
            link(tt(z(7), are, z(2), ALU.mult))
            link(tt(z(8), aim, z(2), ALU.mult))
            link(ts(z(7), z(7), -87.0, 1.0 / 256, ALU.max, ALU.mult))
            expm1_poly(z(5), z(7))
            for _ in range(8):
                link(stt(z(5), z(5), 2.0, z(5), ALU.add, ALU.mult))
            link(ts(z(3), z(8), 1.0 / TWO_PI, ROUND, ALU.mult, ALU.add))
            link(ts(z(3), z(3), ROUND, None, ALU.subtract))
            link(stt(z(4), z(3), -TWO_PI_A, z(8), ALU.mult, ALU.add))
            link(stt(z(4), z(3), -TWO_PI_B, z(4), ALU.mult, ALU.add))
            link(stt(z(4), z(3), -TWO_PI_C, z(4), ALU.mult, ALU.add))
            ts(z(4), z(4), -PI_LOW, PI_LOW, ALU.max, ALU.min).then_inc(trig_in, 1)
            dve.wait_ge(trig_out, 2)
            link(stt(z(6), z(10), -2.0, z(10), ALU.mult, ALU.mult))
            link(ts(z(11), z(6), 1.0, None, ALU.add))
            link(ts(z(8), z(5), 1.0, None, ALU.add))
            link(tt(pw[:, 0, 0], z(8), z(11), ALU.mult))
            link(tt(pw[:, 1, 0], z(8), z(9), ALU.mult))
            link(tt(z(3), z(5), z(11), ALU.mult))
            link(tt(z(3), z(3), z(6), ALU.add))
            link(tt(z(4), are, are, ALU.mult))
            link(tt(z(7), aim, aim, ALU.mult))
            link(tt(z(4), z(4), z(7), ALU.add))
            link(V.reciprocal(z(4), z(4)))
            link(tt(z(5), z(3), are, ALU.mult))
            link(tt(z(6), pw[:, 1, 0], aim, ALU.mult))
            link(tt(z(5), z(5), z(6), ALU.add))
            link(tt(z(5), z(5), z(4), ALU.mult))
            link(tt(z(6), pw[:, 1, 0], are, ALU.mult))
            link(tt(z(7), z(3), aim, ALU.mult))
            link(tt(z(6), z(6), z(7), ALU.subtract))
            link(tt(z(6), z(6), z(4), ALU.mult))
            dve.wait_ge(braw_in, 32)
            wre = z(5).unsqueeze(2).to_broadcast([P, NP, CH])
            wim = z(6).unsqueeze(2).to_broadcast([P, NP, CH])
            link(tt(bbar[:, 0], b_raw[:, 0], wre, ALU.mult))
            link(tt(bbar[:, 1], b_raw[:, 1], wim, ALU.mult))
            link(tt(bbar[:, 0], bbar[:, 0], bbar[:, 1], ALU.subtract))
            link(tt(bbar[:, 1], b_raw[:, 1], wre, ALU.mult))
            link(tt(b_raw[:, 0], b_raw[:, 0], wim, ALU.mult))
            link(tt(bbar[:, 1], bbar[:, 1], b_raw[:, 0], ALU.add))

            def square(dre, dim, re, im):
                link(tt(z(3), im, im, ALU.mult))
                link(tt(z(4), re, re, ALU.mult))
                link(stt(dim, re, 2.0, im, ALU.mult, ALU.mult))
                link(tt(dre, z(4), z(3), ALU.subtract))
            square(pw[:, 0, 1], pw[:, 1, 1], pw[:, 0, 0], pw[:, 1, 0])
            square(pw[:, 0, 2], pw[:, 1, 2], pw[:, 0, 1], pw[:, 1, 1])
            link(tt(rho[:], z(8), z(8), ALU.mult))
            link(tt(rho[:], rho[:], rho[:], ALU.mult))
            link(tt(rho[:], rho[:], rho[:], ALU.mult))
            square(z(5), z(6), z(11), z(9))
            square(z(7), z(8), z(5), z(6))
            square(ph[:, 0, 0], ph[:, 1, 0], z(7), z(8))
            for k in range(6):
                square(ph[:, 0, k + 1], ph[:, 1, k + 1], ph[:, 0, k], ph[:, 1, k])
            V.sem_inc(setup_ready, 1)

            for t in range(MT):
                dve_var(nm, t, stat_m)
                dve_rstd(nm, t, stat_m)
            for i in range(KC):
                dve.wait_ge(v_ready, 2 * i + 3)
                link(ts(conv_acc[:, i, :], conv_in[:, i, 0:S], taps[:, i:i + 1], par[:, 32 + i:33 + i],
                        ALU.mult, ALU.add))
                for k in range(1, TAPS):
                    ins = stt(conv_acc[:, i, :], conv_in[:, i, k:k + S], taps[:, k * KC + i:k * KC + i + 1],
                              conv_acc[:, i, :], ALU.mult, ALU.add)
                    if k < TAPS - 1:
                        link(ins)
                ins.then_inc(conv_done, 1)

            def rotate(q):
                cos, sin = phase[q % 2][:, 0], phase[q % 2][:, 1]
                re, im = (bank[6 + ri][:].rearrange("p (n c) -> p n c", c=NC) for ri in range(2))
                dve.wait_ge(phase_ready, q + 1)
                full(dve, ("S", q, 0))
                full(dve, ("S", q, 1))
                tt(rotated[:, 0], re, cos, ALU.mult)
                tt(rot_tmp[:, 0], im, sin, ALU.mult)
                tt(rotated[:, 1], im, cos, ALU.mult)
                link(tt(rot_tmp[:, 1], re, sin, ALU.mult))
                V.sem_inc(bank_free[6], 1)
                V.sem_inc(bank_free[7], 1)
                tt(rotated[:, 0], rotated[:, 0], rot_tmp[:, 0], ALU.add)
                link(tt(rotated[:, 1], rotated[:, 1], rot_tmp[:, 1], ALU.subtract))
                for ri in range(2):
                    for p in PAIRS:
                        n = q * PQ + p
                        last = V.tensor_tensor_scan(scanned[:, ri, p, :], rho[:, n:n + 1].to_broadcast([P, NC]),
                                                    rotated[:, ri, p, :], 0.0, ALU.mult, ALU.add)
                link(last)
                tt(rotated[:, 0], scanned[:, 0], cos, ALU.mult)
                tt(rot_tmp[:, 0], scanned[:, 1], sin, ALU.mult)
                tt(rotated[:, 1], scanned[:, 0], sin, ALU.mult)
                link(tt(rot_tmp[:, 1], scanned[:, 1], cos, ALU.mult))
                if q == 0:
                    link(V.memset(states[:, :, :, 0:1], 0.0))
                else:
                    full(dve, ("y", q - 1, 1))
                tt(states[:, 0, :, 1:NC + 1], rotated[:, 0], rot_tmp[:, 0], ALU.subtract)
                link(tt(states[:, 1, :, 1:NC + 1], rotated[:, 1], rot_tmp[:, 1], ALU.add))
                V.sem_inc(states_ready, 1)

            def direct(q):
                dve.wait_ge(yf_in, 16 * q + 16)
                stt(y_feat[:], u_perm[:, q], par[:, 44 + q:45 + q], y_feat[:], ALU.mult, ALU.add)\
                    .then_inc(dterm_done, 1)

            def gated(q):
                for jh in range(2):
                    n = 2 * q + jh + 1
                    dve.wait_ge(glu_sig_ready, n)
                    src = full(dve, ("glu", q, jh, 0))
                    tt(yT[:, q, :].rearrange("p (c j) -> p j c", j=T)[:, 4 * jh:4 * jh + 4],
                       src[:].rearrange("p (j c) -> p j c", j=4),
                       glu_sig[:].rearrange("p (j c) -> p j c", j=4), ALU.mult).then_inc(yssm_ready, 1)
                    dve.wait_ge(yssm_ready, n)
                    V.sem_inc(bank_free[use_of[("glu", q, jh, 0)][0]], 1)

            def half_of_conv(half):
                return conv_acc[:, :, half * BANK:(half + 1) * BANK]

            rotate(0)
            for half in range(2):
                src = full(dve, ("mean", half))
                tt(half_of_conv(half), half_of_conv(half), src[:].unsqueeze(1).to_broadcast([P, KC, BANK]),
                   ALU.subtract).then_inc(centered, 1)
                dve.wait_ge(centered, half + 1)
                V.sem_inc(bank_free[use_of[("mean", half)][0]], 1)
            direct(0)
            rotate(1)
            gated(0)
            for half in range(2):
                src = full(dve, ("lnvar", half))
                ts(ln_var[:, half], src[:], EPS, None, ALU.add).then_inc(ln_v, 1)
                dve.wait_ge(ln_v, half + 1)
                V.sem_inc(bank_free[use_of[("lnvar", half)][0]], 1)
            dve.wait_ge(ln_root, 1)
            link(V.reciprocal(ln_var[:], ln_var[:]))
            for half in range(2):
                tt(half_of_conv(half), half_of_conv(half), ln_var[:, half].unsqueeze(1).to_broadcast([P, KC, BANK]),
                   ALU.mult).then_inc(ln_scaled, 1)
            direct(1)
            rotate(2)
            gated(1)
            direct(2)
            rotate(3)
            gated(2)
            direct(3)
            gated(3)

            for t in range(NT):
                dve.wait_ge(x_in[t], 32)
                for half in range(2):
                    src = full(dve, ("h1", t, half))
                    part = h[:, t, half * BANK:(half + 1) * BANK]
                    tt(part, part, src[:], ALU.add).then_inc(h1_ready, 1)
                    dve.wait_ge(h1_ready, 2 * t + half + 1)
                    V.sem_inc(bank_free[use_of[("h1", t, half)][0]], 1)
                if t > 0:
                    dve_store(n1, "h1T", hT[:, :, (t - 1) * P:t * P], t - 1, 8)
                dve_var(n1, t, stat)
                dve_rstd(n1, t, stat)
            dve_store(n1, "h1T", hT[:, :, (NT - 1) * P:NT * P], NT - 1, 8)

            for s in range(NT + 4):
                t = s
                if t < NT:
                    for b in range(2):
                        src = full(dve, ("s", t, b))
                        V.tensor_reduce(out=negmax[:, t % 2, 2 * b:2 * b + 2],
                                        in_=src[:].rearrange("p (h m) -> p h m", m=M), axis=AX.X, op=ALU.max,
                                        negate=True).then_inc(negmax_ready, 1)
                t = s - 1
                if 0 <= t < NT:
                    for b in range(2):
                        src = full(dve, ("pT", t, b))
                        if t >= 2 and b == 0:
                            full(dve, ("o", t - 2, 1))
                        V.tensor_copy(pT[t % 2][:, 4 * b:4 * b + 4, :], src[:].rearrange("p (i n) -> p i n", n=P))\
                            .then_inc(pT_ready, 1)
                        dve.wait_ge(pT_ready, 2 * t + b + 1)
                        V.sem_inc(bank_free[use_of[("pT", t, b)][0]], 1)
                t = s
                if t < NT:
                    dve.wait_ge(exp_done, NH * (t + 1))
                    link(V.reciprocal(expsum[:, t % 2], expsum[:, t % 2]))
                    tt(probs[t % 2][:], probs[t % 2][:], expsum[:, t % 2].unsqueeze(2).to_broadcast([P, NH, M]),
                       ALU.mult).then_inc(probs_ready, 1)
                t = s - 2
                if 0 <= t < NT:
                    for half in range(2):
                        src = full(dve, ("h2", t, half))
                        part = h[:, t, half * BANK:(half + 1) * BANK]
                        tt(part, part, src[:], ALU.add).then_inc(h2_ready, 1)
                        dve.wait_ge(h2_ready, 2 * t + half + 1)
                        V.sem_inc(bank_free[use_of[("h2", t, half)][0]], 1)
                    dve_var(nf, t, stat)
                    dve_rstd(nf, t, stat)
                t = s - 3
                if 0 <= t < NT:
                    if t >= 2:
                        full(dve, ("router", t - 2))
                    dve_store(nf, "h2T", fT[t % 2], t, 24)

            dve.wait_ge(logit_ready, NT)
            dve.wait_ge(route_consts, 5)
            dve.wait_ge(router_in, 64)

            def wide(a, n):
                return a.unsqueeze(2).to_broadcast([P, NT, n])

            def numbers(n):
                return iota_n[:, 0:n].unsqueeze(1).to_broadcast([P, NT, n])

            link(tt(lg[:], logits[:], router_b[:].unsqueeze(1).to_broadcast([P, NT, NR]), ALU.add))

            def first_of_max(src, n, top, which, onehot, tmp):
                link(V.tensor_reduce(out=top, in_=src, axis=AX.X, op=ALU.max))
                link(tt(tmp, src, wide(top, n), ALU.is_ge))
                link(ts(tmp, tmp, -128.0, 128.0, ALU.mult, ALU.add))
                link(tt(tmp, tmp, numbers(n), ALU.add))
                link(V.tensor_reduce(out=which, in_=tmp, axis=AX.X, op=ALU.min))
                link(tt(onehot, numbers(n), wide(which, n), ALU.is_equal))

            first_of_max(lg[:, :, 0:NG], NG, col[:, 0], col[:, 1], gsel[:, 1], gsel[:, 0])
            tt(gsel[:, 0], lg[:, :, 0:NG], wide(col[:, 0], NG), ALU.subtract).then_inc(gexp_in, 1)
            link(ts(etmp[:, :, 0:NG], gsel[:, 1], -1.0, 1e30, ALU.add, ALU.mult))
            link(tt(em[:].rearrange("p t (g e) -> p t g e", e=EPG),
                    lg[:, :, NG:NR].rearrange("p t (g e) -> p t g e", e=EPG),
                    etmp[:, :, 0:NG].unsqueeze(3).to_broadcast([P, NT, NG, EPG]), ALU.add))
            first_of_max(em[:], NE, col[:, 2], col[:, 3], pick[:, 0], etmp[:])
            link(stt(em[:], pick[:, 0], -3e30, em[:], ALU.mult, ALU.add))
            first_of_max(em[:], NE, col[:, 4], col[:, 5], pick[:, 1], etmp[:])
            tt(col[:, 6], col[:, 4], col[:, 2], ALU.subtract).then_inc(pexp_in, 1)
            tt(both[:], pick[:, 0], pick[:, 1], ALU.add).then_inc(both_ready, 1)
            dve.wait_ge(gexp_out, 1)
            link(V.tensor_reduce(out=col[:, 7], in_=gsel[:, 0], axis=AX.X, op=ALU.add))
            link(V.reciprocal(col[:, 7], col[:, 7]))
            dve.wait_ge(pexp_out, 1)
            link(ts(col[:, 8], col[:, 6], 1.0, None, ALU.add))
            link(V.reciprocal(col[:, 8], col[:, 8]))
            link(tt(gates[:, :, 0], col[:, 7], col[:, 8], ALU.mult))
            link(tt(gates[:, :, 1], gates[:, :, 0], col[:, 6], ALU.mult))
            full(dve, "total")
            total = bank[1][:, 0:NT * NE].rearrange("p (t e) -> p t e", e=NE)
            link(V.memset(offs[:, 0, :], 0.0))
            for t in range(NT):
                link(tt(offs[:, t + 1], offs[:, t], total[:, t], ALU.add))
            V.sem_inc(bank_free[1], 1)
            full(dve, "rank")
            link(tt(rank[:], bank[0][:, 0:NT * NE].rearrange("p (t e) -> p t e", e=NE), offs[:, 0:NT], ALU.add))
            V.sem_inc(bank_free[0], 1)
            further, upto_e, shift_e, first_e = ev[:, 0], ev[:, 1], ev[:, 2], ev[:, 3]
            link(tt(over[:], offs[:, NT].unsqueeze(2).to_broadcast([P, NE, 7]),
                    limits[:].unsqueeze(1).to_broadcast([P, NE, 7]), ALU.is_gt))
            link(V.tensor_reduce(out=further, in_=over[:], axis=AX.X, op=ALU.add))
            link(V.tensor_tensor_scan(upto_e, ones[:, 0:NE], further, 0.0, ALU.mult, ALU.add))
            link(tt(shift_e, upto_e, further, ALU.subtract))
            link(tt(shift_e, shift_e, iota_n[:, 0:NE], ALU.subtract))
            link(ts(shift_e, shift_e, float(NE - 1), float(P), ALU.add, ALU.mult))
            link(ts(first_e, iota_n[:, 0:NE], float(P), None, ALU.mult))
            link(ts(etmp[:], rank[:], float(P), None, ALU.is_ge))
            link(tt(etmp[:], etmp[:], shift_e.unsqueeze(1).to_broadcast([P, NT, NE]), ALU.mult))
            link(tt(rank[:], rank[:], etmp[:], ALU.add))
            link(tt(rank[:], rank[:], first_e.unsqueeze(1).to_broadcast([P, NT, NE]), ALU.add))
            for k in range(2):
                link(tt(etmp[:], rank[:], pick[:, k], ALU.mult))
                link(V.tensor_reduce(out=posf[:, 0, k], in_=etmp[:], axis=AX.X, op=ALU.add))
            link(V.tensor_copy(posi[:, 0], posf[:, 0]))
            link(ts(posi[:, 1], posi[:, 0], 7, None, ALU.logical_shift_right))
            link(ts(posi[:, 0], posi[:, 0], P - 1, None, ALU.bitwise_and))
            link(V.tensor_copy(posf[:], posi[:]))
            def spread(a, n):
                return a.rearrange("p k t -> p (k t)").unsqueeze(2).to_broadcast([P, 2 * NT, n])

            def count(n):
                return iota_n[:, 0:n].unsqueeze(1).to_broadcast([P, 2 * NT, n])
            tt(row_of[:], count(P), spread(posf[:, 0], P), ALU.is_equal)
            link(tt(block_of[:], count(NB), spread(posf[:, 1], NB), ALU.is_equal))
            tt(block_of[:], block_of[:], spread(assign_no[:], NB), ALU.mult).then_inc(sel_ready, 1)
            dve.wait_ge(sel_used, 1)
            slots = bank[2][:, 0:NB]
            link(ts(slotv[:, 0], slots, 0.0, float(NO_ROW), ALU.is_equal, ALU.mult))
            link(stt(slotv[:, 1], slots, -1.0, slotv[:, 0], ALU.add, ALU.add))
            V.sem_inc(bank_free[2], 1)
            link(V.tensor_copy(rows_of_block[:, 1], slotv[:, 1]))
            link(ts(rows_of_block[:, 0], rows_of_block[:, 1], 1, None, ALU.logical_shift_right))
            link(tt(ovcmp[:], iota_n[:, 0:MAXOV].unsqueeze(2).to_broadcast([P, MAXOV, NE]),
                    upto_e.unsqueeze(1).to_broadcast([P, MAXOV, NE]), ALU.is_ge))
            link(V.tensor_reduce(out=ovf[:, 0:MAXOV], in_=ovcmp[:], axis=AX.X, op=ALU.add))
            link(ts(ovf[:, 0:MAXOV], ovf[:, 0:MAXOV], float(NE - 1), None, ALU.min))
            link(V.tensor_copy(ovf[:, MAXOV:MAXOV + 1], ev[:, 1, NE - 1:NE]))
            link(V.tensor_copy(meta[:], ovf[:]))

            def copy_rows(which, dst, block, ready):
                V.tensor_copy(dst[:], rows_of_block[:, which, bass.ds(block, 1)]).then_inc(ready, 1)

            def next_gather(b, n, block):
                dve.wait_ge(xg_in[b], 16 * n)
                copy_rows(0, gidx[b], block, gidx_ready)

            def weigh_tokens(i):
                dve.wait_ge(xg_turned, i + 1)
                for half in range(2):
                    w = par[:, 48 + 4 * half:52 + 4 * half].unsqueeze(2).to_broadcast([P, 4, P])
                    last = tt(xw[:, 4 * half:4 * half + 4], bank[half][:].rearrange("p (c n) -> p c n", n=P), w,
                              ALU.mult)
                last.then_inc(xw_ready, 1)

            def tokens_low(b, i):
                dve.wait_ge(xw_ready, i + 1)
                dve.wait_ge(x_hi_ready, i + 1)
                tt(x_lo[b][:], xw[:], x_hi[b][:].bitcast(F32), ALU.subtract).then_inc(x_lo_ready, 1)

            def split_low(j, k):
                dve.wait_ge(hi_ready, 12 * j + k + 1)
                tt(w_lo[k % NSPLIT][:], raw[k % NRAW][:], w_hi[k % NSPLIT][:].bitcast(F32), ALU.subtract)\
                    .then_inc(lo_ready, 1)

            def gate_up(j, k, i):
                dve.wait_ge(gate_ready, i + 1)
                dve.wait_ge(piece_used, 12 * j + k)
                tt(hid[:], gate_act[:], bank[3][:], ALU.mult).then_inc(hid_ready, 1)

            def hidden_low(i):
                dve.wait_ge(hid_hi_ready, i + 1)
                tt(hid_lo[:].rearrange("p f n -> p (f n)"), bank[4][:],
                   hid_hi[:].rearrange("p f n -> p (f n)").bitcast(F32), ALU.subtract).then_inc(hid_lo_ready, 1)

            def scatter_rows(j, b):
                wait_for(dve, y_sent[b], 16 * j)
                copy_rows(1, sidx[b], 2 * j + b, sidx_ready)

            def first_block(j, gather=False):
                i = 2 * j
                weigh_tokens(i)
                tokens_low(0, i)
                split_low(j, 4)
                split_low(j, 5)
                if gather:
                    next_gather(1, j + 1, i + 3)
                weigh_tokens(i + 1)
                tokens_low(1, i + 1)
                split_low(j, 6)
                gate_up(j, 4, i)
                split_low(j, 7)

            def next_block(j, s, gather=False, final=False):
                i, k = 2 * j + 1 + s, 4 + 6 * s
                hidden_low(i - 1)
                split_low(j, k + 4)
                scatter_rows(j, s)
                split_low(j, k + 5)
                split_low(j, k + 6)
                if gather:
                    next_gather(s, j + 2, i + 3)
                if not final:
                    weigh_tokens(i + 1)
                split_low(j, k + 7)
                if not final:
                    tokens_low(s, i + 1)
                    split_low(j, k + 8)
                gate_up(j, k + 6, i)
                if not final:
                    split_low(j, k + 9)

            def last_down(j):
                hidden_low(2 * j + 1)
                scatter_rows(j, 1)

            copy_rows(0, gidx[0], 0, gidx_ready)
            copy_rows(0, gidx[1], 1, gidx_ready)
            next_gather(0, 1, 2)
            first_block(0, gather=True)
            for s in range(2):
                next_block(0, s, gather=True)
            with dve.Fori(1, NE // 2 - 2) as j:
                for s in range(2):
                    next_block(j, s, gather=True)
            for s in range(2):
                next_block(NE // 2 - 2, s)
            next_block(NE // 2 - 1, 0, final=True)
            last_down(NE // 2 - 1)
            count = dve.value_load(meta[0:1, MAXOV:MAXOV + 1], min_val=0, max_val=MAXOV)
            with dve.Fori(0, MAXOV // 2) as o:
                with dve.If(2 * o < count):
                    j = NE // 2 + o
                    for b in range(2):
                        next_gather(b, j, 2 * j + b)
                    for k in range(NSPLIT):
                        split_low(j, k)
                    first_block(j)
                    next_block(j, 0, final=True)
                    last_down(j)

            dve.wait_ge(final_w_in, 16)

            def combine(t):
                dve.wait_ge(y_in[t % NY], 16 * (t // NY + 1))
                link(stt(h[:, t, :], ytile[t % NY][:, 0], gates[:, t, 0:1], h[:, t, :], ALU.mult, ALU.add))
                stt(h[:, t, :], ytile[t % NY][:, 1], gates[:, t, 1:2], h[:, t, :], ALU.mult, ALU.add).then_inc(comb, 1)
            combine(0)
            for t in range(NT):
                if t + 1 < NT:
                    combine(t + 1)
                dve_var(n2, t, stat)
                dve_rstd(n2, t, stat)
                dve.wait_ge(n2.rstd, t + 1)
                dve.wait_ge(comb, t + 1)
                if t >= 2:
                    dve.wait_ge(out_stored[t % 2], 16 * (t // 2))
                stt(otile[t % 2][:], h[:, t, :], stat[:, 2, t:t + 1], fin_w[:], ALU.mult, ALU.mult)\
                    .then_inc(out_ready, 1)


NAMES = ["x", "mem", "norm_mix_w", "w_in", "conv_w", "conv_b", "conv_ln_w", "conv_ln_b",
         "ssm_A_re", "ssm_A_im", "ssm_log_dt", "ssm_B_re", "ssm_B_im", "ssm_C_re", "ssm_C_im",
         "ssm_D", "ssm_glu_w", "w_out", "norm_x_w", "norm_mem_w", "xq_w", "xk_w", "xv_w", "xo_w",
         "norm_ffn_w", "router_group_w", "router_group_b", "router_expert_w", "router_expert_b",
         "moe_w1", "moe_w3", "moe_w2", "final_norm_w"]


def build(nc, shapes):
    args = [nc.dram_tensor(n, shapes[n], F32, kind="ExternalInput").ap() for n in NAMES]
    out = nc.dram_tensor("out", shapes["x"], F32, kind="ExternalOutput").ap()
    hymba_layer(nc, *args, out)


def kernel(**inputs):
    import concourse.bacc as bacc
    from concourse.bass_utils import run_bass_kernel_spmd

    arrays = {n: np.ascontiguousarray(inputs[n]) for n in NAMES}
    nc = bacc.Bacc("TRN2", target_bir_lowering=False, num_devices=1)
    build(nc, {n: a.shape for n, a in arrays.items()})
    result = run_bass_kernel_spmd(nc, [arrays], core_ids=[0])
    return result.results[0]["out"]
```

```python
from contextlib import ExitStack

import numpy as np

import concourse.bass as bass
from concourse import mybir

F32 = mybir.dt.float32
F32R = mybir.dt.float32r
I32 = mybir.dt.int32
ALU = mybir.AluOpType
ACT = mybir.ActivationFunctionType
AX = mybir.AxisListType

P = 128
KB = 1024
BANK = 512
NO_ROW = 1 << 20
ROUND = 12582912.0
LOG2E = 1.4426950408889634
LN2_HI, LN2_LO = 0.693359375, -2.12194440e-4
TWO_PI = 6.283185307179586
TWO_PI_A = 6.28125
TWO_PI_B = round((TWO_PI - TWO_PI_A) * 2.0**21) / 2.0**21
TWO_PI_C = TWO_PI - TWO_PI_A - TWO_PI_B
PI_LOW = 3.1415925


def hymba_layer(nc, x, mem, norm_mix_w, w_in, conv_w, conv_b, conv_ln_w, conv_ln_b,
                A_re, A_im, log_dt, B_re, B_im, C_re, C_im, ssm_D, glu_w, w_out,
                norm_x_w, norm_mem_w, xq_w, xk_w, xv_w, xo_w, norm_ffn_w,
                router_group_w, router_group_b, router_expert_w, router_expert_b,
                moe_w1, moe_w3, moe_w2, final_norm_w, out):
    _, S, D = x.shape
    M = mem.shape[1]
    TAPS, DC = conv_w.shape[1:]
    G, NS, CH = B_re.shape[1:]
    NG = router_group_w.shape[2]
    NE = router_expert_w.shape[2]
    EPG = NE // NG
    F = moe_w1.shape[3]
    EPS = 1e-6
    NT = S // P
    KD = D // P
    KC = DC // P
    KF = F // P
    MT = M // P
    NH = 4
    HD = D // NH
    HK = HD // P
    T = 8
    NC = S // T
    Q4 = KC
    GQ = P // CH
    PQ = GQ // 2
    NP = G // 2
    NR = NG + NE
    MAXOV = 2 * S // P
    NB = NE + MAXOV + 2
    assert CH * T == P and 2 * NS == P and NC == P and S == 2 * BANK and D == 2 * BANK

    u_bounce = nc.dram_tensor("u_bounce", (Q4, GQ, CH, T, NC), F32, kind="Internal").ap()
    y_bounce = nc.dram_tensor("y_bounce", (Q4, GQ, CH, T, NC), F32, kind="Internal").ap()
    xn_rows = nc.dram_tensor("xn_rows", (S, D), F32, kind="Internal").ap()
    y_rows = nc.dram_tensor("y_rows", (2 * S, D), F32, kind="Internal").ap()

    base = (nc.sbuf_base + 63) // 64 * 64

    def sb(name, kb, shape, dt=F32):
        return nc.alloc_sbuf_tensor_at(name, shape, dt, offset=base + int(kb * KB))

    slab = [sb(f"slab{i}", 16 * i, [P, KD, BANK]) for i in range(3)]
    h = sb("h", 48, [P, NT, D])
    uc = [sb(f"uc{i}", 48 + 4 * i, [P, GQ, NC]) for i in range(2)]
    rotated = sb("rotated", 56, [P, 2, PQ, NC])
    scanned = sb("scanned", 60, [P, 2, PQ, NC])
    rot_tmp = sb("rot_tmp", 64, [P, 2, PQ, NC])
    y_chunks = sb("y_chunks", 68, [P, GQ, NC])
    y_feat = sb("y_feat", 72, [P, T, NC])
    shifts = sb("shifts", 76, [P, T, P])
    mem_rows = sb("mem_rows", 68, [P, MT, D])
    xT = sb("xT", 80, [P, KD, S])
    kT = sb("kT", 80, [P, KD, M])
    vT = sb("vT", 88, [P, KD, M])
    memT = sb("memT", 104, [P, KD, M])
    yT = sb("yT", 96, [P, KD, S])
    conv_acc = yT[:, KC:KD, :]
    c_raw = sb("c_raw", 112, [CH, 2, G * NS])
    PAD = TAPS - 1
    conv_in = sb("conv_in", 128, [P, KC, S + PAD])
    squares = sb("squares", 128, [P, 2, KC, BANK])
    u_perm = sb("u_perm", 144.5, [P, Q4, T, NC])
    b_raw = sb("b_raw", 144.5, [P, 2, NP, CH])
    rows_raw = sb("rows_raw", 146.5, [P, P])
    taps_raw = sb("taps_raw", 147, [P, P])
    a_raw = sb("a_raw", 147.5, [NP, 3, P])
    dt_raw = sb("dt_raw", 149, [NP, 2])
    xs0 = [sb(f"xs0_{i}", at_kb, [P, D]) for i, at_kb in enumerate((150, 154, 164.5, 168.5))]
    lift = [sb("lift0", 160.5, [P, 2, PQ, P]), sb("lift1", 32, [P, 2, PQ, P])]
    toep = [sb("toep0", 164.5, [P, GQ, P]), sb("toep1", 36, [P, GQ, P])]
    readout = [sb("readout0", 168.5, [P, 2, PQ, P]), sb("readout1", 40, [P, 2, PQ, P])]
    phase = [sb("phase0", 172.5, [P, 2, PQ, NC]), sb("phase1", 44, [P, 2, PQ, NC])]
    bpow = sb("bpow", 176.5, [P, 2, PQ, P])
    kern = sb("kern", 180.5, [P, GQ, CH])
    glu_sig = sb("glu_sig", 181, [P, BANK])
    conv_a = sb("conv_a", 183, [P, BANK])
    conv_sg = sb("conv_sg", 185, [P, BANK])
    states = sb("states", 187, [P, 2, PQ, NC + 1])
    pool_tmp = sb("pool_tmp", 191.25, [P, 4, PQ * CH * 4])
    at = [195.25]

    def small(name, shape, dt=F32):
        n = int(np.prod(shape[1:])) * 4
        t = sb(name, at[0], shape, dt)
        at[0] += (n + 31) // 32 * 32 / KB
        assert base + at[0] * KB <= nc.sbuf_usable_end, (name, at[0])
        return t

    ident = small("ident", [P, P])
    means = small("means", [P, P])
    par = small("par", [P, 5 * KD + 4 * KC])
    taps = small("taps", [P, TAPS * KC])
    ct = small("ct", [P, 2, NP, CH])
    bbar = small("bbar", [P, 2, NP, CH])
    pw = small("pw", [P, 2, 3, NP])
    ph = small("ph", [P, 2, 7, NP])
    rho = small("rho", [P, NP])
    t16 = small("t16", [P, 12, NP])
    stat = small("stat", [P, 3, NT])
    stat_m = small("stat_m", [P, 3, MT])
    pool_mark = small("pool_mark", [P, 1])
    wout_lo = [sb(f"wout_lo{i}", 16 * i, [P, KD, BANK], F32R) for i in range(2)]
    wout_hi = [sb(f"wout_hi{i}", 128 + 16 * i, [P, KD, BANK], F32R) for i in range(2)]
    y_hi = [sb(f"y_hi{i}", 160 + 8 * i, [P, KD, P], F32R) for i in range(2)]
    y_lo = [sb(f"y_lo{i}", 164 + 8 * i, [P, KD, P], F32R) for i in range(2)]
    NROWS = 3
    w_rows = [sb(f"w_rows{i}", 32 + 4 * i, [P, D]) for i in range(NROWS)]
    wqT = [sb(f"wqT{i}", at_kb, [P, KD, P]) for i, at_kb in enumerate((44, 196.5))]
    key_hi = sb("key_hi", 128, [P, KD, NH * M], F32R)
    key_lo = sb("key_lo", 160, [P, KD, NH * M], F32R)
    value_hi = sb("value_hi", 0, [P, NH * MT, D], F32R)
    value_lo = sb("value_lo", 96, [P, NH * MT, D], F32R)
    wo_rows = [sb(f"wo_rows{i}", 96 + 4 * (i + 2), [P, D]) if i < KD - 2 else w_rows[(KD + i) % NROWS]
               for i in range(KD)]
    hT_hi = sb("hT_hi", 80, [P, KD, P], F32R)
    hT_lo = sb("hT_lo", 84, [P, KD, P], F32R)
    x1s = sb("x1s", 44, [P, D])
    pT_hi = sb("pT_hi", 32, [P, NH * MT, P], F32R)
    pT_lo = sb("pT_lo", 36, [P, NH * MT, P], F32R)
    xs = [sb("xs0", 40, [P, D]), sb("xs1", 88, [P, D])]
    fT = sb("fT", 92, [P, KD, P])
    probs = sb("probs", 196.5, [P, NH, M])
    glu_lhs = sb("glu_lhs", 203.25, [P, Q4, 2, P])
    assert base + 207.25 * KB <= nc.sbuf_usable_end and at[0] <= 203.25, at[0]

    junk_x = sb("junk_x", 128, [P, D])
    junk_m = sb("junk_m", 56, [P, D])
    junk = sb("junk", 192.75, [P, D], mybir.dt.bfloat16)
    ln_var = sb("ln_var", 183, [P, 2, BANK])
    negmax = sb("negmax", 194.75, [P, 2, NH])
    expsum = sb("expsum", 194.8125, [P, 2, NH])
    logits = sb("logits", 203.25, [P, NT, NR])
    router_w = sb("router_w", 204.5, [P, KD, NR])
    router_b = sb("router_b", 205.75, [P, NR])
    at[0] = 160.5

    def late(name, shape, dt=F32):
        n = int(np.prod(shape[1:])) * 4
        t = sb(name, at[0], shape, dt)
        at[0] += (n + 31) // 32 * 32 / KB
        assert at[0] <= 195.25, name
        return t

    upper = late("upper", [P, P])
    ones = late("ones", [P, P])
    iota_n = late("iota_n", [P, P])
    assign_no = late("assign_no", [P, 2, NT])
    limits = late("limits", [P, 7])
    lg = late("lg", [P, NT, NR])
    col = late("col", [P, 12, NT])
    gsel = late("gsel", [P, 2, NT, NG])
    em = late("em", [P, NT, NE])
    etmp = late("etmp", [P, NT, NE])
    pick = late("pick", [P, 2, NT, NE])
    both = late("both", [P, NT, NE])
    offs = late("offs", [P, NT + 1, NE])
    rank = late("rank", [P, NT, NE])
    over = late("over", [P, NE, 7])
    ev = late("ev", [P, 5, NE])
    posi = late("posi", [P, 2, 2, NT], I32)
    posf = late("posf", [P, 2, 2, NT])
    row_of = sb("row_of", 176, [P, 2 * NT, P], F32R)
    block_of = sb("block_of", 188, [P, 2 * NT, NB], F32R)
    slotv = late("slotv", [P, 2, NB])
    ovcmp = late("ovcmp", [P, MAXOV, NE])
    ovf = late("ovf", [P, MAXOV + 1])
    assert at[0] <= 176
    at[0] = 192
    gates = late("gates", [P, NT, 2])
    rows_of_block = late("rows_of_block", [P, 2, NB], I32)
    meta = late("meta", [P, MAXOV + 1], I32)
    gidx = [late(f"gidx{i}", [P, 1], I32) for i in range(2)]
    sidx = [late(f"sidx{i}", [P, 1], I32) for i in range(2)]
    fin_w = sb("fin_w", 203.25, [P, D])
    NRAW, NSPLIT = 6, 4
    HALF = KD // 2
    raw = [sb(f"raw{i}", 8 * i, [P, HALF, F]) for i in range(NRAW)]
    SPLIT_AT = (128, 144, 96, 112)
    w_hi = [sb(f"w_hi{i}", at_kb, [P, HALF, F], F32R) for i, at_kb in enumerate(SPLIT_AT)]
    w_lo = [sb(f"w_lo{i}", at_kb + 8, [P, HALF, F], F32R) for i, at_kb in enumerate(SPLIT_AT)]
    xg = [sb(f"xg{i}", 80 + 4 * i, [P, D]) for i in range(2)]
    xw = sb("xw", 88, [P, KD, P])
    x_hi = [sb(f"x_hi{i}", 160 + 8 * i, [P, KD, P], F32R) for i in range(2)]
    x_lo = [sb(f"x_lo{i}", 164 + 8 * i, [P, KD, P], F32R) for i in range(2)]
    gate_act = sb("gate_act", 176, [P, F])
    hid = sb("hid", 178, [P, F])
    hid_hi = sb("hid_hi", 180, [P, KF, P], F32R)
    hid_lo = sb("hid_lo", 182, [P, KF, P], F32R)
    yb = [sb("yb0", 184, [P, D]), sb("yb1", 92, [P, D])]
    NY = 4
    ytile = [sb(f"ytile{i}", 80 + 8 * i, [P, 2, D]) for i in range(NY)]
    otile = [sb(f"otile{t}", 112 + 4 * t, [P, D]) for t in range(NT)]
    junk_f = sb("junk_f", 144, [P, D])

    bank = [nc.alloc_psum_tensor(f"bank{i}", [P, BANK], F32) for i in range(8)]

    def sem(name):
        return nc.alloc_semaphore(name)

    bank_full = [sem(f"bank_full{i}") for i in range(8)]
    bank_free = [sem(f"bank_free{i}") for i in range(8)]
    bank_uses = [0] * 8
    use_of = {}

    consts_ready = sem("consts_ready")
    pool_step = sem("pool_step")
    dve_step = sem("dve_step")
    act_step = sem("act_step")
    params_in = sem("params_in")
    poles_in = sem("poles_in")
    late_params_in = sem("late_params_in")
    braw_in = sem("braw_in")
    glu_in = sem("glu_in")
    x_in = [sem(f"x_in{t}") for t in range(NT)]
    mem_in = sem("mem_in")
    slab_in = [sem(f"slab_in{i}") for i in range(3)]
    setup_ready = sem("setup_ready")
    trig_in = sem("trig_in")
    trig_out = sem("trig_out")
    conv_a_ready = sem("conv_a_ready")
    conv_sg_ready = sem("conv_sg_ready")
    v_ready = sem("v_ready")
    conv_done = sem("conv_done")
    u_ready = sem("u_ready")
    ub_out = sem("ub_out")
    uc_in = [sem("uc_in0"), sem("uc_in1")]
    memT_ready = sem("memT_ready")
    bpow_ready = sem("bpow_ready")
    readout_ready = sem("readout_ready")
    phase_ready = sem("phase_ready")
    lift_ready = sem("lift_ready")
    kern_ready = sem("kern_ready")
    toep_ready = sem("toep_ready")
    shifts_ready = sem("shifts_ready")
    states_ready = sem("states_ready")
    ychunk_ready = sem("ychunk_ready")
    yb_out = sem("yb_out")
    yf_in = sem("yf_in")
    dterm_done = sem("dterm_done")
    gelu_done = sem("gelu_done")
    glu_sig_ready = sem("glu_sig_ready")
    yssm_ready = sem("yssm_ready")
    kv_ready = sem("kv_ready")
    centered = sem("centered")
    squared = sem("squared")
    ln_v = sem("ln_v")
    ln_root = sem("ln_root")
    ln_scaled = sem("ln_scaled")
    yconv_ready = sem("yconv_ready")
    h1_ready = sem("h1_ready")
    wqT_ready = sem("wqT_ready")
    y_hi_ready = sem("y_hi_ready")
    y_lo_ready = sem("y_lo_ready")
    table_hi_ready = sem("table_hi_ready")
    table_lo_ready = sem("table_lo_ready")
    hT_hi_ready = sem("hT_hi_ready")
    hT_lo_ready = sem("hT_lo_ready")
    negmax_ready = sem("negmax_ready")
    exp_done = sem("exp_done")
    probs_ready = sem("probs_ready")
    pT_hi_ready = sem("pT_hi_ready")
    pT_lo_ready = sem("pT_lo_ready")
    h2_ready = sem("h2_ready")
    router_in = sem("router_in")
    xn_out = [sem("xn_out0"), sem("xn_out1")]
    logit_ready = sem("logit_ready")
    route_consts = sem("route_consts")
    rexp_in = sem("rexp_in")
    rexp_out = sem("rexp_out")
    both_ready = sem("both_ready")
    sel_ready = sem("sel_ready")
    sel_used = sem("sel_used")

    class Norm:

        def __init__(self, name, *more):
            self.squares, self.var, self.root, self.rstd = (
                sem(f"{name}_{x}") for x in ("squares", "var", "root", "rstd"))
            if "scaled" in more:
                self.scaled = sem(f"{name}_scaled")
            if "stored" in more:
                self.stored = sem(f"{name}_stored")

    nx, nf = (Norm(n, "scaled", "stored") for n in ("nx", "nf"))
    nm, n1 = (Norm(n, "scaled") for n in ("nm", "n1"))
    n2 = Norm("n2", "scaled")
    raw_in = [sem(f"raw_in{i}") for i in range(6)]
    hi_ready = sem("hi_ready")
    lo_ready = sem("lo_ready")
    piece_used = sem("piece_used")
    xg_in = [sem("xg_in0"), sem("xg_in1")]
    y_sent = [sem("y_sent0"), sem("y_sent1")]
    gidx_ready = sem("gidx_ready")
    sidx_ready = sem("sidx_ready")
    xg_turned = sem("xg_turned")
    xw_ready = sem("xw_ready")
    x_hi_ready = sem("x_hi_ready")
    x_lo_ready = sem("x_lo_ready")
    gate_ready = sem("gate_ready")
    hid_ready = sem("hid_ready")
    hid_turned = sem("hid_turned")
    hid_hi_ready = sem("hid_hi_ready")
    hid_lo_ready = sem("hid_lo_ready")
    yb_ready = sem("yb_ready")
    final_w_in = sem("final_w_in")
    over_done = sem("over_done")
    rows_moved = sem("rows_moved")
    y_in = [sem(f"y_in{i}") for i in range(NY)]
    comb = sem("comb")
    out_ready = sem("out_ready")
    out_stored = sem("out_stored")

    def full(eng, key):
        b, n = use_of[key]
        eng.wait_ge(bank_full[b], n)
        return bank[b]

    def wait_for(eng, s, n):
        if not (isinstance(n, int) and n <= 0):
            eng.wait_ge(s, n)

    def run_further(eng, further, pair):
        with eng.If(0 < further):
            pair(0)
        with eng.If(2 < further):
            with eng.Fori(1, MAXOV // 2) as o:
                with eng.If(2 * o < further):
                    pair(o)

    def linker(eng, step):
        count = [0]

        def link(ins):
            count[0] += 1
            ins.then_inc(step, 1)
            eng.wait_ge(step, count[0])
        return link

    def col_major(w, c0, n):
        return w[:, c0:c0 + n].rearrange("(c p) n -> p c n", p=P)

    slabs = [(w_in[0], 0, 0, None), (w_in[0], BANK, 1, None), (w_in[0], 2 * BANK, 2, None),
             (xk_w[0], 0, 0, ("g", KC - 1, 1)), (xk_w[0], BANK, 1, ("g", KC - 1, 1)),
             (xv_w[0], 0, 0, ("kv", 1)), (xv_w[0], BANK, 1, ("kv", 5)),
             (w_out[0], 0, 0, ("kv", 9)), (w_out[0], BANK, 1, ("kv", 13))]

    def rows_loaded(eng, r):
        place = r % NROWS
        eng.wait_ge(slab_in[place], 16 * (sum(w[2] == place for w in slabs) + r // NROWS + 1))

    def slab_loaded(eng, n):
        place = slabs[n][2]
        eng.wait_ge(slab_in[place], 16 * sum(w[2] == place for w in slabs[:n + 1]))

    NQ = Q4
    PAIRS = range(PQ)

    with nc.Block() as block:

        @block.tensor
        def _(pe):
            def take(*banks):
                for b in banks:
                    if bank_uses[b]:
                        pe.wait_ge(bank_free[b], bank_uses[b])

            def give(b, ins, key):
                bank_uses[b] += 1
                use_of[key] = (b, bank_uses[b])
                ins.then_inc(bank_full[b], 1)

            def turn(out, src, n=P):
                return nc.tensor.transpose(out, src, ident[0:n, 0:n])

            pe.wait_ge(consts_ready, 1)
            pe.wait_ge(params_in, 16 * 9)
            give(0, turn(bank[0][:, 0:48], rows_raw[0:48, :], 48), "par")
            give(1, turn(bank[1][:, 0:TAPS * KC], taps_raw[0:TAPS * KC, :], TAPS * KC), "taps")
            def turn_rows(norm, src, t, banks, key):
                pe.wait_ge(norm.scaled, t + 1)
                take(*banks)
                for c in range(KD):
                    last = turn(bank[banks[c // 4]][:, (c % 4) * P:(c % 4 + 1) * P], src[:, c * P:(c + 1) * P])
                    if c == 3:
                        give(banks[0], last, (key, t, 0))
                bank_uses[banks[1]] += 1
                use_of[(key, t, 1)] = (banks[1], bank_uses[banks[1]])
                last.then_inc(bank_full[banks[1]], 1)

            for t in range(NT):
                turn_rows(nx, xs0[t % 4], t, (4, 5) if t % 2 else (6, 7), "x")

            pe.wait_ge(poles_in, 16 * 3)
            pe.wait_ge(consts_ready, 3)
            for i in range(3):
                last = turn(bank[2][:, i * NP:(i + 1) * NP], a_raw[:, i, :], NP)
            give(2, last, "a_raw")
            pe.wait_ge(late_params_in, 16 * 3)
            for ri in range(2):
                for p in range(NP):
                    o = (ri * NP + p) * CH
                    last = turn(bank[3][:, o:o + CH], c_raw[:, ri, p * P:(p + 1) * P], CH)
            give(3, last, "c_raw")

            for n in range(2):
                slab_loaded(pe, n)
            for i in range(KC):
                for half in range(2):
                    if i == 0:
                        pe.wait_ge(nx.stored, (half + 1) * NT // 2)
                    for w, b in ((0, half), (1, 2 + half)):
                        take(b)
                        for k in range(KD):
                            last = nc.tensor.matmul(bank[b][:], slab[w][:, k, i * P:(i + 1) * P],
                                                    xT[:, k, half * BANK:(half + 1) * BANK],
                                                    start=(k == 0), stop=(k == KD - 1))
                        give(b, last, ("ag"[w], i, half))
            slab_loaded(pe, 2)
            for i in range(KC):
                for half in range(2):
                    b = 4 + half
                    take(b)
                    for k in range(KD):
                        last = nc.tensor.matmul(bank[b][:], slab[2][:, k, i * P:(i + 1) * P],
                                                xT[:, k, half * BANK:(half + 1) * BANK],
                                                start=(k == 0), stop=(k == KD - 1))
                    give(b, last, ("u", i, half))
            for t in range(MT):
                turn_rows(nm, mem_rows[:, t, :], t, (6, 7), "m")

            def setup(q):
                pe.wait_ge(bpow_ready, q + 1)
                for ri in range(2):
                    take(ri)
                    for p in PAIRS:
                        last = turn(bank[ri][:, p * P:(p + 1) * P], bpow[:, ri, p, :])
                    give(ri, last, ("lift", q, ri))
                for g2 in range(2):
                    take(g2)
                    rows = slice(g2 * NS, (g2 + 1) * NS)
                    for p in PAIRS:
                        for ri in range(2):
                            last = nc.tensor.matmul(bank[g2][:, p * CH:(p + 1) * CH], bpow[rows, ri, p, :],
                                                    ct[rows, ri, q * PQ + p, :], start=(ri == 0), stop=(ri == 1))
                    give(g2, last, ("kern", q, g2))
                pe.wait_ge(kern_ready, 2 * q + 2)
                if q == 0:
                    pe.wait_ge(shifts_ready, 1)
                for jh in range(2):
                    take(jh)
                    for j in range(4):
                        last = nc.tensor.matmul(bank[jh][:, j * P:(j + 1) * P], shifts[:, 7 - 4 * jh - j, :],
                                                kern[:].rearrange("p g o -> p (g o)"), start=True, stop=True)
                    give(jh, last, ("toep", q, jh))

            def chunk_inputs(q):
                pe.wait_ge(uc_in[q % 2], 16 * (q // 2 + 1))
                pe.wait_ge(lift_ready, 2 * q + 2)
                for ri in range(2):
                    take(6 + ri)
                    for p in PAIRS:
                        for g2 in range(2):
                            last = nc.tensor.matmul(
                                bank[6 + ri][g2 * NS:(g2 + 1) * NS, p * NC:(p + 1) * NC],
                                lift[q % 2][:, ri, p, g2 * NS:(g2 + 1) * NS], uc[q % 2][:, 2 * p + g2, :],
                                start=True, stop=True)
                    give(6 + ri, last, ("S", q, ri))

            def chunk_outputs(q):
                pe.wait_ge(toep_ready, 2 * q + 2)
                pe.wait_ge(readout_ready, q + 1)
                pe.wait_ge(states_ready, q + 1)
                take(4, 5)
                for p in PAIRS:
                    for g2 in range(2):
                        nc.tensor.matmul(bank[4 + g2][:, p * NC:(p + 1) * NC], toep[q % 2][:, 2 * p + g2, :],
                                         uc[q % 2][:, 2 * p + g2, :], start=True, stop=False)
                    for ri in range(2):
                        for g2 in range(2):
                            rows = slice(g2 * NS, (g2 + 1) * NS)
                            last = nc.tensor.matmul(bank[4 + g2][:, p * NC:(p + 1) * NC],
                                                    readout[q % 2][rows, ri, p, :], states[rows, ri, p, 0:NC],
                                                    start=False, stop=(ri == 1))
                            if p == PQ - 1 and ri == 1 and g2 == 0:
                                give(4, last, ("y", q, 0))
                give(5, last, ("y", q, 1))

            def kv_piece(n, tiles):
                slab_loaded(pe, 3 + n)
                w = slab[slabs[3 + n][2]]
                if n == 0:
                    pe.wait_ge(memT_ready, MT * KD)
                for m in tiles:
                    take(m)
                    for k in range(KD):
                        last = nc.tensor.matmul(bank[m][:, 0:M], w[:, k, m * P:(m + 1) * P], memT[:, k, :],
                                                start=(k == 0), stop=(k == KD - 1))
                    give(m, last, ("kv", 4 * n + m))

            def glu(q, halves=range(2)):
                pe.wait_ge(gelu_done, q + 1)
                if q == 0:
                    pe.wait_ge(glu_in, 16 * 2 * GQ)
                for jh in halves:
                    for e in range(2):
                        b = (4 if q == NQ - 1 else 2, 6)[jh] + e
                        take(b)
                        last = nc.tensor.matmul(bank[b][:], glu_lhs[:, q, e, :],
                                                y_feat[:, 4 * jh:4 * jh + 4, :].rearrange("p j c -> p (j c)"),
                                                start=True, stop=True)
                        give(b, last, ("glu", q, jh, e))

            def channel_means(src, ready, key):
                for half in range(2):
                    pe.wait_ge(ready, half + 1 if ready is not conv_done else KC)
                    take(2 + half)
                    for k in range(KC):
                        last = nc.tensor.matmul(bank[2 + half][:], means[:], src(k, half),
                                                start=(k == 0), stop=(k == KC - 1))
                    give(2 + half, last, (key, half))

            setup(0)
            for q in range(NQ):
                chunk_inputs(q)
                kv_piece(q, (0, 2, 3))
                chunk_outputs(q)
                if q == NQ - 1:
                    kv_piece(q, (1,))
                    glu(q - 1)
                else:
                    if q > 0:
                        glu(q - 1, (0,))
                    kv_piece(q, (1,))
                    if q > 0:
                        glu(q - 1, (1,))
                if q + 1 < NQ:
                    setup(q + 1)
                if q == 0:
                    channel_means(lambda k, half: conv_acc[:, k, half * BANK:(half + 1) * BANK], conv_done, "mean")
                if q == 1:
                    channel_means(lambda k, half: squares[:, half, k, :], squared, "lnvar")
            def split_product(out, a_hi, a_lo, b_hi, b_lo, first, final):
                nc.tensor.matmul(out, a_hi, b_hi, start=first, stop=False)
                nc.tensor.matmul(out, a_hi, b_lo, start=False, stop=False)
                return nc.tensor.matmul(out, a_lo, b_hi, start=False, stop=final)

            def project(t, half, part):
                b = 2 * (t % 2) + half
                if part == 0:
                    take(b)
                for k in range(KC):
                    feat = k + KC if part == 0 else k
                    last = split_product(bank[b][:], y_hi[t % 2][:, feat, :], y_lo[t % 2][:, feat, :],
                                         wout_hi[half][:, k + KC * part, :], wout_lo[half][:, k + KC * part, :],
                                         part == 0 and k == 0, part == 1 and k == KC - 1)
                if part == 1:
                    give(b, last, ("h1", t, half))

            for n in range(2):
                for ready in (table_hi_ready, table_lo_ready):
                    pe.wait_ge(ready, 2)
                for ready in (y_hi_ready, y_lo_ready):
                    pe.wait_ge(ready, n + 1)
                project(n, 0, 0)
            glu(NQ - 1)

            def turn_query_rows(i):
                rows_loaded(pe, i)
                take(4, 5)
                for c in range(KD):
                    last = turn(bank[4 + c // 4][:, (c % 4) * P:(c % 4 + 1) * P], w_rows[i % NROWS][:, c * P:(c + 1) * P])
                    if c % 4 == 3:
                        give(4 + c // 4, last, ("wqT", i, c // 4))

            def key_products(i):
                pe.wait_ge(wqT_ready, 2 * i + 2)
                if i == 0:
                    pe.wait_ge(kv_ready, 16)
                for b in range(2):
                    take(6 + b)
                    for hd in (2 * b, 2 * b + 1):
                        for k in range(HK):
                            last = nc.tensor.matmul(bank[6 + b][:, (hd % 2) * M:(hd % 2 + 1) * M],
                                                    wqT[i % 2][:, HK * hd + k, :], kT[:, HK * hd + k, :],
                                                    start=(k == 0), stop=(k == HK - 1))
                    give(6 + b, last, ("key", i, b))

            for t0 in range(0, NT, 2):
                for half in range(2):
                    if t0 == 0 and half == 1:
                        pe.wait_ge(table_hi_ready, 4)
                        pe.wait_ge(table_lo_ready, 4)
                    for t in (t0, t0 + 1):
                        pe.wait_ge(y_hi_ready, t + 3)
                        pe.wait_ge(y_lo_ready, t + 3)
                        if t0 > 0 or half > 0:
                            project(t, half, 0)
                        project(t, half, 1)

            turn_query_rows(0)
            for i in range(KD):
                if i + 1 < KD:
                    turn_query_rows(i + 1)
                key_products(i)

            turn_rows(n1, x1s, 0, (6, 7), "h1T")
            for n in range(NH * MT):
                hd, mt = n // MT, n % MT
                for half in range(2):
                    b = 2 * (n % 2) + half
                    take(b)
                    for k in range(HK):
                        r = KD + HK * hd + k
                        if mt == 0 and half == 0:
                            rows_loaded(pe, r)
                        last = nc.tensor.matmul(bank[b][:], vT[:, HK * hd + k, mt * P:(mt + 1) * P],
                                                wo_rows[r - KD][:, half * BANK:(half + 1) * BANK],
                                                start=(k == 0), stop=(k == HK - 1))
                    give(b, last, ("value", n, half))

            pe.wait_ge(table_hi_ready, 4 + 2 * KD)
            pe.wait_ge(table_lo_ready, 4 + 2 * KD)
            for s in range(NT + 2):
                if s < NT:
                    pe.wait_ge(hT_hi_ready, 2 * s + 2)
                    pe.wait_ge(hT_lo_ready, 2 * s + 2)
                    for b in range(2):
                        take(b)
                        for k in range(KD):
                            cols = slice(b * BANK, (b + 1) * BANK)
                            last = split_product(bank[b][:], hT_hi[:, k, :], hT_lo[:, k, :],
                                                 key_hi[:, k, cols], key_lo[:, k, cols], k == 0, k == KD - 1)
                        give(b, last, ("s", s, b))
                if s + 1 < NT:
                    turn_rows(n1, x1s, s + 1, (6, 7), "h1T")
                t = s - 2
                if 0 <= t:
                    turn_rows(nf, xs[t % 2], t, (4, 5), "h2T")
                t = s - 1
                if 0 <= t < NT:
                    pe.wait_ge(pT_hi_ready, 2 * t + 2)
                    pe.wait_ge(pT_lo_ready, 2 * t + 2)
                    if t == 0:
                        pe.wait_ge(table_hi_ready, 4 + 4 * KD)
                        pe.wait_ge(table_lo_ready, 4 + 4 * KD)
                    for half in range(2):
                        take(2 + half)
                        for i in range(NH * MT):
                            cols = slice(half * BANK, (half + 1) * BANK)
                            last = split_product(bank[2 + half][:], pT_hi[:, i, :], pT_lo[:, i, :],
                                                 value_hi[:, i, cols], value_lo[:, i, cols],
                                                 i == 0, i == NH * MT - 1)
                        give(2 + half, last, ("h2", t, half))
                t = s - 2
                if 0 <= t:
                    pe.wait_ge(nf.stored, t + 1)
                    pe.wait_ge(router_in, 16 * 4)
                    take(4)
                    for k in range(KD):
                        last = nc.tensor.matmul(bank[4][:, 0:NR], fT[:, k, :], router_w[:, k, :],
                                                start=(k == 0), stop=(k == KD - 1))
                    give(4, last, ("router", t))
                if s < NT:
                    pe.wait_ge(probs_ready, s + 1)
                    for b in range(2):
                        take(6 + b)
                        for i in range(4):
                            hd, mt = 2 * b + i // 2, i % 2
                            last = turn(bank[6 + b][:, i * P:(i + 1) * P], probs[:, hd, mt * P:(mt + 1) * P])
                        give(6 + b, last, ("pT", s, b))

            pe.wait_ge(both_ready, 1)
            pe.wait_ge(route_consts, 5)
            take(0, 1)
            mask = both[:].rearrange("p t e -> p (t e)")
            give(0, nc.tensor.matmul(bank[0][:, 0:NT * NE], upper[:], mask, start=True, stop=True), "rank")
            give(1, nc.tensor.matmul(bank[1][:, 0:NT * NE], ones[:], mask, start=True, stop=True), "total")
            take(2)
            for i in range(2 * NT):
                if i % NT == 0:
                    pe.wait_ge(sel_ready, i // NT + 1)
                last = nc.tensor.matmul(bank[2][:, 0:NB], row_of[:, i, :], block_of[:, i, :],
                                        start=(i == 0), stop=(i == 2 * NT - 1))
            last.then_inc(sel_used, 1)
            bank_uses[2] += 1
            take(*range(8))

            def turn_tokens(b, n, i):
                pe.wait_ge(xg_in[b], 16 * n)
                wait_for(pe, xw_ready, i)
                for c in range(KD):
                    last = turn(bank[c // 4][:, (c % 4) * P:(c % 4 + 1) * P], xg[b][:, c:D:KD])
                last.then_inc(xg_turned, 1)

            def piece_ready(j, k):
                pe.wait_ge(hi_ready, 12 * j + k + 1)
                pe.wait_ge(lo_ready, 12 * j + k + 1)
                return w_hi[k % NSPLIT], w_lo[k % NSPLIT]

            def up(j, k, b, out, half):
                hi, lo = piece_ready(j, k)
                for c in range(HALF):
                    d = half * HALF + c
                    last = split_product(out, x_hi[b][:, d, :], x_lo[b][:, d, :], hi[:, c, :], lo[:, c, :],
                                         d == 0, d == KD - 1)
                last.then_inc(piece_used, 1)

            def turn_hidden(i):
                pe.wait_ge(hid_ready, i + 1)
                for f in range(KF):
                    last = turn(bank[4][:, f * P:(f + 1) * P], hid[:, f:F:KF])
                last.then_inc(hid_turned, 1)

            def down(j, k, i):
                pe.wait_ge(hid_hi_ready, i + 1)
                pe.wait_ge(hid_lo_ready, i + 1)
                wait_for(pe, yb_ready, i)
                for part in range(2):
                    hi, lo = (w[:].rearrange("p c n -> p (c n)").rearrange("p (f d) -> p f d", d=D)
                              for w in piece_ready(j, k + part))
                    for f in range(KF // 2):
                        g = part * (KF // 2) + f
                        for half in range(2):
                            cols = slice(half * BANK, (half + 1) * BANK)
                            last = split_product(bank[5 + half][:], hid_hi[:, g, :], hid_lo[:, g, :],
                                                 hi[:, f, cols], lo[:, f, cols], g == 0, g == KF - 1)
                    last.then_inc(piece_used, 1)

            def tokens_ready(i):
                pe.wait_ge(x_hi_ready, i + 1)
                pe.wait_ge(x_lo_ready, i + 1)
                wait_for(pe, gate_ready, i)

            def first_block(j):
                tokens_ready(2 * j)
                up(j, 0, 0, bank[2][:], 0)
                up(j, 1, 0, bank[2][:], 1)
                turn_tokens(1, j + 1, 2 * j + 1)
                wait_for(pe, hid_ready, 2 * j)
                up(j, 2, 0, bank[3][:], 0)
                up(j, 3, 0, bank[3][:], 1)

            def next_block(j, s, final=False):
                i, b, k = 2 * j + 1 + s, 1 - s, 4 + 6 * s
                tokens_ready(i)
                up(j, k, b, bank[2][:], 0)
                turn_hidden(i - 1)
                up(j, k + 1, b, bank[2][:], 1)
                down(j, k + 2, i - 1)
                if not final:
                    turn_tokens(s, j + 2, i + 1)
                up(j, k + 4, b, bank[3][:], 0)
                up(j, k + 5, b, bank[3][:], 1)

            def last_down(j):
                turn_hidden(2 * j + 1)
                down(j, 10, 2 * j + 1)

            turn_tokens(0, 1, 0)
            first_block(0)
            for s in range(2):
                next_block(0, s)
            with pe.Fori(1, NE // 2 - 1) as j:
                for s in range(2):
                    next_block(j, s)
            next_block(NE // 2 - 1, 0, final=True)
            last_down(NE // 2 - 1)

            further = pe.value_load(meta[0:1, MAXOV:MAXOV + 1], min_val=0, max_val=MAXOV)

            def further_pair(o):
                turn_tokens(0, NE // 2 + o + 1, NE + 2 * o)
                first_block(NE // 2 + o)
                next_block(NE // 2 + o, 0, final=True)
                last_down(NE // 2 + o)
            run_further(pe, further, further_pair)

        @block.sync
        def _(sp):
            def load_slab(n):
                w, c0, place, after = slabs[n]
                if after:
                    full(sp, after)
                sp.dma_start(slab[place][:], col_major(w, c0, BANK)).then_inc(slab_in[place], 16)

            x_rows = x[0].rearrange("(t p) d -> t p d", p=P)
            for t in range(NT):
                sp.dma_start(h[:, t, :], x_rows[t]).then_inc(x_in[t], 16)
            sp.dma_start(a_raw[:, 0, :], A_re[0].rearrange("(n g) p -> n (g p)", g=2)).then_inc(poles_in, 16)
            sp.dma_start(a_raw[:, 1, :], A_im[0].rearrange("(n g) p -> n (g p)", g=2)).then_inc(poles_in, 16)
            sp.dma_start(dt_raw[:], log_dt[0].rearrange("(n g) -> n g", g=2)).then_inc(poles_in, 16)
            sp.wait_ge(params_in, 16 * 9)
            load_slab(0)
            load_slab(1)
            sp.dma_start(c_raw[:, 0, :].rearrange("h (g p) -> h g p", p=NS),
                         C_re[0].rearrange("g h p -> h g p")).then_inc(late_params_in, 16)
            sp.dma_start(c_raw[:, 1, :].rearrange("h (g p) -> h g p", p=NS),
                         C_im[0].rearrange("g h p -> h g p")).then_inc(late_params_in, 16)
            sp.dma_start(par[:, 48:56], norm_ffn_w[0].rearrange("(p c) -> p c", p=P)).then_inc(late_params_in, 16)
            load_slab(2)
            sp.wait_ge(nx.scaled, 7)
            sp.dma_start(mem_rows[:], mem[0].rearrange("(t p) d -> p t d", p=P)).then_inc(mem_in, 16)
            load_slab(3)
            load_slab(4)
            for q in range(NQ):
                sp.wait_ge(u_ready, 2 * q + 2)
                sp.dma_start(u_bounce[q].rearrange("g h j c -> (g h) (j c)"),
                             u_perm[:, q].rearrange("p j c -> p (j c)")).then_inc(ub_out, 16)
                sp.wait_ge(ub_out, 16 * q + 16)
                if q < 2:
                    sp.dma_start(uc[q][:], u_bounce[q].rearrange("g h j c -> (h j) g c")).then_inc(uc_in[q], 16)
            load_slab(5)
            for q in range(NQ):
                sp.wait_ge(ychunk_ready, 2 * q + 2)
                sp.dma_start(y_bounce[q].rearrange("g h j c -> (h j) g c"), y_chunks[:]).then_inc(yb_out, 16)
                sp.wait_ge(yb_out, 16 * q + 16)
                if q > 0:
                    full(sp, ("glu", q - 1, 1, 1))
                if q == 0:
                    full(sp, ("m", 1, 1))
                sp.dma_start(y_feat[:].rearrange("p j c -> p (j c)"),
                             y_bounce[q].rearrange("g h j c -> (g h) (j c)")).then_inc(yf_in, 16)
                if q + 2 < NQ:
                    full(sp, ("y", q, 1))
                    sp.dma_start(uc[q % 2][:], u_bounce[q + 2].rearrange("g h j c -> (h j) g c"))\
                      .then_inc(uc_in[q % 2], 16)
                if q > 0:
                    load_slab(5 + q)
            full(sp, ("glu", NQ - 1, 1, 1))
            for t in range(NT):
                sp.dma_start(h[:, t, :], x_rows[t]).then_inc(x_in[t], 16)
            full(sp, ("y", NQ - 1, 1))
            for place in range(2):
                slab_loaded(sp, 7 + place)
            for r in range(KD):
                if r >= NROWS:
                    full(sp, ("wqT", r - NROWS, 1))
                sp.dma_start(w_rows[r % NROWS][:], xq_w[0, r * P:(r + 1) * P, :]).then_inc(slab_in[r % NROWS], 16)
            full(sp, ("h1", NT - 1, 1))
            for i in range(KD):
                r = KD + i
                rows_loaded(sp, r - NROWS)
                if i >= KD - 2:
                    full(sp, ("wqT", KD - 1, 1))
                sp.dma_start(wo_rows[i][:], xo_w[0, i * P:(i + 1) * P, :]).then_inc(slab_in[r % NROWS], 16)

            w1, w3, w2 = moe_w1[0], moe_w3[0], moe_w2[0]

            def load_half(j, k, weights, e, half):
                for part in (hi_ready, lo_ready):
                    wait_for(sp, part, 12 * j + k - NRAW + 1)
                n = HALF * F
                sp.dma_start(raw[k % NRAW][:].rearrange("p c f -> p (c f)"),
                             weights[bass.ds(e, 1)].rearrange("o (p c) f -> p (o c f)", p=P)
                             [:, half * n:(half + 1) * n]).then_inc(raw_in[k % NRAW], 16)

            def load_first(j, e):
                for k, (w, half) in enumerate(((w1, 0), (w1, 1), (w3, 0), (w3, 1))):
                    load_half(j, k, w, e, half)

            def load_next(j, s, e, before):
                for k, (w, n, half) in enumerate(((w1, e, 0), (w1, e, 1), (w2, before, 0), (w2, before, 1),
                                                  (w3, e, 0), (w3, e, 1))):
                    load_half(j, 4 + 6 * s + k, w, n, half)

            def load_last(j, e):
                for half in range(2):
                    load_half(j, 10 + half, w2, e, half)

            for half in range(2):
                full(sp, ("h2", NT - 1, half))
            load_first(0, 0)
            full(sp, ("h2T", NT - 2, 1))
            sp.wait_ge(xn_out[0], 16 * NT // 2)
            for s in range(2):
                load_next(0, s, 1 + s, s)
            with sp.Fori(1, NE // 2 - 1) as j:
                for s in range(2):
                    load_next(j, s, 2 * j + 1 + s, 2 * j + s)
            load_next(NE // 2 - 1, 0, NE - 1, NE - 2)
            load_last(NE // 2 - 1, NE - 1)
            sp.wait_ge(gidx_ready, 3)
            further = sp.value_load(meta[0:1, MAXOV:MAXOV + 1], min_val=0, max_val=MAXOV)

            def further_pair(o):
                e0, e1 = (sp.value_load(meta[0:1, bass.ds(2 * o + b, 1)], min_val=0, max_val=NE - 1)
                          for b in range(2))
                load_first(NE // 2 + o, e0)
                load_next(NE // 2 + o, 0, e1, e0)
                load_last(NE // 2 + o, e1)
            run_further(sp, further, further_pair)

            sp.dma_start(fin_w[:], final_norm_w.partition_broadcast(P)).then_inc(final_w_in, 16)
            sp.wait_ge(over_done, 1)
            pairs = y_rows.rearrange("(t p k) d -> t p k d", p=P, k=2)
            for t in range(NT):
                if t >= NY:
                    sp.wait_ge(comb, t - NY + 1)
                sp.dma_start(ytile[t % NY][:], pairs[t]).then_inc(y_in[t % NY], 16)
            out_rows = out[0].rearrange("(t p) d -> t p d", p=P)
            for t in range(NT):
                sp.wait_ge(out_ready, t + 1)
                sp.dma_start(out_rows[t], otile[t][:]).then_inc(out_stored, 16)
            sp.wait_ge(out_stored, 16 * NT)

        @block.gpsimd
        def _(pool):
            link = linker(pool, pool_step)
            link(nc.gpsimd.memset(ident[:], 0.0))
            nc.gpsimd.affine_select(out=ident[:], in_=ident[:], compare_op=ALU.not_equal, fill=1.0, base=0,
                                    pattern=[[-1, P]], channel_multiplier=1).then_inc(consts_ready, 1)
            nc.gpsimd.memset(means[:], 1.0 / DC).then_inc(consts_ready, 1)
            for w, r in ((norm_mix_w, 0), (norm_x_w, 8), (norm_mem_w, 16), (norm_ffn_w, 24)):
                pool.dma_start(rows_raw[r:r + KD, :], w[0].rearrange("(c p) -> c p", p=P)).then_inc(params_in, 16)
            for i, w in enumerate((conv_b, conv_ln_w, conv_ln_b, ssm_D.rearrange("a g c -> a (g c)"))):
                pool.dma_start(rows_raw[32 + 4 * i:36 + 4 * i, :],
                               w[0].rearrange("(c p) -> c p", p=P)).then_inc(params_in, 16)
            pool.dma_start(taps_raw[0:TAPS * KC, :], conv_w[0].rearrange("k (c p) -> (k c) p", p=P))\
                .then_inc(params_in, 16)
            for ri, b in enumerate((B_re, B_im)):
                pool.dma_start(b_raw[:, ri], b[0].rearrange("(n g) p h -> (g p) n h", g=2)).then_inc(braw_in, 16)
            pool.wait_ge(poles_in, 16 * 3)
            nc.gpsimd.tensor_copy(a_raw[:, 2, :].rearrange("n (g p) -> n g p", g=2),
                                  dt_raw[:].unsqueeze(2).to_broadcast([NP, 2, NS])).then_inc(consts_ready, 1)
            link(nc.gpsimd.memset(glu_lhs[:], 0.0))
            for g in range(GQ):
                for e in range(2):
                    pool.dma_start(glu_lhs[g * CH:(g + 1) * CH, :, e, g * CH:(g + 1) * CH],
                                   glu_w[0].rearrange("(q g) h (e o) -> g e h q o", g=GQ, e=2)[g, e])\
                        .then_inc(glu_in, 16)
            pool.wait_ge(nx.squares, NT)
            nc.gpsimd.memset(conv_in[:, :, 0:PAD], 0.0).then_inc(v_ready, 1)
            pool.wait_ge(nx.scaled, NT)
            link(nc.gpsimd.memset(shifts[:], 0.0))
            for d in range(T):
                part = shifts[:, d, :].rearrange("p (h j) -> p h j", j=T)[:, :, 0:T - d]
                last = nc.gpsimd.affine_select(out=part, in_=part, compare_op=ALU.not_equal, fill=1.0, base=-d,
                                               pattern=[[-T, CH], [-1, T - d]], channel_multiplier=1)
            last.then_inc(shifts_ready, 1)

            def gated(i, half):
                n = 2 * i + half + 1
                pool.wait_ge(conv_a_ready, n)
                pool.wait_ge(conv_sg_ready, n)
                nc.gpsimd.tensor_tensor(conv_in[:, i, PAD + half * BANK:PAD + (half + 1) * BANK],
                                        conv_a[:], conv_sg[:], ALU.mult).then_inc(v_ready, 1)

            def power_up(dst, src, coef, conj, shape, ready=None, count=0):
                n = 1
                for x in shape:
                    n *= x

                def flat(i):
                    t = pool_tmp[:, i, 0:n]
                    return t.rearrange("p (a b c) -> p a b c", a=shape[0], b=shape[1]) if len(shape) == 3 \
                        else t.rearrange("p (a b) -> p a b", a=shape[0])
                re, im = coef
                nc.gpsimd.tensor_tensor(flat(0), src[0], re, ALU.mult)
                nc.gpsimd.tensor_tensor(flat(1), src[1], im, ALU.mult)
                nc.gpsimd.tensor_tensor(flat(2), src[1], re, ALU.mult)
                link(nc.gpsimd.tensor_tensor(flat(3), src[0], im, ALU.mult))
                nc.gpsimd.tensor_tensor(dst[0], flat(0), flat(1), ALU.add if conj else ALU.subtract)
                last = nc.gpsimd.tensor_tensor(dst[1], flat(2), flat(3), ALU.subtract if conj else ALU.add)
                if ready is None:
                    link(last)
                else:
                    last.then_inc(ready, 1)
                    pool.wait_ge(ready, count)

            def tables(q):
                if q == 0:
                    pool.wait_ge(setup_ready, 1)
                ps = slice(q * PQ, (q + 1) * PQ)
                vin = bpow[:].rearrange("p r n (h s) -> p r n h s", s=T)
                vout = readout[q % 2][:].rearrange("p r n (h s) -> p r n h s", s=T)

                def coef(k, w):
                    return [pw[:, ri, k, ps].unsqueeze(2).unsqueeze(3).to_broadcast([P, PQ, CH, w])
                            for ri in range(2)]
                if q > 0:
                    full(pool, ("lift", q - 1, 1))
                    full(pool, ("kern", q - 1, 1))
                for ri in range(2):
                    last = nc.gpsimd.tensor_copy(vin[:, ri, :, :, T - 1], bbar[:, ri, ps, :])
                link(last)
                for k, w in enumerate((1, 2, 4)):
                    a, b = T - 2 * w, T - w
                    power_up([vin[:, ri, :, :, a:b] for ri in range(2)],
                             [vin[:, ri, :, :, b:b + w] for ri in range(2)], coef(k, w), False, (PQ, CH, w),
                             bpow_ready if k == 2 else None, q + 1)
                if q >= 2:
                    full(pool, ("y", q - 2, 1))
                if q == 1:
                    full(pool, ("u", KC - 1, 1))
                power_up([vout[:, ri, :, :, 0:1] for ri in range(2)],
                         [ct[:, ri, ps, :].unsqueeze(3) for ri in range(2)], coef(0, 1), True, (PQ, CH, 1))
                for k, w in enumerate((1, 2, 4)):
                    power_up([vout[:, ri, :, :, w:2 * w] for ri in range(2)],
                             [vout[:, ri, :, :, 0:w] for ri in range(2)], coef(k, w), True, (PQ, CH, w),
                             readout_ready if k == 2 else None, q + 1)
                if q >= 2:
                    pool.wait_ge(states_ready, q - 1)
                e = phase[q % 2]
                nc.gpsimd.memset(e[:, 0, :, 0:1], 1.0)
                link(nc.gpsimd.memset(e[:, 1, :, 0:1], 0.0))
                for k in range(7):
                    w = 1 << k
                    power_up([e[:, ri, :, w:2 * w] for ri in range(2)], [e[:, ri, :, 0:w] for ri in range(2)],
                             [ph[:, ri, k, ps].unsqueeze(2).to_broadcast([P, PQ, w]) for ri in range(2)],
                             False, (PQ, w), phase_ready if k == 6 else None, q + 1)

            for i in range(KC):
                gated(i, 0)
                gated(i, 1)
                if i == 1:
                    tables(0)
            for q in range(1, NQ):
                tables(q)

            full(pool, ("s", NT - 1, 1))
            link(nc.gpsimd.memset(upper[:], 1.0))
            nc.gpsimd.affine_select(out=upper[:], in_=upper[:], compare_op=ALU.is_gt, fill=0.0, base=0,
                                    pattern=[[1, P]], channel_multiplier=-1).then_inc(route_consts, 1)
            nc.gpsimd.memset(ones[:], 1.0).then_inc(route_consts, 1)
            iota = dict(allow_small_or_imprecise_dtypes=True)
            nc.gpsimd.iota(iota_n[:], pattern=[[1, P]], base=0, channel_multiplier=0, **iota).then_inc(route_consts, 1)
            nc.gpsimd.iota(assign_no[:], pattern=[[1, 2], [2 * P, NT]], base=1, channel_multiplier=2, **iota)\
                .then_inc(route_consts, 1)
            nc.gpsimd.iota(limits[:], pattern=[[P, 7]], base=P, channel_multiplier=0, **iota).then_inc(route_consts, 1)

            for b in range(2):
                link(nc.gpsimd.memset(xg[b][:], 0.0))

            for k in range(NSPLIT):
                pool.wait_ge(hi_ready, k + 1)
                nc.gpsimd.tensor_tensor(out=w_lo[k][:], in0=raw[k][:], in1=w_hi[k][:].bitcast(F32), op=ALU.subtract)\
                    .then_inc(lo_ready, 1)

            last_token = pool.to_reg(S - 1)
            last_row = pool.to_reg(2 * S - 1)

            def fetch(b):
                pool.sem_inc(rows_moved, 1)
                nc.gpsimd.indirect_dma_start(
                    out=xg[b][:], out_offset=None, in_=xn_rows,
                    in_offset=bass.IndirectOffsetOnAxis(ap=gidx[b][:, 0:1], axis=0),
                    bounds_check=last_token, oob_is_err=False).then_inc(xg_in[b], 16)

            def send(b, i):
                pool.wait_ge(sidx_ready, i + 1)
                pool.wait_ge(yb_ready, i + 1)
                pool.sem_inc(rows_moved, 1)
                nc.gpsimd.indirect_dma_start(
                    out=y_rows, out_offset=bass.IndirectOffsetOnAxis(ap=sidx[b][:, 0:1], axis=0),
                    in_=yb[b][:], in_offset=None,
                    bounds_check=last_row, oob_is_err=False).then_inc(y_sent[b], 16)

            for b in range(2):
                pool.wait_ge(xn_out[b], 16 * NT // 2)
            for b in range(2):
                pool.wait_ge(gidx_ready, b + 1)
                fetch(b)
            for i in (2, 3):
                pool.wait_ge(gidx_ready, i + 1)
                pool.wait_ge(xg_turned, i - 1)
                fetch(i % 2)
            with pool.Fori(0, NE // 2 - 1) as j:
                for b in range(2):
                    send(b, 2 * j + b)
                    pool.wait_ge(gidx_ready, 2 * j + b + 5)
                    pool.wait_ge(xg_turned, 2 * j + b + 3)
                    fetch(b)
            for i in range(NE - 2, NE):
                send(i % 2, i)
            further = pool.value_load(meta[0:1, MAXOV:MAXOV + 1], min_val=0, max_val=MAXOV)

            def further_pair(o):
                for b in range(2):
                    pool.wait_ge(gidx_ready, NE + 2 * o + b + 3)
                    pool.wait_ge(xg_turned, NE + 2 * o + b + 1)
                    fetch(b)
                for b in range(2):
                    send(b, NE + 2 * o + b)
                for b in range(2):
                    pool.wait_ge(y_sent[b], 16 * (NE // 2 + 1) + 16 * o)
                    pool.wait_ge(xg_in[b], 16 * (NE // 2 + 2) + 16 * o)
            run_further(pool, further, further_pair)
            for b in range(2):
                pool.wait_ge(y_sent[b], 16 * (NE // 2))
                pool.wait_ge(xg_in[b], 16 * (NE // 2 + 1))
            nc.gpsimd.memset(pool_mark[:], 0.0).then_inc(over_done, 1)

            pool.wait_ge(final_w_in, 16)
            for t in range(NT):
                pool.wait_ge(n2.scaled, t + 1)
                nc.gpsimd.tensor_tensor(otile[t][:], otile[t][:], fin_w[:], ALU.mult).then_inc(out_ready, 1)

        @block.scalar
        def _(act):
            link = linker(act, act_step)

            def act_squares(norm, src, t, scratch, st):
                if t > 0:
                    act.wait_ge(norm.squares, t)
                nc.scalar.activation(scratch, src, ACT.Square, accum_out=st[:, 0, t:t + 1])\
                    .then_inc(norm.squares, 1)

            def act_root(norm, t, st):
                act.wait_ge(norm.var, t + 1)
                nc.scalar.activation(st[:, 1, t:t + 1], st[:, 1, t:t + 1], ACT.Sqrt).then_inc(norm.root, 1)

            def act_scale(norm, dst, src, t, st):
                act.wait_ge(norm.rstd, t + 1)
                nc.scalar.activation(dst, src, ACT.Copy, scale=st[:, 2, t:t + 1]).then_inc(norm.scaled, 1)

            act.wait_ge(x_in[0], 16)
            act_squares(nx, h[:, 0, :], 0, junk_x[:], stat)
            for t in range(NT):
                if t + 1 < NT:
                    act.wait_ge(x_in[t + 1], 16)
                    act_squares(nx, h[:, t + 1, :], t + 1, junk_x[:], stat)
                act_root(nx, t, stat)
            act.wait_ge(trig_in, 1)
            nc.scalar.activation(t16[:, 9], t16[:, 4], ACT.Sin).then_inc(trig_out, 1)
            nc.scalar.activation(t16[:, 10], t16[:, 4], ACT.Sin, scale=0.5).then_inc(trig_out, 1)
            act.wait_ge(mem_in, 16)
            act.wait_ge(nx.scaled, NT)
            for t in range(MT):
                act_squares(nm, mem_rows[:, t, :], t, junk_m[:], stat_m)
                act_root(nm, t, stat_m)
                act_scale(nm, mem_rows[:, t, :], mem_rows[:, t, :], t, stat_m)

            for i in range(KC):
                for half in range(2):
                    n = 2 * i + half
                    if n > 0:
                        act.wait_ge(v_ready, n + 1)
                    src = full(act, ("a", i, half))
                    nc.scalar.activation(conv_a[:], src[:], ACT.Copy).then_inc(conv_a_ready, 1)
                    act.wait_ge(conv_a_ready, n + 1)
                    nc.scalar.sem_inc(bank_free[half], 1)
                    src = full(act, ("g", i, half))
                    nc.scalar.activation(conv_sg[:], src[:], ACT.Sigmoid).then_inc(conv_sg_ready, 1)
                    act.wait_ge(conv_sg_ready, n + 1)
                    nc.scalar.sem_inc(bank_free[2 + half], 1)
            for q in range(NQ):
                for half in range(2):
                    src = full(act, ("u", q, half))
                    nc.scalar.activation(u_perm[:, q, :, half * NC // 2:(half + 1) * NC // 2],
                                         src[:].rearrange("p (c j) -> p j c", j=T), ACT.Copy).then_inc(u_ready, 1)
                    act.wait_ge(u_ready, 2 * q + half + 1)
                    nc.scalar.sem_inc(bank_free[4 + half], 1)
            for t in range(MT):
                for c in range(KD):
                    src = full(act, ("m", t, c // 4))
                    nc.scalar.activation(memT[:, c, t * P:(t + 1) * P], src[:, (c % 4) * P:(c % 4 + 1) * P], ACT.Copy,
                                         scale=par[:, 16 + c:17 + c]).then_inc(memT_ready, 1)
                    if c % 4 == 3:
                        act.wait_ge(memT_ready, t * KD + c + 1)
                        nc.scalar.sem_inc(bank_free[6 + c // 4], 1)

            def read_out(key, dst, src, ready, count, **how):
                b, _ = use_of[key]
                full(act, key)
                nc.scalar.activation(dst, src(bank[b]), how.pop("func", ACT.Copy), **how).then_inc(ready, 1)
                act.wait_ge(ready, count)
                nc.scalar.sem_inc(bank_free[b], 1)

            def setup_out(q):
                for ri in range(2):
                    if ri == 0 and q >= 2:
                        full(act, ("S", q - 2, 1))
                    read_out(("lift", q, ri), lift[q % 2][:, ri].rearrange("p n m -> p (n m)"), lambda b: b[:],
                             lift_ready, 2 * q + ri + 1)
                for g2 in range(2):
                    if q > 0 and g2 == 0:
                        full(act, ("toep", q - 1, 1))
                    read_out(("kern", q, g2), kern[:].rearrange("p (n g) o -> p g n o", g=2)[:, g2],
                             lambda b: b[:, 0:PQ * CH].rearrange("p (n o) -> p n o", o=CH), kern_ready, 2 * q + g2 + 1)
                for jh in range(2):
                    if q >= 2 and jh == 0:
                        full(act, ("y", q - 2, 1))
                    read_out(("toep", q, jh),
                             toep[q % 2][:].rearrange("p g (o j) -> p j g o", j=T)[:, 4 * jh:4 * jh + 4],
                             lambda b: b[:].rearrange("p (j g o) -> p j g o", j=4, g=GQ), toep_ready, 2 * q + jh + 1)

            kv = [0]

            def kv_out(n, tiles):
                for m in tiles:
                    kv[0] += 1
                    dst = (kT if n < 2 else vT)[:, 4 * (n % 2) + m, :]
                    read_out(("kv", 4 * n + m), dst, lambda b: b[:, 0:M], kv_ready, kv[0],
                             scale=float(HD) ** -0.5 if n < 2 else 1.0)

            def gelu(q):
                act.wait_ge(dterm_done, q + 1)
                nc.scalar.activation(y_feat[:], y_feat[:], ACT.Gelu_apprx_tanh).then_inc(gelu_done, 1)

            def glu_gates(q, halves=range(2)):
                for jh in halves:
                    n = 2 * q + jh
                    if n > 0:
                        act.wait_ge(yssm_ready, n)
                    read_out(("glu", q, jh, 1), glu_sig[:], lambda b: b[:], glu_sig_ready, n + 1, func=ACT.Sigmoid)

            def wout_high(half):
                slab_loaded(act, 7 + half)
                for k in (0, KC):
                    nc.scalar.activation(wout_hi[half][:, k:k + KC, :], slab[half][:, k:k + KC, :], ACT.Copy)\
                        .then_inc(table_hi_ready, 1)

            def y_high(t, feats=slice(0, KD)):
                if t >= 2:
                    full(act, ("h1", t - 2, 1))
                nc.scalar.activation(y_hi[t % 2][:, feats, :], yT[:, feats, t * P:(t + 1) * P], ACT.Copy)\
                    .then_inc(y_hi_ready, 1)

            setup_out(0)
            for q in range(NQ):
                kv_out(q, (0,))
                if q > 0:
                    gelu(q - 1)
                kv_out(q, (2, 3))
                if q == NQ - 1:
                    for t in range(2):
                        y_high(t, slice(KC, KD))
                for g2 in range(2):
                    if g2 == 0 and q > 0:
                        act.wait_ge(yb_out, 16 * q)
                    read_out(("y", q, g2), y_chunks[:].rearrange("p (n g) c -> p g n c", g=2)[:, g2],
                             lambda b: b[:].rearrange("p (n c) -> p n c", c=NC), ychunk_ready, 2 * q + g2 + 1)
                if q == NQ - 1:
                    wout_high(0)
                    kv_out(q, (1,))
                    glu_gates(q - 1)
                else:
                    if q > 0:
                        glu_gates(q - 1, (0,))
                    kv_out(q, (1,))
                    if q > 0:
                        glu_gates(q - 1, (1,))
                if q + 1 < NQ:
                    setup_out(q + 1)
                if q == 0:
                    for half in range(2):
                        act.wait_ge(centered, half + 1)
                        nc.scalar.activation(squares[:, half], conv_acc[:, :, half * BANK:(half + 1) * BANK],
                                             ACT.Square).then_inc(squared, 1)
                if q == 1:
                    act.wait_ge(ln_v, 2)
                    nc.scalar.activation(ln_var[:], ln_var[:], ACT.Sqrt).then_inc(ln_root, 1)
                if q == 2:
                    act.wait_ge(ln_scaled, 2)
                    for k in range(KC):
                        nc.scalar.activation(conv_acc[:, k, :], conv_acc[:, k, :], ACT.Silu,
                                             bias=par[:, 40 + k:41 + k], scale=par[:, 36 + k:37 + k])\
                            .then_inc(yconv_ready, 1)
            gelu(NQ - 1)
            glu_gates(NQ - 1)
            act.wait_ge(yssm_ready, 2 * NQ)
            for t in range(2):
                y_high(t, slice(0, KC))
            wout_high(1)

            full(act, ("glu", NQ - 1, 1, 1))
            act.dma_start(router_w[:, :, 0:NG], router_group_w[0].rearrange("(c p) n -> p c n", p=P))\
               .then_inc(router_in, 16)
            act.dma_start(router_w[:, :, NG:NR], router_expert_w[0].rearrange("(c p) n -> p c n", p=P))\
               .then_inc(router_in, 16)
            act.dma_start(router_b[:, 0:NG], router_group_b[0].partition_broadcast(P)).then_inc(router_in, 16)
            act.dma_start(router_b[:, NG:NR], router_expert_b[0].rearrange("g e -> (g e)").partition_broadcast(P))\
               .then_inc(router_in, 16)

            def high_part(key, dst, ready, **how):
                src = full(act, key)
                nc.scalar.activation(dst, src[:], ACT.Copy, **how).then_inc(ready, 1)

            def key_high(i):
                for b in range(2):
                    high_part(("key", i, b), key_hi[:, i, b * BANK:(b + 1) * BANK], table_hi_ready,
                              scale=par[:, 8 + i:9 + i])

            for t in range(NT):
                if t + 2 < NT:
                    y_high(t + 2)
                act.wait_ge(h1_ready, 2 * t + 2)
                act_squares(n1, h[:, t, :], t, junk[:], stat)
                act_root(n1, t, stat)

            for i in range(KD + 1):
                if i < KD:
                    for b in range(2):
                        if i >= 2 and b == 0:
                            full(act, ("key", i - 2, 1))
                        read_out(("wqT", i, b), wqT[i % 2][:, 4 * b:4 * b + 4, :].rearrange("p c n -> p (c n)"),
                                 lambda x: x[:], wqT_ready, 2 * i + b + 1)
                if i > 0:
                    key_high(i - 1)

            def turned_high(key, t, dst, ready):
                for b in range(2):
                    high_part((key, t, b), dst[:, 4 * b:4 * b + 4, :].rearrange("p c n -> p (c n)"), ready)

            act_scale(n1, x1s[:], h[:, 0, :], 0, stat)
            turned_high("h1T", 0, hT_hi, hT_hi_ready)
            act_scale(n1, x1s[:], h[:, 1, :], 1, stat)
            for n in range(NH * MT):
                for half in range(2):
                    high_part(("value", n, half), value_hi[:, n, half * BANK:(half + 1) * BANK], table_hi_ready)

            for s in range(NT + 2):
                if s < NT:
                    act.wait_ge(negmax_ready, 2 * s + 2)
                    if s >= 1:
                        full(act, ("pT", s - 1, 1))
                    for hd in range(NH):
                        nc.scalar.activation(probs[:, hd, :], bank[hd // 2][:, (hd % 2) * M:(hd % 2 + 1) * M],
                                             ACT.Exp, bias=negmax[:, s % 2, hd:hd + 1],
                                             accum_out=expsum[:, s % 2, hd:hd + 1]).then_inc(exp_done, 1)
                        if hd % 2:
                            act.wait_ge(exp_done, NH * s + hd + 1)
                            nc.scalar.sem_inc(bank_free[hd // 2], 1)
                if s + 1 < NT:
                    turned_high("h1T", s + 1, hT_hi, hT_hi_ready)
                if s + 2 < NT:
                    act_scale(n1, x1s[:], h[:, s + 2, :], s + 2, stat)
                t = s - 1
                if 0 <= t < NT:
                    act.wait_ge(h2_ready, 2 * t + 2)
                    if t == 0:
                        act.wait_ge(n1.squares, NT)
                    act_squares(nf, h[:, t, :], t, junk[:], stat)
                    act_root(nf, t, stat)
                    if t >= 2:
                        full(act, ("h2T", t - 2, 1))
                        act.wait_ge(xn_out[t % 2], 16 * (t // 2))
                    act_scale(nf, xs[t % 2][:], h[:, t, :], t, stat)
                    act.wait_ge(nf.scaled, t + 1)
                    act.dma_start(xn_rows[t * P:(t + 1) * P, :], xs[t % 2][:]).then_inc(xn_out[t % 2], 16)
                t = s - 2
                if 0 <= t:
                    read_out(("router", t), logits[:, t, :], lambda b: b[:, 0:NR], logit_ready, t + 1)
                if s < NT:
                    turned_high("pT", s, pT_hi, pT_hi_ready)

            def split_high(j, k):
                act.wait_ge(raw_in[k % NRAW], 16 * (2 * j + k // NRAW + 1))
                wait_for(act, piece_used, 12 * j + k - NSPLIT + 1)
                nc.scalar.activation(w_hi[k % NSPLIT][:], raw[k % NRAW][:], ACT.Copy).then_inc(hi_ready, 1)

            for half in range(2):
                full(act, ("h2", NT - 1, half))
            for k in range(2):
                split_high(0, k)

            act.wait_ge(rexp_in, 1)
            nc.scalar.activation(gsel[:, 0], gsel[:, 0], ACT.Exp).then_inc(rexp_out, 1)
            act.wait_ge(rexp_in, 2)
            nc.scalar.activation(col[:, 6], col[:, 6], ACT.Exp).then_inc(rexp_out, 1)

            for k in range(2, NSPLIT):
                split_high(0, k)

            def tokens_high(b, i):
                act.wait_ge(xw_ready, i + 1)
                nc.scalar.activation(x_hi[b][:], xw[:], ACT.Copy).then_inc(x_hi_ready, 1)

            def gate_of(j, k):
                act.wait_ge(piece_used, 12 * j + k)
                nc.scalar.activation(gate_act[:], bank[2][:], ACT.Silu).then_inc(gate_ready, 1)

            def hidden_high(i):
                act.wait_ge(hid_turned, i + 1)
                nc.scalar.activation(hid_hi[:].rearrange("p f n -> p (f n)"), bank[4][:], ACT.Copy)\
                    .then_inc(hid_hi_ready, 1)

            def rows_out(j, k, b):
                act.wait_ge(piece_used, 12 * j + k)
                wait_for(act, y_sent[b], 16 * j)
                nc.scalar.activation(yb[b][:, 0:BANK], bank[5][:], ACT.Copy)
                nc.scalar.activation(yb[b][:, BANK:D], bank[6][:], ACT.Copy).then_inc(yb_ready, 1)

            def first_block(j, unsplit=()):
                tokens_high(0, 2 * j)
                for k in unsplit:
                    split_high(j, k)
                split_high(j, 4)
                gate_of(j, 2)
                split_high(j, 5)
                tokens_high(1, 2 * j + 1)
                split_high(j, 6)
                split_high(j, 7)

            def next_block(j, s, final=False):
                i, k = 2 * j + 1 + s, 4 + 6 * s
                hidden_high(i - 1)
                split_high(j, k + 4)
                gate_of(j, k + 2)
                split_high(j, k + 5)
                split_high(j, k + 6)
                rows_out(j, k + 4, s)
                split_high(j, k + 7)
                if not final:
                    tokens_high(s, i + 1)
                    split_high(j, k + 8)
                    split_high(j, k + 9)

            def last_down(j):
                hidden_high(2 * j + 1)
                rows_out(j, 12, 1)

            first_block(0)
            for s in range(2):
                next_block(0, s)
            with act.Fori(1, NE // 2 - 1) as j:
                for s in range(2):
                    next_block(j, s)
            next_block(NE // 2 - 1, 0, final=True)
            last_down(NE // 2 - 1)
            further = act.value_load(meta[0:1, MAXOV:MAXOV + 1], min_val=0, max_val=MAXOV)

            def further_pair(o):
                split_high(NE // 2 + o, 0)
                first_block(NE // 2 + o, unsplit=range(1, NSPLIT))
                next_block(NE // 2 + o, 0, final=True)
                last_down(NE // 2 + o)
            run_further(act, further, further_pair)

            act.wait_ge(comb, 1)
            act_squares(n2, h[:, 0, :], 0, junk_f[:], stat)
            for t in range(NT):
                if t + 1 < NT:
                    act.wait_ge(comb, t + 2)
                    act_squares(n2, h[:, t + 1, :], t + 1, junk_f[:], stat)
                act_root(n2, t, stat)
                act_scale(n2, otile[t][:], h[:, t, :], t, stat)

        @block.vector
        def _(dve):
            link = linker(dve, dve_step)
            V = nc.vector

            def ts(out, a, s1, s2, op0, op1=ALU.bypass):
                return V.tensor_scalar(out, a, s1, s2, op0, op1)

            def stt(out, a, s, b, op0, op1):
                return V.scalar_tensor_tensor(out=out, in0=a, scalar=s, in1=b, op0=op0, op1=op1)

            def tt(out, a, b, op):
                return V.tensor_tensor(out, a, b, op)

            def frees(key, ins):
                ins.then_inc(bank_free[use_of[key][0]], 1)

            def dve_var(norm, t, st):
                dve.wait_ge(norm.squares, t + 1)
                ts(st[:, 1, t:t + 1], st[:, 0, t:t + 1], 1.0 / D, EPS, ALU.mult, ALU.add).then_inc(norm.var, 1)

            def dve_rstd(norm, t, st):
                dve.wait_ge(norm.root, t + 1)
                V.reciprocal(st[:, 2, t:t + 1], st[:, 1, t:t + 1]).then_inc(norm.rstd, 1)

            def dve_store(norm, key, dst, t, c0):
                for b in range(2):
                    src = full(dve, (key, t, b))
                    w = par[:, c0 + 4 * b:c0 + 4 * b + 4].unsqueeze(2).to_broadcast([P, 4, P])
                    link(tt(dst[:, 4 * b:4 * b + 4], src[:].rearrange("p (c n) -> p c n", n=P), w, ALU.mult))
                    V.sem_inc(bank_free[use_of[(key, t, b)][0]], 1)
                V.sem_inc(norm.stored, 1)

            dve_var(nx, 0, stat)
            for s in range(NT + 3):
                if s < NT:
                    if s + 1 < NT:
                        dve_var(nx, s + 1, stat)
                    dve_rstd(nx, s, stat)
                    dve.wait_ge(nx.rstd, s + 1)
                    if s >= 4:
                        full(dve, ("x", s - 4, 1))
                    ts(xs0[s % 4][:], h[:, s, :], stat[:, 2, s:s + 1], None, ALU.mult).then_inc(nx.scaled, 1)
                t = s - 3
                if t == 0:
                    full(dve, "par")
                    link(V.tensor_copy(par[:, 0:48], bank[0][:, 0:48]))
                    V.sem_inc(bank_free[0], 1)
                if t >= 0:
                    dve_store(nx, "x", xT[:, :, t * P:(t + 1) * P], t, 0)
            full(dve, "taps")
            link(V.tensor_copy(taps[:], bank[1][:, 0:TAPS * KC]))
            V.sem_inc(bank_free[1], 1)
            full(dve, "a_raw")
            link(V.tensor_copy(t16[:, 0:3], bank[2][:, 0:3 * NP].rearrange("p (i n) -> p i n", n=NP)))
            V.sem_inc(bank_free[2], 1)
            full(dve, "c_raw")
            c_turned = bank[3][:].rearrange("p (r n h) -> p r n h", r=2, n=NP)
            link(V.tensor_copy(ct[:, 0], c_turned[:, 0]))
            link(ts(ct[:, 1], c_turned[:, 1], -1.0, None, ALU.mult))
            V.sem_inc(bank_free[3], 1)


            def z(i):
                return t16[:, i]
            are, aim, ldt = z(0), z(1), z(2)

            def expm1_poly(out, f):
                link(ts(out, f, 1.0 / 5040, None, ALU.mult))
                for c in (1.0 / 720, 1.0 / 120, 1.0 / 24, 1.0 / 6, 0.5, 1.0):
                    link(stt(out, out, c, f, ALU.add, ALU.mult))

            link(ts(z(3), ldt, LOG2E, ROUND, ALU.mult, ALU.add))
            link(ts(z(3), z(3), ROUND, None, ALU.subtract))
            link(stt(z(4), z(3), -LN2_HI, ldt, ALU.mult, ALU.add))
            link(stt(z(4), z(3), -LN2_LO, z(4), ALU.mult, ALU.add))
            expm1_poly(z(5), z(4))
            link(ts(z(3), z(3), -127.0, 128.0, ALU.max, ALU.min))
            link(ts(z(6).bitcast(I32), z(3), 127.0, float(1 << 23), ALU.add, ALU.mult))
            link(stt(z(2), z(5), 1.0, z(6), ALU.add, ALU.mult))
            link(tt(z(7), are, z(2), ALU.mult))
            link(tt(z(8), aim, z(2), ALU.mult))
            link(ts(z(7), z(7), -87.0, 1.0 / 256, ALU.max, ALU.mult))
            expm1_poly(z(5), z(7))
            for _ in range(8):
                link(stt(z(5), z(5), 2.0, z(5), ALU.add, ALU.mult))
            link(ts(z(3), z(8), 1.0 / TWO_PI, ROUND, ALU.mult, ALU.add))
            link(ts(z(3), z(3), ROUND, None, ALU.subtract))
            link(stt(z(4), z(3), -TWO_PI_A, z(8), ALU.mult, ALU.add))
            link(stt(z(4), z(3), -TWO_PI_B, z(4), ALU.mult, ALU.add))
            link(stt(z(4), z(3), -TWO_PI_C, z(4), ALU.mult, ALU.add))
            ts(z(4), z(4), -PI_LOW, PI_LOW, ALU.max, ALU.min).then_inc(trig_in, 1)
            dve.wait_ge(trig_out, 2)
            link(stt(z(6), z(10), -2.0, z(10), ALU.mult, ALU.mult))
            link(ts(z(11), z(6), 1.0, None, ALU.add))
            link(ts(z(8), z(5), 1.0, None, ALU.add))
            link(tt(pw[:, 0, 0], z(8), z(11), ALU.mult))
            link(tt(pw[:, 1, 0], z(8), z(9), ALU.mult))
            link(tt(z(3), z(5), z(11), ALU.mult))
            link(tt(z(3), z(3), z(6), ALU.add))
            link(tt(z(4), are, are, ALU.mult))
            link(tt(z(7), aim, aim, ALU.mult))
            link(tt(z(4), z(4), z(7), ALU.add))
            link(V.reciprocal(z(4), z(4)))
            link(tt(z(5), z(3), are, ALU.mult))
            link(tt(z(6), pw[:, 1, 0], aim, ALU.mult))
            link(tt(z(5), z(5), z(6), ALU.add))
            link(tt(z(5), z(5), z(4), ALU.mult))
            link(tt(z(6), pw[:, 1, 0], are, ALU.mult))
            link(tt(z(7), z(3), aim, ALU.mult))
            link(tt(z(6), z(6), z(7), ALU.subtract))
            link(tt(z(6), z(6), z(4), ALU.mult))
            dve.wait_ge(braw_in, 32)
            dve.wait_ge(late_params_in, 16 * 3)
            wre = z(5).unsqueeze(2).to_broadcast([P, NP, CH])
            wim = z(6).unsqueeze(2).to_broadcast([P, NP, CH])
            link(tt(bbar[:, 0], b_raw[:, 0], wre, ALU.mult))
            link(tt(bbar[:, 1], b_raw[:, 1], wim, ALU.mult))
            link(tt(bbar[:, 0], bbar[:, 0], bbar[:, 1], ALU.subtract))
            link(tt(bbar[:, 1], b_raw[:, 1], wre, ALU.mult))
            link(tt(b_raw[:, 0], b_raw[:, 0], wim, ALU.mult))
            link(tt(bbar[:, 1], bbar[:, 1], b_raw[:, 0], ALU.add))

            def square(dre, dim, re, im):
                link(tt(z(3), im, im, ALU.mult))
                link(tt(z(4), re, re, ALU.mult))
                link(stt(dim, re, 2.0, im, ALU.mult, ALU.mult))
                link(tt(dre, z(4), z(3), ALU.subtract))
            square(pw[:, 0, 1], pw[:, 1, 1], pw[:, 0, 0], pw[:, 1, 0])
            square(pw[:, 0, 2], pw[:, 1, 2], pw[:, 0, 1], pw[:, 1, 1])
            link(tt(rho[:], z(8), z(8), ALU.mult))
            link(tt(rho[:], rho[:], rho[:], ALU.mult))
            link(tt(rho[:], rho[:], rho[:], ALU.mult))
            square(z(5), z(6), z(11), z(9))
            square(z(7), z(8), z(5), z(6))
            square(ph[:, 0, 0], ph[:, 1, 0], z(7), z(8))
            for k in range(6):
                square(ph[:, 0, k + 1], ph[:, 1, k + 1], ph[:, 0, k], ph[:, 1, k])
            V.sem_inc(setup_ready, 1)

            for t in range(MT):
                dve_var(nm, t, stat_m)
                dve_rstd(nm, t, stat_m)
            def rotate(q):
                cos, sin = phase[q % 2][:, 0], phase[q % 2][:, 1]
                re, im = (bank[6 + ri][:].rearrange("p (n c) -> p n c", c=NC) for ri in range(2))
                dve.wait_ge(phase_ready, q + 1)
                full(dve, ("S", q, 0))
                full(dve, ("S", q, 1))
                tt(rotated[:, 0], re, cos, ALU.mult)
                tt(rot_tmp[:, 0], im, sin, ALU.mult)
                tt(rotated[:, 1], im, cos, ALU.mult)
                link(tt(rot_tmp[:, 1], re, sin, ALU.mult))
                V.sem_inc(bank_free[6], 1)
                V.sem_inc(bank_free[7], 1)
                tt(rotated[:, 0], rotated[:, 0], rot_tmp[:, 0], ALU.add)
                link(tt(rotated[:, 1], rotated[:, 1], rot_tmp[:, 1], ALU.subtract))
                for ri in range(2):
                    for p in PAIRS:
                        n = q * PQ + p
                        last = V.tensor_tensor_scan(scanned[:, ri, p, :], rho[:, n:n + 1].to_broadcast([P, NC]),
                                                    rotated[:, ri, p, :], 0.0, ALU.mult, ALU.add)
                link(last)
                tt(rotated[:, 0], scanned[:, 0], cos, ALU.mult)
                tt(rot_tmp[:, 0], scanned[:, 1], sin, ALU.mult)
                tt(rotated[:, 1], scanned[:, 0], sin, ALU.mult)
                link(tt(rot_tmp[:, 1], scanned[:, 1], cos, ALU.mult))
                if q == 0:
                    link(V.memset(states[:, :, :, 0:1], 0.0))
                else:
                    full(dve, ("y", q - 1, 1))
                tt(states[:, 0, :, 1:NC + 1], rotated[:, 0], rot_tmp[:, 0], ALU.subtract)
                link(tt(states[:, 1, :, 1:NC + 1], rotated[:, 1], rot_tmp[:, 1], ALU.add))
                V.sem_inc(states_ready, 1)

            for i in range(KC):
                dve.wait_ge(v_ready, 2 * i + 3)
                link(ts(conv_acc[:, i, :], conv_in[:, i, 0:S], taps[:, i:i + 1], par[:, 32 + i:33 + i],
                        ALU.mult, ALU.add))
                for k in range(1, TAPS):
                    ins = stt(conv_acc[:, i, :], conv_in[:, i, k:k + S], taps[:, k * KC + i:k * KC + i + 1],
                              conv_acc[:, i, :], ALU.mult, ALU.add)
                    if k < TAPS - 1:
                        link(ins)
                    if i == KC - 1 and k == 2 * TAPS // 3:
                        rotate(0)
                ins.then_inc(conv_done, 1)

            def direct(q):
                dve.wait_ge(yf_in, 16 * q + 16)
                stt(y_feat[:], u_perm[:, q], par[:, 44 + q:45 + q], y_feat[:], ALU.mult, ALU.add)\
                    .then_inc(dterm_done, 1)

            def gated(q):
                for jh in range(2):
                    n = 2 * q + jh + 1
                    dve.wait_ge(glu_sig_ready, n)
                    src = full(dve, ("glu", q, jh, 0))
                    tt(yT[:, q, :].rearrange("p (c j) -> p j c", j=T)[:, 4 * jh:4 * jh + 4],
                       src[:].rearrange("p (j c) -> p j c", j=4),
                       glu_sig[:].rearrange("p (j c) -> p j c", j=4), ALU.mult).then_inc(yssm_ready, 1)
                    dve.wait_ge(yssm_ready, n)
                    V.sem_inc(bank_free[use_of[("glu", q, jh, 0)][0]], 1)

            def wout_low(half):
                for i, k in enumerate((0, KC)):
                    dve.wait_ge(table_hi_ready, 2 * half + i + 1)
                    tt(wout_lo[half][:, k:k + KC, :], slab[half][:, k:k + KC, :],
                       wout_hi[half][:, k:k + KC, :].bitcast(F32), ALU.subtract).then_inc(table_lo_ready, 1)

            def y_low(t, count, feats=slice(0, KD)):
                dve.wait_ge(y_hi_ready, count)
                tt(y_lo[t % 2][:, feats, :], yT[:, feats, t * P:(t + 1) * P], y_hi[t % 2][:, feats, :].bitcast(F32),
                   ALU.subtract).then_inc(y_lo_ready, 1)

            def half_of_conv(half):
                return conv_acc[:, :, half * BANK:(half + 1) * BANK]

            for half in range(2):
                src = full(dve, ("mean", half))
                tt(half_of_conv(half), half_of_conv(half), src[:].unsqueeze(1).to_broadcast([P, KC, BANK]),
                   ALU.subtract).then_inc(centered, 1)
                dve.wait_ge(centered, half + 1)
                V.sem_inc(bank_free[use_of[("mean", half)][0]], 1)
            direct(0)
            rotate(1)
            gated(0)
            for half in range(2):
                src = full(dve, ("lnvar", half))
                ts(ln_var[:, half], src[:], EPS, None, ALU.add).then_inc(ln_v, 1)
                dve.wait_ge(ln_v, half + 1)
                V.sem_inc(bank_free[use_of[("lnvar", half)][0]], 1)
            direct(1)
            rotate(2)
            gated(1)
            dve.wait_ge(ln_root, 1)
            link(V.reciprocal(ln_var[:], ln_var[:]))
            for half in range(2):
                tt(half_of_conv(half), half_of_conv(half), ln_var[:, half].unsqueeze(1).to_broadcast([P, KC, BANK]),
                   ALU.mult).then_inc(ln_scaled, 1)
            direct(2)
            rotate(3)
            dve.wait_ge(yconv_ready, KC)
            for t in range(2):
                y_low(t, t + 1, slice(KC, KD))
            wout_low(0)
            gated(2)
            direct(3)
            gated(3)
            for t in range(2):
                y_low(t, t + 3, slice(0, KC))
            wout_low(1)

            def low_part(key, dst, high, ready, made, counts, scale=None):
                hi_count, lo_count = counts
                src = full(dve, key)
                dve.wait_ge(made, hi_count)
                if scale is None:
                    ins = tt(dst, src[:], high.bitcast(F32), ALU.subtract)
                else:
                    ins = stt(dst, src[:], scale, high.bitcast(F32), ALU.mult, ALU.subtract)
                ins.then_inc(ready, 1)
                dve.wait_ge(ready, lo_count)
                V.sem_inc(bank_free[use_of[key][0]], 1)

            def key_low(i):
                for b in range(2):
                    n, cols = 4 + 2 * i + b + 1, slice(b * BANK, (b + 1) * BANK)
                    low_part(("key", i, b), key_lo[:, i, cols], key_hi[:, i, cols], table_lo_ready, table_hi_ready,
                             (n, n), par[:, 8 + i:9 + i])

            def turned_low(key, t, dst, high, ready, made):
                for b in range(2):
                    n = 2 * t + b + 1
                    low_part((key, t, b), *(a[:, 4 * b:4 * b + 4, :].rearrange("p c n -> p (c n)") for a in (dst, high)),
                             ready, made, (n, n))

            for t in range(NT):
                dve.wait_ge(x_in[t], 32)
                for half in range(2):
                    src = full(dve, ("h1", t, half))
                    part = h[:, t, half * BANK:(half + 1) * BANK]
                    tt(part, part, src[:], ALU.add).then_inc(h1_ready, 1)
                    dve.wait_ge(h1_ready, 2 * t + half + 1)
                    V.sem_inc(bank_free[use_of[("h1", t, half)][0]], 1)
                if t + 2 < NT:
                    y_low(t + 2, t + 5)
                dve_var(n1, t, stat)
                dve_rstd(n1, t, stat)
            for i in range(KD):
                key_low(i)
            turned_low("h1T", 0, hT_lo, hT_hi, hT_lo_ready, hT_hi_ready)
            for i in range(NH * MT):
                for half in range(2):
                    n, cols = 4 + 2 * KD + 2 * i + half + 1, slice(half * BANK, (half + 1) * BANK)
                    low_part(("value", i, half), value_lo[:, i, cols], value_hi[:, i, cols], table_lo_ready,
                             table_hi_ready, (n, n))

            for s in range(NT + 2):
                if s < NT:
                    for b in range(2):
                        src = full(dve, ("s", s, b))
                        V.tensor_reduce(out=negmax[:, s % 2, 2 * b:2 * b + 2],
                                        in_=src[:].rearrange("p (h m) -> p h m", m=M), axis=AX.X, op=ALU.max,
                                        negate=True).then_inc(negmax_ready, 1)
                    dve.wait_ge(exp_done, NH * (s + 1))
                    link(V.reciprocal(expsum[:, s % 2], expsum[:, s % 2]))
                    tt(probs[:], probs[:], expsum[:, s % 2].unsqueeze(2).to_broadcast([P, NH, M]),
                       ALU.mult).then_inc(probs_ready, 1)
                if s + 1 < NT:
                    turned_low("h1T", s + 1, hT_lo, hT_hi, hT_lo_ready, hT_hi_ready)
                t = s - 2
                if 0 <= t:
                    if t >= 1:
                        full(dve, ("router", t - 1))
                    dve_store(nf, "h2T", fT, t, 24)
                t = s - 1
                if 0 <= t < NT:
                    for half in range(2):
                        src = full(dve, ("h2", t, half))
                        part = h[:, t, half * BANK:(half + 1) * BANK]
                        tt(part, part, src[:], ALU.add).then_inc(h2_ready, 1)
                        dve.wait_ge(h2_ready, 2 * t + half + 1)
                        V.sem_inc(bank_free[use_of[("h2", t, half)][0]], 1)
                    dve_var(nf, t, stat)
                    dve_rstd(nf, t, stat)
                if s < NT:
                    turned_low("pT", s, pT_lo, pT_hi, pT_lo_ready, pT_hi_ready)

            dve.wait_ge(logit_ready, NT)
            dve.wait_ge(route_consts, 5)
            dve.wait_ge(router_in, 64)

            def wide(a, n):
                return a.unsqueeze(2).to_broadcast([P, NT, n])

            def numbers(n):
                return iota_n[:, 0:n].unsqueeze(1).to_broadcast([P, NT, n])

            link(tt(lg[:], logits[:], router_b[:].unsqueeze(1).to_broadcast([P, NT, NR]), ALU.add))

            def first_of_max(src, n, top, which, onehot, tmp):
                link(V.tensor_reduce(out=top, in_=src, axis=AX.X, op=ALU.max))
                link(tt(tmp, src, wide(top, n), ALU.is_ge))
                link(ts(tmp, tmp, -128.0, 128.0, ALU.mult, ALU.add))
                link(tt(tmp, tmp, numbers(n), ALU.add))
                link(V.tensor_reduce(out=which, in_=tmp, axis=AX.X, op=ALU.min))
                link(tt(onehot, numbers(n), wide(which, n), ALU.is_equal))

            first_of_max(lg[:, :, 0:NG], NG, col[:, 0], col[:, 1], gsel[:, 1], gsel[:, 0])
            tt(gsel[:, 0], lg[:, :, 0:NG], wide(col[:, 0], NG), ALU.subtract).then_inc(rexp_in, 1)
            link(ts(etmp[:, :, 0:NG], gsel[:, 1], -1.0, 1e30, ALU.add, ALU.mult))
            link(tt(em[:].rearrange("p t (g e) -> p t g e", e=EPG),
                    lg[:, :, NG:NR].rearrange("p t (g e) -> p t g e", e=EPG),
                    etmp[:, :, 0:NG].unsqueeze(3).to_broadcast([P, NT, NG, EPG]), ALU.add))
            first_of_max(em[:], NE, col[:, 2], col[:, 3], pick[:, 0], etmp[:])
            link(stt(em[:], pick[:, 0], -3e30, em[:], ALU.mult, ALU.add))
            first_of_max(em[:], NE, col[:, 4], col[:, 5], pick[:, 1], etmp[:])
            tt(col[:, 6], col[:, 4], col[:, 2], ALU.subtract).then_inc(rexp_in, 1)
            tt(both[:], pick[:, 0], pick[:, 1], ALU.add).then_inc(both_ready, 1)
            dve.wait_ge(rexp_out, 1)
            link(V.tensor_reduce(out=col[:, 7], in_=gsel[:, 0], axis=AX.X, op=ALU.add))
            link(V.reciprocal(col[:, 7], col[:, 7]))
            dve.wait_ge(rexp_out, 2)
            link(ts(col[:, 8], col[:, 6], 1.0, None, ALU.add))
            link(V.reciprocal(col[:, 8], col[:, 8]))
            link(tt(gates[:, :, 0], col[:, 7], col[:, 8], ALU.mult))
            link(tt(gates[:, :, 1], gates[:, :, 0], col[:, 6], ALU.mult))
            full(dve, "total")
            total = bank[1][:, 0:NT * NE].rearrange("p (t e) -> p t e", e=NE)
            link(V.memset(offs[:, 0, :], 0.0))
            for t in range(NT):
                link(tt(offs[:, t + 1], offs[:, t], total[:, t], ALU.add))
            V.sem_inc(bank_free[1], 1)
            full(dve, "rank")
            link(tt(rank[:], bank[0][:, 0:NT * NE].rearrange("p (t e) -> p t e", e=NE), offs[:, 0:NT], ALU.add))
            V.sem_inc(bank_free[0], 1)
            further, upto_e, shift_e, first_e = ev[:, 0], ev[:, 1], ev[:, 2], ev[:, 3]
            link(tt(over[:], offs[:, NT].unsqueeze(2).to_broadcast([P, NE, 7]),
                    limits[:].unsqueeze(1).to_broadcast([P, NE, 7]), ALU.is_gt))
            link(V.tensor_reduce(out=further, in_=over[:], axis=AX.X, op=ALU.add))
            link(V.tensor_tensor_scan(upto_e, ones[:, 0:NE], further, 0.0, ALU.mult, ALU.add))
            link(tt(shift_e, upto_e, further, ALU.subtract))
            link(tt(shift_e, shift_e, iota_n[:, 0:NE], ALU.subtract))
            link(ts(shift_e, shift_e, float(NE - 1), float(P), ALU.add, ALU.mult))
            link(ts(first_e, iota_n[:, 0:NE], float(P), None, ALU.mult))
            link(ts(etmp[:], rank[:], float(P), None, ALU.is_ge))
            link(tt(etmp[:], etmp[:], shift_e.unsqueeze(1).to_broadcast([P, NT, NE]), ALU.mult))
            link(tt(rank[:], rank[:], etmp[:], ALU.add))
            link(tt(rank[:], rank[:], first_e.unsqueeze(1).to_broadcast([P, NT, NE]), ALU.add))
            for k in range(2):
                link(tt(etmp[:], rank[:], pick[:, k], ALU.mult))
                link(V.tensor_reduce(out=posf[:, 0, k], in_=etmp[:], axis=AX.X, op=ALU.add))
            link(V.tensor_copy(posi[:, 0], posf[:, 0]))
            link(ts(posi[:, 1], posi[:, 0], 7, None, ALU.logical_shift_right))
            link(ts(posi[:, 0], posi[:, 0], P - 1, None, ALU.bitwise_and))
            link(V.tensor_copy(posf[:], posi[:]))
            def spread(a, n):
                return a.rearrange("p k t -> p (k t)").unsqueeze(2).to_broadcast([P, 2 * NT, n])

            def count(n):
                return iota_n[:, 0:n].unsqueeze(1).to_broadcast([P, 2 * NT, n])
            link(tt(block_of[:], count(NB), spread(posf[:, 1], NB), ALU.is_equal))
            tt(block_of[:], block_of[:].bitcast(F32), spread(assign_no[:], NB), ALU.mult)
            for k in range(2):
                tt(row_of[:, k * NT:(k + 1) * NT], iota_n[:].unsqueeze(1).to_broadcast([P, NT, P]),
                   wide(posf[:, 0, k], P), ALU.is_equal).then_inc(sel_ready, 1)
            dve.wait_ge(sel_used, 1)
            slots = bank[2][:, 0:NB]
            link(ts(slotv[:, 0], slots, 0.0, float(NO_ROW), ALU.is_equal, ALU.mult))
            link(stt(slotv[:, 1], slots, -1.0, slotv[:, 0], ALU.add, ALU.add))
            V.sem_inc(bank_free[2], 1)
            link(V.tensor_copy(rows_of_block[:, 1], slotv[:, 1]))
            link(ts(rows_of_block[:, 0], rows_of_block[:, 1], 1, None, ALU.logical_shift_right))
            def copy_rows(which, dst, block, ready):
                V.tensor_copy(dst[:], rows_of_block[:, which, bass.ds(block, 1)]).then_inc(ready, 1)

            def next_gather(b, n, block):
                dve.wait_ge(xg_in[b], 16 * n)
                copy_rows(0, gidx[b], block, gidx_ready)

            def weigh_tokens(i):
                dve.wait_ge(xg_turned, i + 1)
                for half in range(2):
                    w = par[:, 48 + 4 * half:52 + 4 * half].unsqueeze(2).to_broadcast([P, 4, P])
                    last = tt(xw[:, 4 * half:4 * half + 4], bank[half][:].rearrange("p (c n) -> p c n", n=P), w,
                              ALU.mult)
                last.then_inc(xw_ready, 1)

            def tokens_low(b, i):
                dve.wait_ge(xw_ready, i + 1)
                dve.wait_ge(x_hi_ready, i + 1)
                tt(x_lo[b][:], xw[:], x_hi[b][:].bitcast(F32), ALU.subtract).then_inc(x_lo_ready, 1)

            def split_low(j, k):
                dve.wait_ge(hi_ready, 12 * j + k + 1)
                tt(w_lo[k % NSPLIT][:], raw[k % NRAW][:], w_hi[k % NSPLIT][:].bitcast(F32), ALU.subtract)\
                    .then_inc(lo_ready, 1)

            def gate_up(j, k, i):
                dve.wait_ge(gate_ready, i + 1)
                dve.wait_ge(piece_used, 12 * j + k)
                tt(hid[:], gate_act[:], bank[3][:], ALU.mult).then_inc(hid_ready, 1)

            def hidden_low(i):
                dve.wait_ge(hid_hi_ready, i + 1)
                tt(hid_lo[:].rearrange("p f n -> p (f n)"), bank[4][:],
                   hid_hi[:].rearrange("p f n -> p (f n)").bitcast(F32), ALU.subtract).then_inc(hid_lo_ready, 1)

            def scatter_rows(j, b):
                wait_for(dve, y_sent[b], 16 * j)
                copy_rows(1, sidx[b], 2 * j + b, sidx_ready)

            def first_block(j, gather=False, unsplit=()):
                i = 2 * j
                weigh_tokens(i)
                for k in unsplit[:1]:
                    split_low(j, k)
                tokens_low(0, i)
                for k in unsplit[1:]:
                    split_low(j, k)
                split_low(j, 4)
                weigh_tokens(i + 1)
                split_low(j, 5)
                if gather:
                    next_gather(1, j + 1, i + 3)
                tokens_low(1, i + 1)
                split_low(j, 6)
                gate_up(j, 4, i)
                split_low(j, 7)

            def next_block(j, s, gather=False, final=False):
                i, k = 2 * j + 1 + s, 4 + 6 * s
                hidden_low(i - 1)
                split_low(j, k + 4)
                scatter_rows(j, s)
                split_low(j, k + 5)
                split_low(j, k + 6)
                if gather:
                    next_gather(s, j + 2, i + 3)
                if not final:
                    weigh_tokens(i + 1)
                split_low(j, k + 7)
                if not final:
                    tokens_low(s, i + 1)
                    split_low(j, k + 8)
                gate_up(j, k + 6, i)
                if not final:
                    split_low(j, k + 9)

            def last_down(j):
                hidden_low(2 * j + 1)
                scatter_rows(j, 1)

            copy_rows(0, gidx[0], 0, gidx_ready)
            copy_rows(0, gidx[1], 1, gidx_ready)
            link(tt(ovcmp[:], iota_n[:, 0:MAXOV].unsqueeze(2).to_broadcast([P, MAXOV, NE]),
                    upto_e.unsqueeze(1).to_broadcast([P, MAXOV, NE]), ALU.is_ge))
            link(V.tensor_reduce(out=ovf[:, 0:MAXOV], in_=ovcmp[:], axis=AX.X, op=ALU.add))
            link(ts(ovf[:, 0:MAXOV], ovf[:, 0:MAXOV], float(NE - 1), None, ALU.min))
            link(V.tensor_copy(ovf[:, MAXOV:MAXOV + 1], ev[:, 1, NE - 1:NE]))
            link(V.tensor_copy(meta[:], ovf[:]))

            next_gather(0, 1, 2)
            dve.wait_ge(raw_in[(NSPLIT - 1) % NRAW], 32)
            first_block(0, gather=True)
            for s in range(2):
                next_block(0, s, gather=True)
            with dve.Fori(1, NE // 2 - 1) as j:
                for s in range(2):
                    next_block(j, s, gather=True)
            next_block(NE // 2 - 1, 0, final=True)
            last_down(NE // 2 - 1)
            further = dve.value_load(meta[0:1, MAXOV:MAXOV + 1], min_val=0, max_val=MAXOV)

            def further_pair(o):
                j = NE // 2 + o
                first_block(j, unsplit=range(NSPLIT))
                for b in range(2):
                    next_gather(b, j + 1, 2 * j + 2 + b)
                next_block(j, 0, final=True)
                last_down(j)
            run_further(dve, further, further_pair)


            def combine(t):
                dve.wait_ge(y_in[t % NY], 16 * (t // NY + 1))
                link(stt(h[:, t, :], ytile[t % NY][:, 0], gates[:, t, 0:1], h[:, t, :], ALU.mult, ALU.add))
                stt(h[:, t, :], ytile[t % NY][:, 1], gates[:, t, 1:2], h[:, t, :], ALU.mult, ALU.add).then_inc(comb, 1)
            combine(0)
            combine(1)
            for t in range(NT):
                if t + 2 < NT:
                    combine(t + 2)
                dve_var(n2, t, stat)
                dve_rstd(n2, t, stat)


NAMES = ["x", "mem", "norm_mix_w", "w_in", "conv_w", "conv_b", "conv_ln_w", "conv_ln_b",
         "ssm_A_re", "ssm_A_im", "ssm_log_dt", "ssm_B_re", "ssm_B_im", "ssm_C_re", "ssm_C_im",
         "ssm_D", "ssm_glu_w", "w_out", "norm_x_w", "norm_mem_w", "xq_w", "xk_w", "xv_w", "xo_w",
         "norm_ffn_w", "router_group_w", "router_group_b", "router_expert_w", "router_expert_b",
         "moe_w1", "moe_w3", "moe_w2", "final_norm_w"]


def build(nc, shapes):
    args = [nc.dram_tensor(n, shapes[n], F32, kind="ExternalInput").ap() for n in NAMES]
    out = nc.dram_tensor("out", shapes["x"], F32, kind="ExternalOutput").ap()
    hymba_layer(nc, *args, out)


def kernel(**inputs):
    import concourse.bacc as bacc
    from concourse.bass_utils import run_bass_kernel_spmd

    arrays = {n: np.ascontiguousarray(inputs[n]) for n in NAMES}
    nc = bacc.Bacc("TRN2", target_bir_lowering=False, num_devices=1)
    build(nc, {n: a.shape for n, a in arrays.items()})
    result = run_bass_kernel_spmd(nc, [arrays], core_ids=[0])
    return result.results[0]["out"]
```
